# Optimizing a Trainium2 kernel written in Bass

```python
import math
import jax
import jax.numpy as jnp
from jax import lax
import numpy as np
import jax, jax.numpy as jnp

D_MODEL = 1024
BATCH = 1
SEQ = 512
DEPTH = 1

D_HEAD = 64
NSA_HEADS = 8
NSA_KV_HEADS = 2
NSA_GROUP = NSA_HEADS // NSA_KV_HEADS
D_NSA = NSA_HEADS * D_HEAD
D_KV = NSA_KV_HEADS * D_HEAD
N_BRANCH = 3
N_GATES = NSA_HEADS * N_BRANCH
CMP_BLOCK = 32
CMP_STRIDE = 16
CMP_HIDDEN = 256
SEL_BLOCK = 64
SEL_TOPK = 16
WINDOW = 512
Q_BLOCK = 64
GMLP_GROUPS = 8
GMLP_GROUP_DIM = 64
D_GMLP = GMLP_GROUPS * GMLP_GROUP_DIM
CHUNK = 128
D_MIX = D_NSA + D_GMLP
D_PROJ = D_NSA + 6 * D_KV + N_GATES + 2 * D_GMLP
SPLITS = (D_NSA, D_NSA + D_KV, D_NSA + 2 * D_KV, D_NSA + 3 * D_KV, D_NSA + 4 * D_KV, D_NSA + 5 * D_KV, D_NSA + 6 * D_KV, D_NSA + 6 * D_KV + N_GATES)
REL_BUCKETS = 32
REL_MAX_DIST = 128
D_FF = 2816
CONV_WIDTH = 3
EPS = 1e-6
NEG_INF = -1e30
FORCED_SCORE = 1e4


def _rms_norm(x, g):
    xf = x.astype(jnp.float32)
    y = xf * lax.rsqrt(jnp.mean(xf * xf, axis=-1, keepdims=True) + EPS)
    return (y * g.astype(jnp.float32)).astype(x.dtype)

def _rel_bucket(dist):
    max_exact = REL_BUCKETS // 2
    d = jnp.maximum(dist, 1).astype(jnp.float32)
    log_b = max_exact + (jnp.log(d / max_exact) / math.log(REL_MAX_DIST / max_exact) * (REL_BUCKETS - max_exact)).astype(jnp.int32)
    log_b = jnp.clip(log_b, max_exact, REL_BUCKETS - 1)
    return jnp.where(dist < max_exact, jnp.maximum(dist, 0), log_b)

def _bias_shared(dist, rel_bias):
    b = rel_bias[_rel_bucket(dist)]
    return jnp.transpose(b, (2, 0, 1)).reshape(NSA_KV_HEADS, NSA_GROUP, dist.shape[0], dist.shape[1]).astype(jnp.float32)

def _bias_gathered(dist, rel_bias):
    table = rel_bias.T.reshape(NSA_KV_HEADS, NSA_GROUP, REL_BUCKETS)
    gi = jnp.arange(NSA_KV_HEADS)[None, :, None, None, None]
    ri = jnp.arange(NSA_GROUP)[None, None, :, None, None]
    return table[gi, ri, _rel_bucket(dist)[:, :, None]].astype(jnp.float32)

def _heads(t, B, T):
    return jnp.transpose(t.reshape(B, T, NSA_KV_HEADS, D_HEAD), (0, 2, 1, 3))

def _compress(tok, pe, w1, b1, w2):
    B, G, T, D = tok.shape
    nc = (T - CMP_BLOCK) // CMP_STRIDE + 1
    idx = jnp.arange(nc)[:, None] * CMP_STRIDE + jnp.arange(CMP_BLOCK)[None, :]
    blk = (tok[:, :, idx] + pe).reshape(B, G, nc, CMP_BLOCK * D)
    return jax.nn.gelu(blk @ w1 + b1) @ w2

def _nsa(q, k_cmp, v_cmp, k_slc, v_slc, k_win, v_win, gates, rel_bias):
    B, G, R, T, D = q.shape
    nc = k_cmp.shape[2]
    ns = T // SEL_BLOCK
    n_sel = min(SEL_TOPK, ns)
    cmp_end = jnp.arange(nc) * CMP_STRIDE + (CMP_BLOCK - 1)
    cs = jnp.arange(nc)[:, None] * CMP_STRIDE
    ss = jnp.arange(ns)[None, :] * SEL_BLOCK
    overlap = ((cs < ss + SEL_BLOCK) & (cs + CMP_BLOCK > ss)).astype(jnp.float32)
    blk_start = jnp.arange(ns) * SEL_BLOCK
    k_blocks = k_slc.reshape(B, G, ns, SEL_BLOCK, D)
    v_blocks = v_slc.reshape(B, G, ns, SEL_BLOCK, D)
    k_pad = jnp.pad(k_win, ((0, 0), (0, 0), (WINDOW, 0), (0, 0)))
    v_pad = jnp.pad(v_win, ((0, 0), (0, 0), (WINDOW, 0), (0, 0)))
    bi = jnp.arange(B)[:, None, None, None]
    gi = jnp.arange(G)[None, :, None, None]

    def block(qi):
        t0 = qi * Q_BLOCK
        tpos = t0 + jnp.arange(Q_BLOCK)
        qb = lax.dynamic_slice_in_dim(q, t0, Q_BLOCK, axis=3)
        gb = lax.dynamic_slice_in_dim(gates, t0, Q_BLOCK, axis=3)

        dist_c = tpos[:, None] - cmp_end[None, :]
        valid_c = dist_c >= 0
        s_c = jnp.einsum('bgrqd,bgnd->bgrqn', qb, k_cmp).astype(jnp.float32) + _bias_shared(dist_c, rel_bias)
        p_c = jnp.where(valid_c, jax.nn.softmax(jnp.where(valid_c, s_c, NEG_INF), axis=-1), 0.0)
        o_c = jnp.einsum('bgrqn,bgnd->bgrqd', p_c.astype(v_cmp.dtype), v_cmp)

        imp = jnp.einsum('bgrqn,ns->bgqs', p_c, overlap)
        cur = tpos[:, None] // SEL_BLOCK
        j = jnp.arange(ns)[None, :]
        forced = (j == 0) | (j == cur) | (j == cur - 1)
        causal_blk = blk_start[None, :] <= tpos[:, None]
        score = jnp.where(forced, FORCED_SCORE, jnp.where(causal_blk, imp, NEG_INF))
        _, sel = lax.top_k(score, n_sel)

        k_sel = k_blocks[bi, gi, sel].reshape(B, G, Q_BLOCK, n_sel * SEL_BLOCK, D)
        v_sel = v_blocks[bi, gi, sel].reshape(B, G, Q_BLOCK, n_sel * SEL_BLOCK, D)
        kpos = (sel[..., None] * SEL_BLOCK + jnp.arange(SEL_BLOCK)).reshape(B, G, Q_BLOCK, n_sel * SEL_BLOCK)
        dist_s = tpos[None, None, :, None] - kpos
        s_s = jnp.einsum('bgrqd,bgqkd->bgrqk', qb, k_sel).astype(jnp.float32) + _bias_gathered(dist_s, rel_bias)
        p_s = jax.nn.softmax(jnp.where((dist_s >= 0)[:, :, None], s_s, NEG_INF), axis=-1)
        o_s = jnp.einsum('bgrqk,bgqkd->bgrqd', p_s.astype(v_sel.dtype), v_sel)

        kw = lax.dynamic_slice_in_dim(k_pad, t0, Q_BLOCK + WINDOW, axis=2)
        vw = lax.dynamic_slice_in_dim(v_pad, t0, Q_BLOCK + WINDOW, axis=2)
        kpos_w = t0 - WINDOW + jnp.arange(Q_BLOCK + WINDOW)
        dist_w = tpos[:, None] - kpos_w[None, :]
        valid_w = (dist_w >= 0) & (dist_w < WINDOW) & (kpos_w[None, :] >= 0)
        s_w = jnp.einsum('bgrqd,bgkd->bgrqk', qb, kw).astype(jnp.float32) + _bias_shared(dist_w, rel_bias)
        p_w = jax.nn.softmax(jnp.where(valid_w, s_w, NEG_INF), axis=-1)
        o_w = jnp.einsum('bgrqk,bgkd->bgrqd', p_w.astype(vw.dtype), vw)

        return gb[..., 0:1] * o_c + gb[..., 1:2] * o_s + gb[..., 2:3] * o_w

    o = lax.map(block, jnp.arange(T // Q_BLOCK))
    return jnp.transpose(o, (1, 0, 4, 2, 3, 5)).reshape(B, T, G * R * D)

def _sgu(uv, sgu_norm, sgu_w, sgu_b):
    B, T, _ = uv.shape
    u, v = jnp.split(jax.nn.gelu(uv), 2, axis=-1)
    v = _rms_norm(v, sgu_norm).reshape(B, T // CHUNK, CHUNK, GMLP_GROUPS, GMLP_GROUP_DIM)
    w = sgu_w * jnp.tril(jnp.ones((CHUNK, CHUNK), sgu_w.dtype))
    z = jnp.einsum('gij,bcjge->bcige', w, v) + sgu_b.T[:, :, None]
    return u * z.reshape(B, T, D_GMLP)

def _conv_ffn(h, w_up, conv_w, conv_b, w_down):
    up = h @ w_up
    up = lax.conv_general_dilated(up, conv_w[:, None, :], (1,), [(CONV_WIDTH - 1, 0)], dimension_numbers=('NWC', 'WIO', 'NWC'), feature_group_count=up.shape[-1]) + conv_b
    a, g = jnp.split(up, 2, axis=-1)
    return (jax.nn.silu(g) * a) @ w_down

def first_inputs(seed: int = 0) -> dict:
    key = jax.random.key(seed)
    ks = jax.random.split(key, 32)
    L = DEPTH

    def nrm(k, shape, scale):
        return jax.random.normal(k, shape, jnp.float32) * scale

    def gain(k, shape):
        return 1.0 + 0.01 * jax.random.normal(k, shape, jnp.float32)

    return {
        "x": nrm(ks[0], (BATCH, SEQ, D_MODEL), 1.0),
        "rel_bias": nrm(ks[1], (REL_BUCKETS, NSA_HEADS), 0.5),
        "attn_norm": gain(ks[2], (L, D_MODEL)),
        "w_in": nrm(ks[3], (L, D_MODEL, D_PROJ), D_MODEL ** -0.5),
        "q_norm": gain(ks[4], (L, D_HEAD)),
        "k_norm_cmp": gain(ks[5], (L, D_HEAD)),
        "k_norm_slc": gain(ks[6], (L, D_HEAD)),
        "k_norm_win": gain(ks[7], (L, D_HEAD)),
        "cmp_pe_k": nrm(ks[8], (L, CMP_BLOCK, D_HEAD), 0.1),
        "cmp_w1_k": nrm(ks[9], (L, CMP_BLOCK * D_HEAD, CMP_HIDDEN), (CMP_BLOCK * D_HEAD) ** -0.5),
        "cmp_b1_k": nrm(ks[10], (L, CMP_HIDDEN), 0.01),
        "cmp_w2_k": nrm(ks[11], (L, CMP_HIDDEN, D_HEAD), CMP_HIDDEN ** -0.5),
        "cmp_pe_v": nrm(ks[12], (L, CMP_BLOCK, D_HEAD), 0.1),
        "cmp_w1_v": nrm(ks[13], (L, CMP_BLOCK * D_HEAD, CMP_HIDDEN), (CMP_BLOCK * D_HEAD) ** -0.5),
        "cmp_b1_v": nrm(ks[14], (L, CMP_HIDDEN), 0.01),
        "cmp_w2_v": nrm(ks[15], (L, CMP_HIDDEN, D_HEAD), CMP_HIDDEN ** -0.5),
        "sgu_norm": gain(ks[16], (L, D_GMLP)),
        "sgu_w": nrm(ks[17], (L, GMLP_GROUPS, CHUNK, CHUNK), CHUNK ** -0.5),
        "sgu_b": gain(ks[18], (L, GMLP_GROUPS, CHUNK)),
        "w_out": nrm(ks[19], (L, D_MIX, D_MODEL), D_MIX ** -0.5),
        "ffn_norm": gain(ks[20], (L, D_MODEL)),
        "w_up": nrm(ks[21], (L, D_MODEL, 2 * D_FF), D_MODEL ** -0.5),
        "conv_w": nrm(ks[22], (L, CONV_WIDTH, 2 * D_FF), CONV_WIDTH ** -0.5),
        "conv_b": nrm(ks[23], (L, 2 * D_FF), 0.01),
        "w_down": nrm(ks[24], (L, D_FF, D_MODEL), D_FF ** -0.5),
    }

def first_block(x, rel_bias, attn_norm, w_in, q_norm, k_norm_cmp, k_norm_slc, k_norm_win,
              cmp_pe_k, cmp_w1_k, cmp_b1_k, cmp_w2_k, cmp_pe_v, cmp_w1_v, cmp_b1_v, cmp_w2_v,
              sgu_norm, sgu_w, sgu_b, w_out, ffn_norm, w_up, conv_w, conv_b, w_down):
    B, T, _ = x.shape
    G, R = NSA_KV_HEADS, NSA_GROUP
    for l in range(DEPTH):
        h = _rms_norm(x, attn_norm[l])
        proj = h @ w_in[l]
        q, kc, vc, ks_, vs, kw, vw, gl, uv = jnp.split(proj, SPLITS, axis=-1)
        q = _rms_norm(q.reshape(B, T, G, R, D_HEAD), q_norm[l]) * (D_HEAD ** -0.5)
        q = jnp.transpose(q, (0, 2, 3, 1, 4))
        k_cmp = _rms_norm(_compress(_heads(kc, B, T), cmp_pe_k[l], cmp_w1_k[l], cmp_b1_k[l], cmp_w2_k[l]), k_norm_cmp[l])
        v_cmp = _compress(_heads(vc, B, T), cmp_pe_v[l], cmp_w1_v[l], cmp_b1_v[l], cmp_w2_v[l])
        k_slc = _rms_norm(_heads(ks_, B, T), k_norm_slc[l])
        v_slc = _heads(vs, B, T)
        k_win = _rms_norm(_heads(kw, B, T), k_norm_win[l])
        v_win = _heads(vw, B, T)
        gates = jnp.transpose(jax.nn.sigmoid(gl.reshape(B, T, G, R, N_BRANCH)), (0, 2, 3, 1, 4))
        o_nsa = _nsa(q, k_cmp, v_cmp, k_slc, v_slc, k_win, v_win, gates, rel_bias)
        o_sgu = _sgu(uv, sgu_norm[l], sgu_w[l], sgu_b[l])
        x = x + jnp.concatenate([o_nsa, o_sgu], axis=-1) @ w_out[l]
        x = x + _conv_ffn(_rms_norm(x, ffn_norm[l]), w_up[l], conv_w[l], conv_b[l], w_down[l])
    return x


_first_inputs = first_inputs


def first_inputs(seed=0):
    import zlib

    import numpy as np

    out = dict(_first_inputs(seed))
    spreads = {}
    factors = {}
    for name, (base, spread) in spreads.items():
        noise = np.random.default_rng([zlib.crc32(name.encode()), seed]).standard_normal(out[name].shape)
        drawn = base * np.exp(spread * noise) if base else spread * noise
        out[name] = jnp.asarray(drawn.astype(out[name].dtype))
    for name, factor in factors.items():
        out[name] = (out[name] * factor).astype(out[name].dtype)
    return out


_narrow_inputs = first_inputs


def first_inputs(seed=0):

    out = dict(_narrow_inputs(seed))
    wider = {'attn_norm': 9.2,
     'q_norm': 12.0,
     'k_norm_cmp': 12.0,
     'k_norm_slc': 12.0,
     'k_norm_win': 12.0,
     'cmp_pe_k': 12.0,
     'cmp_b1_k': 12.0,
     'cmp_pe_v': 3.5,
     'cmp_b1_v': 12.0,
     'sgu_norm': 12.0,
     'sgu_b': 12.0,
     'ffn_norm': 9.95,
     'conv_b': 9.92}
    for name, times in wider.items():
        mean = out[name].mean()
        out[name] = (mean + times * (out[name] - mean)).astype(out[name].dtype)
    return out


DEPTH_2 = 2

CHUNK_2 = 64
Q_BLOCK_2 = 128
ROPE_THETA = 10000.0
RMS_EPS = 1e-6

A_HEADS = D_MODEL // 128
A_HEAD_DIM = 64
D_A = A_HEADS * A_HEAD_DIM
IDX_HEADS = 8
IDX_DIM = 32
TOPK_MAX = 256

B_HEADS = D_MODEL // 256
B_HEAD_DIM = 64
D_B = B_HEADS * 2 * B_HEAD_DIM

D_MIX_2 = D_A + D_B
D_FF_2 = -(-8 * D_MODEL // (3 * 256)) * 256

IN_SPLITS = (D_A, D_A, D_A, IDX_HEADS * IDX_DIM, IDX_DIM, IDX_HEADS, D_B, D_B, D_B)
D_IN = D_A * 3 + IDX_HEADS * IDX_DIM + IDX_DIM + IDX_HEADS + D_B * 3


def rms_norm(x, g):
    x32 = x.astype(jnp.float32)
    r = lax.rsqrt(jnp.mean(x32 * x32, axis=-1, keepdims=True) + RMS_EPS)
    return (x32 * r * g.astype(jnp.float32)).astype(x.dtype)

def rope_tables(seq_len, dim):
    pos = jnp.arange(seq_len, dtype=jnp.float32)
    inv = ROPE_THETA ** (-jnp.arange(0, dim, 2, dtype=jnp.float32) / dim)
    ang = pos[:, None] * inv[None, :]
    return jnp.cos(ang), jnp.sin(ang)

def apply_rope(x, cos, sin):
    half = x.shape[-1] // 2
    x32 = x.astype(jnp.float32)
    x1, x2 = x32[..., :half], x32[..., half:]
    c = cos[None, :, None, :]
    s = sin[None, :, None, :]
    return jnp.concatenate([x1 * c - x2 * s, x2 * c + x1 * s], axis=-1).astype(x.dtype)

def to_blocks(a):
    b, s = a.shape[:2]
    return jnp.swapaxes(a.reshape(b, s // Q_BLOCK_2, Q_BLOCK_2, *a.shape[2:]), 0, 1)

def from_blocks(a):
    nb, b = a.shape[:2]
    return jnp.swapaxes(a, 0, 1).reshape(b, nb * a.shape[2], *a.shape[3:])

def dsa_mixer(q, k, v, iq, ik, iw):
    s_len = q.shape[1]
    topk = min(TOPK_MAX, s_len // 4)
    key_chunk = jnp.arange(s_len) // CHUNK_2
    scale = A_HEAD_DIM ** -0.5
    gather = jax.vmap(lambda a, i: a[i])

    def block(args):
        bi, qb, iqb, iwb = args
        q_chunk = (bi * Q_BLOCK_2 + jnp.arange(Q_BLOCK_2)) // CHUNK_2
        admissible = key_chunk[None, :] <= q_chunk[:, None]
        dots = jnp.einsum('bqhd,bsd->bqhs', iqb, ik,
                          preferred_element_type=jnp.float32) * (IDX_DIM ** -0.5)
        w = iwb.astype(jnp.float32) * (IDX_HEADS ** -0.5)
        score = jnp.einsum('bqhs,bqh->bqs', jax.nn.relu(dots), w)
        score = jnp.where(admissible[None], score, -jnp.inf)
        _, idx = lax.top_k(score, topk)
        k_sel = gather(k, idx)
        v_sel = gather(v, idx)
        valid = (idx // CHUNK_2) <= q_chunk[None, :, None]
        logits = jnp.einsum('bqhd,bqkhd->bhqk', qb, k_sel,
                            preferred_element_type=jnp.float32) * scale
        logits = jnp.where(valid[:, None], logits, -jnp.inf)
        p = jax.nn.softmax(logits, axis=-1)
        return jnp.einsum('bhqk,bqkhd->bqhd', p.astype(v.dtype), v_sel)

    nb = s_len // Q_BLOCK_2
    out = lax.map(block, (jnp.arange(nb), to_blocks(q), to_blocks(iq), to_blocks(iw)))
    return from_blocks(out)

def diff_mixer(q, k, v, lam, lam_init, g_subln):
    s_len = q.shape[1]
    key_chunk = jnp.arange(s_len) // CHUNK_2
    scale = B_HEAD_DIM ** -0.5

    def block(args):
        bi, qb = args
        q_chunk = (bi * Q_BLOCK_2 + jnp.arange(Q_BLOCK_2)) // CHUNK_2
        admissible = key_chunk[None, :] <= q_chunk[:, None]
        logits = jnp.einsum('bqhcd,bshcd->bchqs', qb, k,
                            preferred_element_type=jnp.float32) * scale
        logits = jnp.where(admissible[None, None, None], logits, -jnp.inf)
        p = jax.nn.softmax(logits, axis=-1)
        attn = p[:, 0] - lam * p[:, 1]
        return jnp.einsum('bhqs,bshe->bqhe', attn.astype(v.dtype), v)

    nb = s_len // Q_BLOCK_2
    out = from_blocks(lax.map(block, (jnp.arange(nb), to_blocks(q))))
    return rms_norm(out, g_subln) * (1.0 - lam_init)

def second_inputs(seed: int = 0) -> dict:
    key = jax.random.key(seed)
    ks = jax.random.split(key, 14)
    f32 = jnp.float32
    nrm = lambda k, shape, fan_in: jax.random.normal(k, shape, f32) * (fan_in ** -0.5)
    gain = lambda k, shape: 1.0 + 0.02 * jax.random.normal(k, shape, f32)
    return {
        "x": jax.random.normal(ks[0], (BATCH, SEQ, D_MODEL), f32),
        "w_in": nrm(ks[1], (DEPTH_2, D_MODEL, D_IN), D_MODEL),
        "w_out": nrm(ks[2], (DEPTH_2, D_MIX_2, D_MODEL), D_MIX_2),
        "g_mix": gain(ks[3], (DEPTH_2, D_MODEL)),
        "lam_q1": 0.1 * jax.random.normal(ks[4], (DEPTH_2, B_HEAD_DIM), f32),
        "lam_k1": 0.1 * jax.random.normal(ks[5], (DEPTH_2, B_HEAD_DIM), f32),
        "lam_q2": 0.1 * jax.random.normal(ks[6], (DEPTH_2, B_HEAD_DIM), f32),
        "lam_k2": 0.1 * jax.random.normal(ks[7], (DEPTH_2, B_HEAD_DIM), f32),
        "g_subln": gain(ks[8], (DEPTH_2, 2 * B_HEAD_DIM)),
        "g_ffn": gain(ks[9], (DEPTH_2, D_MODEL)),
        "w_gate": nrm(ks[10], (DEPTH_2, D_MODEL, D_FF_2), D_MODEL),
        "w_up": nrm(ks[11], (DEPTH_2, D_MODEL, D_FF_2), D_MODEL),
        "w_down": nrm(ks[12], (DEPTH_2, D_FF_2, D_MODEL), D_FF_2),
        "g_final": gain(ks[13], (D_MODEL,)),
    }

def second_block(x, w_in, w_out, g_mix, lam_q1, lam_k1, lam_q2, lam_k2, g_subln,
              g_ffn, w_gate, w_up, w_down, g_final):
    b_, s_len, _ = x.shape
    cos_a, sin_a = rope_tables(s_len, A_HEAD_DIM)
    cos_i, sin_i = rope_tables(s_len, IDX_DIM)
    cos_b, sin_b = rope_tables(s_len, B_HEAD_DIM)
    split_points = [int(o) for o in np.cumsum(IN_SPLITS)[:-1]]

    for layer in range(DEPTH_2):
        h = rms_norm(x, g_mix[layer])
        proj = jnp.einsum('bsd,dc->bsc', h, w_in[layer])
        qa, ka, va, iq, ik, iw, qb, kb, vb = jnp.split(proj, split_points, axis=-1)

        qa = apply_rope(qa.reshape(b_, s_len, A_HEADS, A_HEAD_DIM), cos_a, sin_a)
        ka = apply_rope(ka.reshape(b_, s_len, A_HEADS, A_HEAD_DIM), cos_a, sin_a)
        va = va.reshape(b_, s_len, A_HEADS, A_HEAD_DIM)
        iq = apply_rope(iq.reshape(b_, s_len, IDX_HEADS, IDX_DIM), cos_i, sin_i)
        ik = apply_rope(ik[:, :, None, :], cos_i, sin_i)[:, :, 0, :]
        out_a = dsa_mixer(qa, ka, va, iq, ik, iw).reshape(b_, s_len, D_A)

        qb = apply_rope(qb.reshape(b_, s_len, 2 * B_HEADS, B_HEAD_DIM), cos_b, sin_b)
        kb = apply_rope(kb.reshape(b_, s_len, 2 * B_HEADS, B_HEAD_DIM), cos_b, sin_b)
        qb = qb.reshape(b_, s_len, B_HEADS, 2, B_HEAD_DIM)
        kb = kb.reshape(b_, s_len, B_HEADS, 2, B_HEAD_DIM)
        vb = vb.reshape(b_, s_len, B_HEADS, 2 * B_HEAD_DIM)
        lam_init = 0.8 - 0.6 * math.exp(-0.3 * layer)
        lam = (jnp.exp(jnp.sum(lam_q1[layer].astype(jnp.float32) * lam_k1[layer].astype(jnp.float32)))
               - jnp.exp(jnp.sum(lam_q2[layer].astype(jnp.float32) * lam_k2[layer].astype(jnp.float32)))
               + lam_init)
        out_b = diff_mixer(qb, kb, vb, lam, lam_init, g_subln[layer]).reshape(b_, s_len, D_B)

        mixed = jnp.concatenate([out_a, out_b], axis=-1)
        x = x + jnp.einsum('bsc,cd->bsd', mixed, w_out[layer])

        h2 = rms_norm(x, g_ffn[layer])
        gate = jnp.einsum('bsd,df->bsf', h2, w_gate[layer])
        up = jnp.einsum('bsd,df->bsf', h2, w_up[layer])
        x = x + jnp.einsum('bsf,fd->bsd', jax.nn.silu(gate) * up, w_down[layer])

    return rms_norm(x, g_final)


SSM_HEADS = 16
SSM_HEAD_DIM = 64
SSM_D_INNER = SSM_HEADS * SSM_HEAD_DIM
SSM_GROUPS = 2
SSM_STATE = 128
SSM_CONV_DIM = SSM_D_INNER + 2 * SSM_GROUPS * SSM_STATE
GDN_HEADS = 8
GDN_HEAD_K = 128
GDN_HEAD_V = 128
GDN_K_DIM = GDN_HEADS * GDN_HEAD_K
GDN_V_DIM = GDN_HEADS * GDN_HEAD_V
GDN_QKV_DIM = 2 * GDN_K_DIM + GDN_V_DIM
CONV_K = 4
CHUNK_3 = 64
FFN_HIDDEN = -(-8 * D_MODEL // (3 * 256)) * 256
IN_SPLIT_SIZES = (SSM_D_INNER, SSM_CONV_DIM, SSM_HEADS,
                  GDN_QKV_DIM, GDN_V_DIM, GDN_HEADS, GDN_HEADS,
                  D_MODEL, D_MODEL)
IN_DIM = sum(IN_SPLIT_SIZES)
IN_SPLIT_IDX = tuple(int(i) for i in np.cumsum(IN_SPLIT_SIZES)[:-1])


def rmsnorm(x, w):
    xf = x.astype(jnp.float32)
    y = xf * lax.rsqrt(jnp.mean(xf * xf, axis=-1, keepdims=True) + EPS)
    return (y * w.astype(jnp.float32)).astype(x.dtype)

def causal_dwconv(u, w):
    c = u.shape[-1]
    return lax.conv_general_dilated(
        u, w[:, None, :].astype(u.dtype), window_strides=(1,),
        padding=[(CONV_K - 1, 0)], dimension_numbers=("NWC", "WIO", "NWC"),
        feature_group_count=c)

def to_chunks(t):
    b, s = t.shape[:2]
    return jnp.moveaxis(t.reshape(b, s // CHUNK_3, CHUNK_3, *t.shape[2:]), 1, 0)

def from_chunks(t):
    t = jnp.moveaxis(t, 0, 1)
    return t.reshape(t.shape[0], t.shape[1] * t.shape[2], *t.shape[3:])

def ssd_scan(xdt, a, bm, cm):
    bsz, s = xdt.shape[:2]
    r = SSM_HEADS // SSM_GROUPS
    xdt = xdt.reshape(bsz, s, SSM_GROUPS, r, SSM_HEAD_DIM)
    a = a.reshape(bsz, s, SSM_GROUPS, r)
    causal = jnp.tril(jnp.ones((CHUNK_3, CHUNK_3), dtype=bool))[None, :, :, None, None]

    def body(state, inp):
        xc, ac, bc, cc = inp
        acum = jnp.cumsum(ac, axis=1)
        seg = acum[:, :, None] - acum[:, None, :]
        lmat = jnp.exp(jnp.where(causal, seg, -jnp.inf))
        cb = jnp.einsum("bign,bjgn->bijg", cc, bc)
        y_diag = jnp.einsum("bijg,bijgr,bjgrp->bigrp", cb, lmat, xc)
        y_off = jnp.einsum("bign,bgrpn->bigrp", cc, state) * jnp.exp(acum)[..., None]
        decay_end = jnp.exp(acum[:, -1:] - acum)
        new_state = state * jnp.exp(acum[:, -1])[..., None, None] + jnp.einsum(
            "bjgn,bjgr,bjgrp->bgrpn", bc, decay_end, xc)
        return new_state, y_diag + y_off

    state0 = jnp.zeros((bsz, SSM_GROUPS, r, SSM_HEAD_DIM, SSM_STATE), jnp.float32)
    _, y = lax.scan(body, state0, (to_chunks(xdt), to_chunks(a), to_chunks(bm), to_chunks(cm)))
    return from_chunks(y).reshape(bsz, s, SSM_HEADS, SSM_HEAD_DIM)

def mamba2_mixer(z, xbc, dt_raw, conv_w, conv_b, dt_bias, a_log, d_skip, norm_w):
    dtype = z.dtype
    bsz, s = z.shape[:2]
    xbc = jax.nn.silu(causal_dwconv(xbc, conv_w) + conv_b.astype(xbc.dtype))
    xs, bm, cm = jnp.split(xbc.astype(jnp.float32),
                           [SSM_D_INNER, SSM_D_INNER + SSM_GROUPS * SSM_STATE], axis=-1)
    xs = xs.reshape(bsz, s, SSM_HEADS, SSM_HEAD_DIM)
    bm = bm.reshape(bsz, s, SSM_GROUPS, SSM_STATE)
    cm = cm.reshape(bsz, s, SSM_GROUPS, SSM_STATE)
    dt = jax.nn.softplus(dt_raw.astype(jnp.float32) + dt_bias.astype(jnp.float32))
    a = -jnp.exp(a_log.astype(jnp.float32))
    y = ssd_scan(xs * dt[..., None], dt * a, bm, cm)
    y = y + d_skip.astype(jnp.float32)[:, None] * xs
    y = y.reshape(bsz, s, SSM_D_INNER) * jax.nn.silu(z.astype(jnp.float32))
    y = y.reshape(bsz, s, SSM_GROUPS, SSM_D_INNER // SSM_GROUPS)
    y = y * lax.rsqrt(jnp.mean(y * y, axis=-1, keepdims=True) + EPS)
    y = y.reshape(bsz, s, SSM_D_INNER) * norm_w.astype(jnp.float32)
    return y.astype(dtype)

def gdn_scan(q, k, v, g, beta):
    bsz = q.shape[0]
    tril = jnp.tril(jnp.ones((CHUNK_3, CHUNK_3), dtype=bool))
    strict = jnp.tril(jnp.ones((CHUNK_3, CHUNK_3), dtype=bool), -1)
    eye = jnp.eye(CHUNK_3, dtype=jnp.float32)

    def body(state, inp):
        qc, kc, vc, gcv, bc = inp
        gc = jnp.cumsum(gcv, axis=1)
        gch = jnp.swapaxes(gc, 1, 2)
        decay = jnp.exp(jnp.where(tril, gch[..., :, None] - gch[..., None, :], -jnp.inf))
        kk = jnp.einsum("bihd,bjhd->bhij", kc, kc)
        amat = jnp.where(strict, kk * decay * jnp.swapaxes(bc, 1, 2)[..., :, None], 0.0)
        rhs = jnp.concatenate([vc * bc[..., None], kc * (bc * jnp.exp(gc))[..., None]], axis=-1)
        rhs = jnp.swapaxes(rhs, 1, 2)
        t = lax.linalg.triangular_solve(eye + amat, rhs, left_side=True, lower=True,
                                        unit_diagonal=True)
        u, w = t[..., :GDN_HEAD_V], t[..., GDN_HEAD_V:]
        v_new = u - jnp.einsum("bhqk,bhkv->bhqv", w, state)
        qk = jnp.einsum("bihd,bjhd->bhij", qc, kc) * decay
        o = (jnp.einsum("bihk,bhkv->bhiv", qc * jnp.exp(gc)[..., None], state)
             + jnp.einsum("bhij,bhjv->bhiv", qk, v_new))
        new_state = state * jnp.exp(gch[..., -1])[..., None, None] + jnp.einsum(
            "bjhk,bhjv->bhkv", kc * jnp.exp(gc[:, -1:] - gc)[..., None], v_new)
        return new_state, jnp.swapaxes(o, 1, 2)

    state0 = jnp.zeros((bsz, GDN_HEADS, GDN_HEAD_K, GDN_HEAD_V), jnp.float32)
    _, o = lax.scan(body, state0, (to_chunks(q), to_chunks(k), to_chunks(v),
                                   to_chunks(g), to_chunks(beta)))
    return from_chunks(o)

def gdn_mixer(qkv, z, a_raw, b_raw, conv_w, a_log, dt_bias, norm_w):
    dtype = z.dtype
    bsz, s = z.shape[:2]
    qkv = jax.nn.silu(causal_dwconv(qkv, conv_w)).astype(jnp.float32)
    q, k, v = jnp.split(qkv, [GDN_K_DIM, 2 * GDN_K_DIM], axis=-1)
    q = q.reshape(bsz, s, GDN_HEADS, GDN_HEAD_K)
    k = k.reshape(bsz, s, GDN_HEADS, GDN_HEAD_K)
    v = v.reshape(bsz, s, GDN_HEADS, GDN_HEAD_V)
    q = q * lax.rsqrt(jnp.sum(q * q, axis=-1, keepdims=True) + EPS) * (GDN_HEAD_K ** -0.5)
    k = k * lax.rsqrt(jnp.sum(k * k, axis=-1, keepdims=True) + EPS)
    beta = jax.nn.sigmoid(b_raw.astype(jnp.float32))
    g = -jnp.exp(a_log.astype(jnp.float32)) * jax.nn.softplus(
        a_raw.astype(jnp.float32) + dt_bias.astype(jnp.float32))
    o = gdn_scan(q, k, v, g, beta)
    o = o * lax.rsqrt(jnp.mean(o * o, axis=-1, keepdims=True) + EPS) * norm_w.astype(jnp.float32)
    o = o * jax.nn.silu(z.astype(jnp.float32).reshape(bsz, s, GDN_HEADS, GDN_HEAD_V))
    return o.reshape(bsz, s, GDN_V_DIM).astype(dtype)

def third_inputs(seed: int = 0) -> dict:
    key = jax.random.key(seed)
    ks = jax.random.split(key, 24)
    f32 = jnp.float32

    def nrm(k, shape, scale):
        return jax.random.normal(k, shape, f32) * scale

    def gain(k, shape):
        return 1.0 + 0.02 * jax.random.normal(k, shape, f32)

    def dt_bias_init(k, shape):
        dt = jnp.exp(jax.random.uniform(k, shape, f32, math.log(1e-3), math.log(1e-1)))
        return dt + jnp.log(-jnp.expm1(-dt))

    return {
        "x": jax.random.normal(ks[0], (BATCH, SEQ, D_MODEL), f32),
        "norm_mix_w": gain(ks[1], (DEPTH, D_MODEL)),
        "w_in": nrm(ks[2], (DEPTH, D_MODEL, IN_DIM), D_MODEL ** -0.5),
        "ssm_conv_w": nrm(ks[3], (DEPTH, CONV_K, SSM_CONV_DIM), CONV_K ** -0.5),
        "ssm_conv_b": nrm(ks[4], (DEPTH, SSM_CONV_DIM), 0.02),
        "ssm_dt_bias": dt_bias_init(ks[5], (DEPTH, SSM_HEADS)),
        "ssm_a_log": jnp.log(jax.random.uniform(ks[6], (DEPTH, SSM_HEADS), f32, 1.0, 16.0)),
        "ssm_d": gain(ks[7], (DEPTH, SSM_HEADS)),
        "ssm_norm_w": gain(ks[8], (DEPTH, SSM_D_INNER)),
        "gdn_conv_w": nrm(ks[9], (DEPTH, CONV_K, GDN_QKV_DIM), CONV_K ** -0.5),
        "gdn_a_log": jnp.log(jax.random.uniform(ks[10], (DEPTH, GDN_HEADS), f32, 1.0, 16.0)),
        "gdn_dt_bias": dt_bias_init(ks[11], (DEPTH, GDN_HEADS)),
        "gdn_norm_w": gain(ks[12], (DEPTH, GDN_HEAD_V)),
        "w_proj_ssm": nrm(ks[13], (DEPTH, SSM_D_INNER, D_MODEL), SSM_D_INNER ** -0.5),
        "w_proj_gdn": nrm(ks[14], (DEPTH, GDN_V_DIM, D_MODEL), GDN_V_DIM ** -0.5),
        "w_out": nrm(ks[15], (DEPTH, D_MODEL, D_MODEL), D_MODEL ** -0.5),
        "norm_ffn_w": gain(ks[16], (DEPTH, D_MODEL)),
        "w_ffn_in": nrm(ks[17], (DEPTH, D_MODEL, 2 * FFN_HIDDEN), D_MODEL ** -0.5),
        "w_ffn_down": nrm(ks[18], (DEPTH, FFN_HIDDEN, D_MODEL), FFN_HIDDEN ** -0.5),
        "final_norm_w": gain(ks[19], (D_MODEL,)),
    }

def third_block(x, norm_mix_w, w_in, ssm_conv_w, ssm_conv_b, ssm_dt_bias, ssm_a_log, ssm_d,
              ssm_norm_w, gdn_conv_w, gdn_a_log, gdn_dt_bias, gdn_norm_w, w_proj_ssm,
              w_proj_gdn, w_out, norm_ffn_w, w_ffn_in, w_ffn_down, final_norm_w):
    for l in range(DEPTH):
        h = rmsnorm(x, norm_mix_w[l])
        proj = h @ w_in[l]
        (ssm_z, ssm_xbc, ssm_dt, gdn_qkv, gdn_z, gdn_a, gdn_b,
         gate_ssm, gate_gdn) = jnp.split(proj, IN_SPLIT_IDX, axis=-1)
        y_ssm = mamba2_mixer(ssm_z, ssm_xbc, ssm_dt, ssm_conv_w[l], ssm_conv_b[l],
                             ssm_dt_bias[l], ssm_a_log[l], ssm_d[l], ssm_norm_w[l])
        y_gdn = gdn_mixer(gdn_qkv, gdn_z, gdn_a, gdn_b, gdn_conv_w[l], gdn_a_log[l],
                          gdn_dt_bias[l], gdn_norm_w[l])
        merged = (jax.nn.sigmoid(gate_ssm) * (y_ssm @ w_proj_ssm[l])
                  + jax.nn.sigmoid(gate_gdn) * (y_gdn @ w_proj_gdn[l]))
        x = x + merged @ w_out[l]
        h = rmsnorm(x, norm_ffn_w[l])
        gate, up = jnp.split(h @ w_ffn_in[l], [FFN_HIDDEN], axis=-1)
        x = x + (jax.nn.silu(gate) * up) @ w_ffn_down[l]
    return rmsnorm(x, final_norm_w)


_first_inputs_3 = third_inputs


def third_inputs(seed=0):
    import zlib

    import numpy as np

    out = dict(_first_inputs_3(seed))
    spreads = {}
    factors = {'norm_mix_w': 2.779,
     'ssm_conv_b': 4.141,
     'ssm_d': 8.0,
     'ssm_norm_w': 6.076,
     'gdn_norm_w': 8.0,
     'norm_ffn_w': 4.392,
     'final_norm_w': 2.838}
    for name, (base, spread) in spreads.items():
        noise = np.random.default_rng([zlib.crc32(name.encode()), seed]).standard_normal(out[name].shape)
        drawn = base * np.exp(spread * noise) if base else spread * noise
        out[name] = __import__('jax').numpy.asarray(drawn.astype(out[name].dtype))
    for name, factor in factors.items():
        out[name] = (out[name] * factor).astype(out[name].dtype)
    return out


_narrow_inputs_3 = third_inputs


def third_inputs(seed=0):

    out = dict(_narrow_inputs_3(seed))
    wider = {'ssm_conv_b': 3.7, 'ssm_d': 12.0, 'ssm_norm_w': 7.07, 'final_norm_w': 3.19}
    for name, times in wider.items():
        mean = out[name].mean()
        out[name] = (mean + times * (out[name] - mean)).astype(out[name].dtype)
    return out


def setup_inputs(seed=0):
    out = dict(first_inputs(seed))
    for name, value in second_inputs(seed + 1).items():
        if name != "x":
            out[name + "_2"] = value
    for name, value in third_inputs(seed + 2).items():
        if name != "x":
            out[name + "_3"] = value
    return out


def reference(
    x, rel_bias, attn_norm, w_in, q_norm, k_norm_cmp, k_norm_slc, k_norm_win, cmp_pe_k,
    cmp_w1_k, cmp_b1_k, cmp_w2_k, cmp_pe_v, cmp_w1_v, cmp_b1_v, cmp_w2_v, sgu_norm, sgu_w,
    sgu_b, w_out, ffn_norm, w_up, conv_w, conv_b, w_down, w_in_2, w_out_2, g_mix_2, lam_q1_2,
    lam_k1_2, lam_q2_2, lam_k2_2, g_subln_2, g_ffn_2, w_gate_2, w_up_2, w_down_2, g_final_2,
    norm_mix_w_3, w_in_3, ssm_conv_w_3, ssm_conv_b_3, ssm_dt_bias_3, ssm_a_log_3, ssm_d_3,
    ssm_norm_w_3, gdn_conv_w_3, gdn_a_log_3, gdn_dt_bias_3, gdn_norm_w_3, w_proj_ssm_3,
    w_proj_gdn_3, w_out_3, norm_ffn_w_3, w_ffn_in_3, w_ffn_down_3, final_norm_w_3,
):
    x = first_block(
        x, rel_bias, attn_norm, w_in, q_norm, k_norm_cmp, k_norm_slc, k_norm_win, cmp_pe_k,
        cmp_w1_k, cmp_b1_k, cmp_w2_k, cmp_pe_v, cmp_w1_v, cmp_b1_v, cmp_w2_v, sgu_norm, sgu_w,
        sgu_b, w_out, ffn_norm, w_up, conv_w, conv_b, w_down,
    )
    x = second_block(
        x, w_in_2, w_out_2, g_mix_2, lam_q1_2, lam_k1_2, lam_q2_2, lam_k2_2, g_subln_2, g_ffn_2,
        w_gate_2, w_up_2, w_down_2, g_final_2,
    )
    return third_block(
        x, norm_mix_w_3, w_in_3, ssm_conv_w_3, ssm_conv_b_3, ssm_dt_bias_3, ssm_a_log_3,
        ssm_d_3, ssm_norm_w_3, gdn_conv_w_3, gdn_a_log_3, gdn_dt_bias_3, gdn_norm_w_3,
        w_proj_ssm_3, w_proj_gdn_3, w_out_3, norm_ffn_w_3, w_ffn_in_3, w_ffn_down_3,
        final_norm_w_3,
    )


_drawn_inputs = setup_inputs


def setup_inputs(seed=0):
    import zlib

    import numpy as np

    out = dict(_drawn_inputs(seed))
    spreads = {}
    factors = {'cmp_b1_k': 3.767, 'k_norm_cmp': 2.838}
    for name, (base, spread) in spreads.items():
        noise = np.random.default_rng([zlib.crc32(name.encode()), seed]).standard_normal(out[name].shape)
        drawn = base * np.exp(spread * noise) if base else spread * noise
        out[name] = jnp.asarray(drawn.astype(out[name].dtype))
    for name, factor in factors.items():
        out[name] = (out[name] * factor).astype(out[name].dtype)
    return out
```

```python
import math
from contextlib import ExitStack, contextmanager

import numpy as np

import concourse.bass as bass
from concourse import mybir
from concourse.alu_op_type import AluOpType as ALU

F32 = mybir.dt.float32
ACT = mybir.ActivationFunctionType
AX_X = mybir.AxisListType.X

P = 128
T = 512
TT = T // P
D = 1024
KD = D // P
BANK = 512
BANKS = 8
D_FF = 2816
KF = D_FF // P
EPS = 1e-6
NEG = -1e30


X_AT = 0
H_AT = X_AT + KD * T
RING_AT = H_AT + KD * T
SLOT = KD * BANK
CONST_AT = RING_AT + 2 * SLOT
CONST_WORDS = 2000
WORK_AT = CONST_AT + CONST_WORDS
ARENA = 52176
WORK_WORDS = ARENA - WORK_AT


class Core:

    def __init__(self, nc):
        self.nc = nc
        self.arena = nc.alloc_sbuf_tensor("arena", [P, ARENA], F32)
        self.psum = nc.alloc_psum_tensor("psum", [P, BANKS, BANK], F32)
        self.x = self.cut(X_AT, KD, T)
        self.h = self.cut(H_AT, KD, T)
        self.const_used = CONST_AT

    def cut(self, at, *dims):
        n = int(np.prod(dims))
        assert at + n <= ARENA, (at, dims, ARENA)
        v = self.arena[:, at:at + n]
        if len(dims) == 2:
            v = v.rearrange("p (a b) -> p a b", a=dims[0])
        elif len(dims) == 3:
            v = v.rearrange("p (a b c) -> p a b c", a=dims[0], b=dims[1])
        return v

    def work(self, at, *dims):
        return self.cut(WORK_AT + at, *dims)

    def const(self, *dims):
        at = self.const_used
        self.const_used += int(np.prod(dims))
        assert self.const_used <= WORK_AT
        return self.cut(at, *dims)

    def slot(self, j, a, b):
        return self.cut(RING_AT + j * SLOT, a, b)

    def bank(self, b):
        return self.psum[:, b, :]


@contextmanager
def stage(nc, *names, from_one=()):
    mark = nc.get_next_instruction_name()
    sems = [nc.alloc_semaphore(f"{n}_{mark}") for n in names]
    for n in from_one:
        nc.sync.sem_inc(sems[names.index(n)], 1)
    with nc.Block() as block:
        yield (block, *sems)
    nc.clear_and_free_semaphores(sems)
    nc.all_engine_barrier()


class Count:

    def __init__(self, engine, sem, base=0):
        self.engine, self.sem, self.base, self.n = engine, sem, base, 0

    def step(self, ins):
        self.n += 1
        ins.then_inc(self.sem, 1)

    def settle(self):
        self.engine.wait_ge(self.sem, self.base + self.n)

    def link(self, ins):
        self.step(ins)
        self.settle()


def hold(engine, sem, value):
    engine.wait_ge(sem, value)
    engine.nop(nofuse=True)


def pairs(n):
    return n // 2, n % 2


def norm_stage(core, ones, gain, out=None):
    nc, x = core.nc, core.x
    out = core.h if out is None else out
    sq = core.cut(RING_AT, KD, T)
    rstd = core.cut(RING_AT + SLOT, 2, T)
    total = core.bank(0)
    with stage(nc, "squared", "summed", "mean_ready", "root_ready", "norm_steps") as (
            block, squared, summed, mean_ready, root_ready, norm_steps):
        @block.scalar
        def _(act):
            for k in range(KD):
                nc.scalar.activation(sq[:, k, :], x[:, k, :], ACT.Square).then_inc(squared, 1)
            act.wait_ge(mean_ready, 1)
            nc.scalar.activation(rstd[:, 1, :], rstd[:, 0, :], ACT.Sqrt).then_inc(root_ready, 1)

        @block.tensor
        def _(pe):
            for k in range(KD):
                pe.wait_ge(squared, k + 1)
                mm = nc.tensor.matmul(total, ones, sq[:, k, :], start=(k == 0), stop=(k == KD - 1))
            mm.then_inc(summed, 1)

        @block.vector
        def _(dve):
            steps = Count(dve, norm_steps)
            dve.wait_ge(summed, 1)
            nc.vector.tensor_scalar(rstd[:, 0, :], total, 1.0 / D, EPS, ALU.mult, ALU.add).then_inc(mean_ready, 1)
            dve.wait_ge(root_ready, 1)
            steps.link(nc.vector.reciprocal(rstd[:, 0, :], rstd[:, 1, :]))
            for k in range(KD):
                steps.step(nc.vector.scalar_tensor_tensor(
                    out=out[:, k, :], in0=x[:, k, :], scalar=gain[:, k:k + 1], in1=rstd[:, 0, :],
                    op0=ALU.mult, op1=ALU.mult))


def project_tokens(core, weight, cols, dst, func=None):
    nc, h = core.nc, core.h
    full, rest = cols // BANK, cols % BANK
    bodies, odd = pairs(full)
    tail = [(2 * bodies, BANK)] * odd + ([(full, rest)] if rest else [])
    with stage(nc, "weights0", "weights1", "products0", "products1", "stored0", "stored1",
               from_one=("products0", "products1", "stored0", "stored1")) as (block, *sems):
        weights, products, stored = sems[0:2], sems[2:4], sems[4:6]

        def each(engine, unit):
            if bodies:
                with engine.Fori(0, bodies) as i:
                    for j in range(2):
                        unit(i, j, (2 * i + j) * BANK, BANK)
            for j, (c, n) in enumerate(tail):
                unit(bodies, j, c * BANK, n)

        @block.sync
        def _(sp):
            def load(i, j, lo, n):
                sp.wait_ge(products[j], i + 1)
                sp.dma_start(core.slot(j, KD, BANK)[:, :, 0:n], weight(lo, n)).then_inc(weights[j], 16)
            each(sp, load)

        @block.tensor
        def _(pe):
            def multiply(i, j, lo, n):
                pe.wait_ge(weights[j], 16 * i + 16)
                pe.wait_ge(stored[j], 4 * i + 1)
                w = core.slot(j, KD, BANK)
                for t in range(TT):
                    for k in range(KD):
                        mm = nc.tensor.matmul(core.bank(4 * j + t)[:, 0:n], h[:, k, t * P:(t + 1) * P],
                                              w[:, k, 0:n], start=(k == 0), stop=(k == KD - 1))
                mm.then_inc(products[j], 1)
            each(pe, multiply)

        @block.vector
        def _(dve):
            def store(i, j, lo, n):
                dve.wait_ge(products[j], i + 2)
                for t in range(TT):
                    to = dst[:, t, bass.ds(lo, n)]
                    nc.vector.tensor_copy(to, core.bank(4 * j + t)[:, 0:n]).then_inc(stored[j], 1)
            if func is None:
                each(dve, store)

        @block.scalar
        def _(act):
            def store(i, j, lo, n):
                hold(act, products[j], i + 2)
                for t in range(TT):
                    to = dst[:, t, bass.ds(lo, n)]
                    nc.scalar.activation(to, core.bank(4 * j + t)[:, 0:n], func).then_inc(stored[j], 1)
            if func is not None:
                each(act, store)


def rows_product(core, src, tiles, weight, finish):
    nc = core.nc
    units = tiles // 2
    bodies, odd = pairs(units)
    with stage(nc, "weights0", "weights1", "products0", "products1", "banks_full", "finished") as (
            block, *sems):
        weights, products, banks_full, finished = sems[0:2], sems[2:4], sems[4], sems[5]

        @block.sync
        def _(sp):
            def load(i, j, first=False):
                if not first:
                    sp.wait_ge(products[j], i)
                sp.dma_start(core.slot(j, 2, D), weight(4 * i + 2 * j)).then_inc(weights[j], 16)
            load(0, 0, first=True)
            load(0, 1, first=True)
            with sp.Fori(1, bodies) as i:
                load(i, 0)
                load(i, 1)
            if odd:
                load(bodies, 0)

        @block.tensor
        def _(pe):
            def multiply(i, j, first=False, last=False):
                pe.wait_ge(weights[j], 16 * i + 16)
                w = core.slot(j, 2, D)
                for a in range(2):
                    for m in range(KD):
                        mm = nc.tensor.matmul(core.bank(m), w[:, a, m * P:(m + 1) * P],
                                              src[:, 4 * i + 2 * j + a, :],
                                              start=(first and a == 0), stop=(last and a == 1))
                        if last and a == 1:
                            mm.then_inc(banks_full, 1)
                if not last:
                    mm.then_inc(products[j], 1)
            multiply(0, 0, first=True)
            multiply(0, 1)
            if bodies - 1 - (1 - odd) > 0:
                with pe.Fori(1, bodies - (1 - odd)) as i:
                    multiply(i, 0)
                    multiply(i, 1)
            if odd:
                multiply(bodies, 0, last=True)
            else:
                multiply(bodies - 1, 0)
                multiply(bodies - 1, 1, last=True)

        @block.vector
        def _(dve):
            for m in range(KD):
                dve.wait_ge(banks_full, m + 1)
                finish(m).then_inc(finished, 1)


def add_to_residual(core):
    def finish(m):
        return core.nc.vector.tensor_tensor(core.x[:, m, :], core.x[:, m, :], core.bank(m), ALU.add)
    return finish


UNIT_COLS = 256
FF_UNITS = D_FF // UNIT_COLS
UT = UNIT_COLS // P


def gated_hidden(core, gate_w, up_w, hidden, conv=None):
    nc, h = core.nc, core.h
    bodies, odd = pairs(FF_UNITS)
    scratch = core.work(KF * T, 4 * UT, T)
    taps, width, bias = conv if conv else (None, 0, None)
    with stage(nc, "weights0", "weights1", "products0", "products1", "silu0", "silu1",
               "hidden0", "hidden1", "biased", "convolved", "conv_steps",
               from_one=("products0", "products1", "hidden0", "hidden1")) as (block, *sems):
        weights, products, silus, hiddens = sems[0:2], sems[2:4], sems[4:6], sems[6:8]
        biased, convolved, conv_steps = sems[8:11]

        def each(engine, unit):
            with engine.Fori(0, bodies) as i:
                for j in range(2):
                    unit(i, j)
            if odd:
                unit(bodies, 0)

        def tile(i, j, m):
            return (2 * i + j) * UT + m

        @block.sync
        def _(sp):
            def load(i, j):
                lo = (2 * i + j) * UNIT_COLS
                sp.wait_ge(products[j], 2 * UT * i + 1)
                w = core.slot(j, 2 * KD, UNIT_COLS)
                sp.dma_start(w[:, 0:KD, :], gate_w(lo, UNIT_COLS)).then_inc(weights[j], 16)
                sp.dma_start(w[:, KD:2 * KD, :], up_w(lo, UNIT_COLS)).then_inc(weights[j], 16)
            each(sp, load)

        @block.tensor
        def _(pe):
            def multiply(i, j):
                pe.wait_ge(weights[j], 32 * i + 32)
                pe.wait_ge(hiddens[j], UT * i + 1)
                w = core.slot(j, 2 * KD, UNIT_COLS)
                for part in range(2):
                    for m in range(UT):
                        for k in range(KD):
                            mm = nc.tensor.matmul(core.bank(4 * j + UT * part + m),
                                                  w[:, KD * part + k, m * P:(m + 1) * P], h[:, k, :],
                                                  start=(k == 0), stop=(k == KD - 1))
                        mm.then_inc(products[j], 1)
            each(pe, multiply)

        @block.scalar
        def _(act):
            def work(i, j):
                if conv is None:
                    for m in range(UT):
                        act.wait_ge(products[j], 2 * UT * i + m + 2)
                        act.wait_ge(hiddens[j], UT * i + 1)
                        nc.scalar.activation(scratch[:, 2 * UT * j + m, :], core.bank(4 * j + m),
                                             ACT.Silu).then_inc(silus[j], 1)
                    return
                base = 2 * UT * (2 * i + j)
                for n in range(2 * UT):
                    part, m = n // UT, n % UT
                    act.wait_ge(products[j], 2 * UT * i + n + 2)
                    hold(act, hiddens[j], UT * i + 1)
                    f = (1 - part) * KF
                    nc.scalar.activation(scratch[:, 2 * UT * j + n, :], core.bank(4 * j + n), ACT.Identity,
                                         scale=taps[:, bass.ds(2 * KF * (width - 1) + f + tile(i, j, m), 1)],
                                         bias=bias[:, bass.ds(f + tile(i, j, m), 1)]).then_inc(biased, 1)
                for m in range(UT):
                    act.wait_ge(convolved, base + m + 1)
                    nc.scalar.activation(scratch[:, 2 * UT * j + m, :], scratch[:, 2 * UT * j + m, :],
                                         ACT.Silu).then_inc(silus[j], 1)
            each(act, work)

        @block.vector
        def _(dve):
            def work(i, j):
                base = 2 * UT * (2 * i + j)
                for n in range(2 * UT if conv else 0):
                    part, m = n // UT, n % UT
                    dve.wait_ge(biased, base + n + 1)
                    f = (1 - part) * KF
                    s = scratch[:, 2 * UT * j + n, :]
                    for back in range(1, width):
                        tap = taps[:, bass.ds(2 * KF * (width - 1 - back) + f + tile(i, j, m), 1)]
                        ins = nc.vector.scalar_tensor_tensor(
                            out=s[:, back:T], in0=core.bank(4 * j + n)[:, 0:T - back], scalar=tap,
                            in1=s[:, back:T], op0=ALU.mult, op1=ALU.add)
                        if back < width - 1:
                            ins.then_inc(conv_steps, 1)
                            dve.wait_ge(conv_steps, (width - 2) * (base + n) + back)
                    ins.then_inc(convolved, 1)
                for m in range(UT):
                    dve.wait_ge(silus[j], UT * i + m + 1)
                    if conv is None:
                        dve.wait_ge(products[j], 2 * UT * i + UT + m + 2)
                        up = core.bank(4 * j + UT + m)
                    else:
                        dve.wait_ge(convolved, base + UT + m + 1)
                        up = scratch[:, 2 * UT * j + UT + m, :]
                    nc.vector.tensor_tensor(hidden[:, tile(i, j, m), :], scratch[:, 2 * UT * j + m, :], up,
                                            ALU.mult).then_inc(hiddens[j], 1)
            each(dve, work)


def flip(core, jobs, ident, evac_scale=None):
    nc = core.nc
    with stage(nc, "turned", "stored_act", "stored_dve") as (block, turned, stored_act, stored_dve):
        stored = [stored_act, stored_dve]

        @block.tensor
        def _(pe):
            for n, (sources, dst, scale) in enumerate(jobs):
                if n >= BANKS:
                    pe.wait_ge(stored[n % 2], (n - BANKS) // 2 + 1)
                at = 0
                for src in sources:
                    p, c = src.shape
                    mm = nc.tensor.transpose(core.bank(n % BANKS)[0:c, at:at + p], src, ident[0:p, 0:p])
                    at += p
                mm.then_inc(turned, 1)

        def store(engine, parity, put):
            for n, (sources, dst, scale) in enumerate(jobs):
                if n % 2 == parity:
                    c, w = dst.shape
                    all_w = sum(src.shape[0] for src in sources)
                    engine.wait_ge(turned, n + 1)
                    put(dst, core.bank(n % BANKS)[0:c, all_w - w:all_w], scale).then_inc(stored[parity], 1)

        @block.scalar
        def _(act):
            store(act, 0, lambda to, what, scale: nc.scalar.activation(to, what, ACT.Copy, scale=scale))

        @block.vector
        def _(dve):
            store(dve, 1, lambda to, what, scale: nc.vector.tensor_scalar(to, what, scale, None, ALU.mult))


DH = 64
ATTEND_WORDS = 8 * T + 16


def attend(core, scratch_at, ident, loops, unroll, q_of, k_of, v_of, bias_of, out_of, width, keys):
    nc = core.nc
    qs = core.work(scratch_at, 2, T)
    sb = core.work(scratch_at + 2 * T, 2, T)
    pb = core.work(scratch_at + 4 * T, 2, T)
    pt = core.work(scratch_at + 6 * T, 2, T)
    stats = core.work(scratch_at + 8 * T, 4, 4)
    steps = unroll * TT

    def cuts(n):
        return [(k, min(P, n - k)) for k in range(0, n, P)]

    with stage(nc, "q_ready", "scored", "biased", "max_ready", "exp_done", "turned", "turned_stored",
               "weighed", "sum_inverted", "out_done",
               from_one=("scored", "biased", "max_ready", "exp_done", "turned", "turned_stored", "weighed",
                         "sum_inverted", "out_done")) as (
            block, q_ready, scored, biased, max_ready, exp_done, turned, turned_stored,
            weighed, sum_inverted, out_done):

        @block.gpsimd
        def _(pool):
            with pool.Fori(0, loops) as i:
                base = i * steps + 1
                for u in range(unroll):
                    if u >= 2:
                        hold(pool, scored, base + TT * (u - 1))
                    else:
                        hold(pool, weighed, base)
                    nc.gpsimd.tensor_copy(qs[0:DH, u % 2, :], q_of(i, u)).then_inc(q_ready, 1)

        @block.tensor
        def _(pe):
            with pe.Fori(0, loops) as i:
                base = i * steps + 1
                for n in range(steps + 2):
                    if n < steps:
                        u, t, b = n // TT, n % TT, n % 2
                        nk = keys(t)
                        if t == 0:
                            pe.wait_ge(q_ready, i * unroll + u + 1)
                        if n >= 2:
                            pe.wait_ge(biased, base + n - 1)
                        pe.nop(nofuse=True)
                        nc.tensor.matmul(core.bank(b)[:, 0:nk], qs[0:DH, u % 2, t * P:(t + 1) * P],
                                         k_of(i, u, nk), start=True, stop=True).then_inc(scored, 1)
                    if 1 <= n <= steps:
                        s = n - 1
                        t, b = s % TT, s % 2
                        pe.wait_ge(exp_done, base + s + 1)
                        if s >= 2:
                            pe.wait_ge(turned_stored, base + s - 1)
                        for k, kn in cuts(keys(t)):
                            mm = nc.tensor.transpose(core.bank(2 + b)[0:kn, k:k + P], pb[:, b, k:k + kn], ident)
                        mm.then_inc(turned, 1)
                    if n >= 2:
                        s = n - 2
                        u, t, b = s // TT, s % TT, s % 2
                        pe.wait_ge(turned_stored, base + s + 1)
                        pe.wait_ge(out_done, base + (s - 1 if s >= 2 else 0))
                        pe.nop(nofuse=True)
                        parts = cuts(keys(t))
                        for c, (k, kn) in enumerate(parts):
                            mm = nc.tensor.matmul(core.bank(4 + b)[:, 0:width], pt[0:kn, b, k:k + P],
                                                  v_of(i, u, c, kn), start=(c == 0), stop=(c == len(parts) - 1))
                        mm.then_inc(weighed, 1)

        @block.vector
        def _(dve):
            with dve.Fori(0, loops) as i:
                base = i * steps + 1
                for n in range(steps + 2):
                    if n < steps:
                        u, t, b = n // TT, n % TT, n % 2
                        nk = keys(t)
                        dve.wait_ge(scored, base + n + 1)
                        dve.wait_ge(exp_done, base + (n - 1 if n >= 2 else 0))
                        nc.vector.tensor_tensor(sb[:, b, 0:nk], core.bank(b)[:, 0:nk], bias_of(i, u, t, nk),
                                                ALU.add).then_inc(biased, 1)
                        dve.wait_ge(biased, base + n + 1)
                        nc.vector.tensor_reduce(stats[:, n % 4, 1:2], sb[:, b, 0:nk], AX_X, ALU.max,
                                                negate=True).then_inc(max_ready, 1)
                    if n >= 2:
                        s = n - 2
                        u, t, b = s // TT, s % TT, s % 2
                        dve.wait_ge(exp_done, base + s + 1)
                        nc.vector.reciprocal(stats[:, s % 4, 3:4], stats[:, s % 4, 2:3]).then_inc(sum_inverted, 1)
                        dve.wait_ge(sum_inverted, base + s + 1)
                        dve.wait_ge(weighed, base + s + 1)
                        nc.vector.tensor_scalar(out_of(i, u, t), core.bank(4 + b)[:, 0:width],
                                                stats[:, s % 4, 3:4], None, ALU.mult).then_inc(out_done, 1)

        @block.scalar
        def _(act):
            with act.Fori(0, loops) as i:
                base = i * steps + 1
                for n in range(steps + 1):
                    if n < steps:
                        t, b = n % TT, n % 2
                        nk = keys(t)
                        act.wait_ge(max_ready, base + n + 1)
                        act.wait_ge(turned, base + (n - 1 if n >= 2 else 0))
                        nc.scalar.activation(pb[:, b, 0:nk], sb[:, b, 0:nk], ACT.Exp,
                                             bias=stats[:, n % 4, 1:2],
                                             accum_out=stats[:, n % 4, 2:3]).then_inc(exp_done, 1)
                    if n >= 1:
                        s = n - 1
                        t, b = s % TT, s % 2
                        act.wait_ge(turned, base + s + 1)
                        act.wait_ge(weighed, base + (s - 1 if s >= 2 else 0))
                        parts = cuts(keys(t))
                        kn, kw = parts[0][1], P * len(parts)
                        nc.scalar.copy(pt[0:kn, b, 0:kw], core.bank(2 + b)[0:kn, 0:kw]).then_inc(turned_stored, 1)


def load_stage(nc, pairs_of):
    with stage(nc, "small_loaded") as (block, small_loaded):
        @block.sync
        def _(sp):
            for dst, src in pairs_of:
                sp.dma_start(dst, src).then_inc(small_loaded, 16)
            sp.wait_ge(small_loaded, 16 * len(pairs_of))


def load_input(core, x, ident):
    nc = core.nc
    xt = core.work(0, TT, D)
    load_stage(nc, [(xt, x.rearrange("(t p) d -> p t d", p=P))])
    flip(core, [([xt[:, t, k * P:(k + 1) * P] for t in range(TT)], core.x[:, k, :], 1.0) for k in range(KD)], ident)


def store_output(core, src, y, ident):
    nc = core.nc
    yt = core.work(0, TT, D)
    flip(core, [([src[:, 4 * g + k, t * P:(t + 1) * P] for k in range(4)],
                 yt[:, t, g * 4 * P:(g + 1) * 4 * P], 1.0) for t in range(TT) for g in range(KD // 4)], ident)
    with stage(nc, "written") as (block, written):
        @block.sync
        def _(sp):
            sp.dma_start(y.rearrange("(t p) d -> p t d", p=P), yt).then_inc(written, 16)
            sp.wait_ge(written, 16)


def load_columns(core, rows_at, entries, dst, ident, width=P):
    parts, at = [], 0
    for src in entries:
        r = src.shape[0]
        done = 0
        while done < r:
            n = min(r - done, P - at % P)
            parts.append((at // P, at % P, n, src[done:done + n, :]))
            at += n
            done += n
    tiles = -(-at // P)
    rows = core.work(rows_at, tiles, P)
    load_stage(core.nc, [(rows[p:p + n, tile, 0:width], src) for tile, p, n, src in parts])
    flip(core, [([rows[0:min(P, at - P * c), c, 0:width] for c in range(tiles)], dst[0:width, 0:at], 1.0)], ident)


Q_HEADS, KV = 8, 2
GROUP = Q_HEADS // KV
D_Q, D_KV = Q_HEADS * DH, KV * DH
Q_COL = 0
KC_COL = Q_COL + D_Q
VC_COL, KS_COL, VS_COL, KW_COL, VW_COL = (KC_COL + D_KV * n for n in range(1, 6))
GATE_COL = VW_COL + D_KV
BRANCHES = 3
U_COL = GATE_COL + Q_HEADS * BRANCHES
D_GMLP = 512
V_COL = U_COL + D_GMLP
D_PROJ = V_COL + D_GMLP
CMP_BLOCK, CMP_STRIDE, CMP_HIDDEN = 32, 16, 256
CMP_N = (T - CMP_BLOCK) // CMP_STRIDE + 1
REL_BUCKETS, REL_MAX_DIST = 32, 128
SGU_GROUPS = 8
BIAS_ROW = T + P


def head_norms(core, views, at, sq_words=4 * T):
    nc = core.nc
    sizes = [v.shape[1] * v.shape[2] for v in views]
    total = sum(sizes)
    p = views[0].shape[0]
    sq = core.work(at, sq_words)
    ms = core.work(at + sq_words, 3, total)
    with stage(nc, "norm_steps", "mean_ready", "root_ready") as (block, norm_steps, mean_ready, root_ready):
        @block.scalar
        def _(act):
            act.wait_ge(mean_ready, len(views))
            nc.scalar.activation(ms[0:p, 1, :], ms[0:p, 0, :], ACT.Sqrt).then_inc(root_ready, 1)

        @block.vector
        def _(dve):
            steps = Count(dve, norm_steps)
            lo = 0
            for v, n in zip(views, sizes):
                a, heads, width = v.shape[1:]
                s = sq[0:p, 0:n * width].rearrange("p (a h w) -> p a h w", a=a, h=heads)
                m = ms[0:p, 0, lo:lo + n].rearrange("p (a h) -> p a h", a=a)
                steps.link(nc.vector.tensor_tensor(s, v, v, ALU.mult))
                steps.link(nc.vector.tensor_reduce(m, s, AX_X, ALU.add))
                nc.vector.tensor_scalar(m, m, 1.0 / width, EPS, ALU.mult, ALU.add).then_inc(mean_ready, 1)
                lo += n
            dve.wait_ge(root_ready, 1)
            steps.link(nc.vector.reciprocal(ms[0:p, 2, :], ms[0:p, 1, :]))
            lo = 0
            for v, n in zip(views, sizes):
                a, heads, width = v.shape[1:]
                r = ms[0:p, 2, lo:lo + n].rearrange("p (a h) -> p a h", a=a)
                steps.step(nc.vector.tensor_tensor(v, v, r.unsqueeze(3).broadcast_to([p, a, heads, width]), ALU.mult))
                lo += n


def bias_stage(core, a, bias, scratch_dram, at):
    nc = core.nc
    table = core.work(at, Q_HEADS)
    buckets = core.work(at + Q_HEADS, BIAS_ROW)
    rows = core.work(at + Q_HEADS + BIAS_ROW, BIAS_ROW)
    back = core.work(at + Q_HEADS + 2 * BIAS_ROW, P)
    shifted = core.slot(0, KD, BANK)
    with stage(nc, "small_loaded", "table_ready", "rows_ready", "rows_stored", "shifted_ready", "round_ready",
               "rows_saved", "bias_stored") as (
            block, small_loaded, table_ready, rows_ready, rows_stored, shifted_ready, round_ready, rows_saved,
            bias_stored):
        @block.gpsimd
        def _(pool):
            nc.gpsimd.memset(table[REL_BUCKETS:REL_BUCKETS + 1, :], NEG).then_inc(table_ready, 1)

        @block.sync
        def _(sp):
            sp.dma_start(table[0:REL_BUCKETS, :], a["rel_bias"]).then_inc(small_loaded, 16)
            sp.dma_start(buckets[0:REL_BUCKETS + 1, :], a["buckets"]).then_inc(small_loaded, 16)
            sp.dma_start(back, a["reversed"]).then_inc(small_loaded, 16)
            sp.wait_ge(rows_stored, 2)
            sp.dma_start(scratch_dram, rows[0:Q_HEADS, :]).then_inc(rows_saved, 16)
            sp.wait_ge(rows_saved, 16)
            for h in range(Q_HEADS):
                sp.dma_start(shifted[:, h, :], bass.AP(scratch_dram.tensor, h * BIAS_ROW, [[1, P], [1, T]])
                             ).then_inc(shifted_ready, 16)

        @block.tensor
        def _(pe):
            pe.wait_ge(small_loaded, 48)
            pe.wait_ge(table_ready, 1)
            n = REL_BUCKETS + 1
            for c, (lo, w) in enumerate([(0, T), (T, BIAS_ROW - T)]):
                nc.tensor.matmul(core.bank(c)[0:Q_HEADS, 0:w], table[0:n, :], buckets[0:n, lo:lo + w],
                                 start=True, stop=True).then_inc(rows_ready, 1)
            pe.wait_ge(rows_stored, 2)
            pe.wait_ge(shifted_ready, 16 * Q_HEADS)
            for h in range(Q_HEADS):
                nc.tensor.matmul(core.bank(h), back, shifted[:, h, :], start=True, stop=True).then_inc(round_ready, 1)

        @block.vector
        def _(dve):
            for c, (lo, w) in enumerate([(0, T), (T, BIAS_ROW - T)]):
                dve.wait_ge(rows_ready, c + 1)
                nc.vector.tensor_copy(rows[0:Q_HEADS, lo:lo + w], core.bank(c)[0:Q_HEADS, 0:w]).then_inc(rows_stored, 1)
            for h in range(Q_HEADS):
                dve.wait_ge(round_ready, h + 1)
                nc.vector.tensor_copy(bias[:, h, :], core.bank(h)).then_inc(bias_stored, 1)


def activation_stage(core, jobs):
    nc = core.nc
    with stage(nc, "activated") as (block, activated):
        @block.scalar
        def _(act):
            for out, x, func in jobs:
                nc.scalar.activation(out, x, func).then_inc(activated, 1)


def compress_stage(core, a, turned, pe_cols, b1_cols, out, at):
    nc = core.nc
    pairs_n = CMP_BLOCK // 2
    N = KV * CMP_N
    blocks = core.work(at, 2 * pairs_n, N)
    hid = core.work(at + 2 * pairs_n * N, 4, N)
    w2 = core.work(at + 2 * pairs_n * N + 4 * N, 4, DH)
    hid_tiles = CMP_HIDDEN // P
    with stage(nc, "weights_in", "blocks_ready", "hidden_ready", "hidden_stored", "compressed", "out_stored") as (
            block, weights_in, blocks_ready, hidden_ready, hidden_stored, compressed, out_stored):
        @block.sync
        def _(sp):
            for kind, name in enumerate("kv"):
                w1 = a[f"cmp_w1_{name}"][0].rearrange("(c p) n -> p c n", p=P)
                sp.dma_start(core.slot(kind, pairs_n, CMP_HIDDEN), w1).then_inc(weights_in, 16)
                sp.dma_start(w2[:, 2 * kind:2 * kind + 2, :],
                             a[f"cmp_w2_{name}"][0].rearrange("(k p) n -> p k n", p=P)).then_inc(weights_in, 16)

        @block.vector
        def _(dve):
            half = pairs_n // 2
            for kind in range(2):
                for g in range(KV):
                    x = turned[kind][:, g, :].rearrange("p (n s) -> p s n", s=CMP_STRIDE)
                    for hh in range(2):
                        c = kind * pairs_n + half * hh
                        pe_v = pe_cols[:, c:c + half].unsqueeze(2).broadcast_to([P, half, CMP_N])
                        nc.vector.tensor_tensor(blocks[:, c:c + half, g * CMP_N:(g + 1) * CMP_N],
                                                x[:, 0:CMP_STRIDE:2, hh:hh + CMP_N], pe_v,
                                                ALU.add).then_inc(blocks_ready, 1)
            for kind in range(2):
                for g in range(KV):
                    n = kind * KV + g
                    dve.wait_ge(compressed, n + 1)
                    nc.vector.tensor_copy(out[kind][0:CMP_N, g, :], core.bank(4 + n)[0:CMP_N, 0:DH]).then_inc(out_stored, 1)

        @block.tensor
        def _(pe):
            pe.wait_ge(weights_in, 64)
            pe.wait_ge(blocks_ready, 8)
            for kind in range(2):
                w1 = core.slot(kind, pairs_n, CMP_HIDDEN)
                for m in range(hid_tiles):
                    for c in range(pairs_n):
                        mm = nc.tensor.matmul(core.bank(2 * kind + m)[:, 0:N], w1[:, c, m * P:(m + 1) * P],
                                              blocks[:, kind * pairs_n + c, :], start=(c == 0), stop=(c == pairs_n - 1))
                    mm.then_inc(hidden_ready, 1)
            for kind in range(2):
                pe.wait_ge(hidden_stored, 2 * kind + 2)
                for g in range(KV):
                    for k in range(hid_tiles):
                        mm = nc.tensor.matmul(core.bank(4 + kind * KV + g)[0:CMP_N, 0:DH],
                                              hid[:, 2 * kind + k, g * CMP_N:(g + 1) * CMP_N],
                                              w2[:, 2 * kind + k, :], start=(k == 0), stop=(k == hid_tiles - 1))
                    mm.then_inc(compressed, 1)

        @block.scalar
        def _(act):
            for n in range(4):
                act.wait_ge(hidden_ready, n + 1)
                nc.scalar.activation(hid[:, n, :], core.bank(n)[:, 0:N], ACT.Gelu_apprx_tanh,
                                     bias=b1_cols[:, n:n + 1]).then_inc(hidden_stored, 1)


def spatial_stage(core, pr, w_T, keep, gain_row, bias_cols, mixed, col):
    nc = core.nc
    width = D_GMLP // SGU_GROUPS
    v = pr[:, :, V_COL:V_COL + D_GMLP]
    with stage(nc, "masked", "gained", "mixed_ready", "gated") as (block, masked, gained, mixed_ready, gated):
        @block.gpsimd
        def _(pool):
            nc.gpsimd.tensor_tensor(w_T, w_T, keep.unsqueeze(1).broadcast_to([P, SGU_GROUPS, P]),
                                    ALU.mult).then_inc(masked, 1)

        @block.tensor
        def _(pe):
            pe.wait_ge(masked, 1)
            pe.wait_ge(gained, 1)
            for g in range(SGU_GROUPS):
                nc.tensor.matmul(core.bank(g)[:, 0:TT * width], w_T[:, g, :], v[:, :, g * width:(g + 1) * width],
                                 start=True, stop=True).then_inc(mixed_ready, 1)

        @block.vector
        def _(dve):
            nc.vector.tensor_tensor(v, v, gain_row.unsqueeze(1).broadcast_to([P, TT, D_GMLP]),
                                    ALU.mult).then_inc(gained, 1)
            for g in range(SGU_GROUPS):
                dve.wait_ge(mixed_ready, g + 1)
                nc.vector.scalar_tensor_tensor(
                    out=mixed[:, :, col + g * width:col + (g + 1) * width],
                    in0=core.bank(g)[:, 0:TT * width].rearrange("p (t w) -> p t w", t=TT),
                    scalar=bias_cols[:, g:g + 1],
                    in1=pr[:, :, U_COL + g * width:U_COL + (g + 1) * width],
                    op0=ALU.add, op1=ALU.mult).then_inc(gated, 1)


def branches_stage(core, outs, gates, row_valid, mixed):
    nc = core.nc
    with stage(nc, "valid_ready", "scaled", "summed") as (block, valid_ready, scaled, summed):
        def scale(engine, n):
            o = outs[n].rearrange("p t (h w) -> p t h w", h=Q_HEADS)
            g = gates[:, :, n:Q_HEADS * BRANCHES:BRANCHES].unsqueeze(3).broadcast_to([P, TT, Q_HEADS, DH])
            engine.tensor_tensor(o, o, g, ALU.mult).then_inc(scaled, 1)

        @block.gpsimd
        def _(pool):
            scale(nc.gpsimd, 2)

        @block.vector
        def _(dve):
            nc.vector.tensor_scalar(gates[:, 0, 0:Q_HEADS * BRANCHES:BRANCHES],
                                    gates[:, 0, 0:Q_HEADS * BRANCHES:BRANCHES], row_valid, None,
                                    ALU.mult).then_inc(valid_ready, 1)
            scale(nc.vector, 1)
            dve.wait_ge(valid_ready, 1)
            scale(nc.vector, 0)
            dve.wait_ge(scaled, 3)
            m = mixed[:, :, 0:D_Q]
            nc.vector.tensor_tensor(m, outs[0], outs[1], ALU.add).then_inc(summed, 1)
            dve.wait_ge(summed, 1)
            nc.vector.tensor_tensor(m, m, outs[2], ALU.add).then_inc(summed, 1)


def first_block(core, a, scratch_dram, ident, ones):
    nc = core.nc
    cols = core.const(2 * KD + SGU_GROUPS + CMP_BLOCK + 4)
    heads_cols = core.const(5)
    taps = core.const(3 * 2 * KF + 2 * KF)
    row_valid = core.const(1)
    kc_T = core.const(KV, CMP_N)
    kc = core.const(KV, DH)
    vc = core.const(KV, DH)
    PE_AT, B1_AT = 2 * KD + SGU_GROUPS, 2 * KD + SGU_GROUPS + CMP_BLOCK
    pr = core.work(0, TT, D_PROJ)
    at = TT * D_PROJ
    bias = core.work(at, Q_HEADS, T)
    qT = core.work(at + 8 * T, Q_HEADS, T)
    kT = core.work(at + 16 * T, 2 * KV, T)
    scratch_at = at + 20 * T
    ob_at = scratch_at + ATTEND_WORDS
    outs = [core.work(ob_at + n * TT * D_Q, TT, D_Q) for n in range(BRANCHES)]
    mixed = core.cut(H_AT, TT, D)
    mixed_T = core.work(at + 8 * T, KD, T)

    rows = lambda v: v.rearrange("(k p) -> k p", p=P)
    pe_rows = lambda v: v.rearrange("(c a) d -> c (a d)", a=2)
    load_columns(core, 0, [rows(a["attn_norm"][0]), rows(a["ffn_norm"][0]), a["sgu_b"][0],
                           pe_rows(a["cmp_pe_k"][0]), pe_rows(a["cmp_pe_v"][0]),
                           rows(a["cmp_b1_k"][0]), rows(a["cmp_b1_v"][0])], cols, ident)
    load_columns(core, 0, [a[n] for n in ("q_norm", "k_norm_cmp", "k_norm_slc", "k_norm_win")], heads_cols,
                 ident, width=DH)
    load_columns(core, 0, [a["conv_w"][0].rearrange("w (f p) -> (w f) p", p=P), rows(a["conv_b"][0])], taps, ident)
    norm_stage(core, ones, cols[:, 0:KD])
    project_tokens(core, columns_of(a["w_in"][0]), D_PROJ, pr)
    bias_stage(core, a, bias, scratch_dram, scratch_at)

    gates = pr[:, :, GATE_COL:GATE_COL + Q_HEADS * BRANCHES]
    activation_stage(core, [(pr[:, t, U_COL:U_COL + 2 * D_GMLP],) * 2 + (ACT.Gelu_apprx_tanh,) for t in range(TT)]
                     + [(gates, gates, ACT.Sigmoid)])
    by_head = lambda lo, heads, w: pr[:, :, lo:lo + heads * w].rearrange("p t (h w) -> p t h w", h=heads)
    head_norms(core, [by_head(Q_COL, Q_HEADS, DH), by_head(KS_COL, KV, DH), by_head(KW_COL, KV, DH),
                      by_head(V_COL, 1, D_GMLP)], scratch_at)

    w_sgu = core.work(scratch_at, SGU_GROUPS, P)
    w_T = core.work(scratch_at + SGU_GROUPS * P, SGU_GROUPS, P)
    gain_row = core.work(scratch_at + 2 * SGU_GROUPS * P, D_GMLP)
    keep = core.work(scratch_at + 2 * SGU_GROUPS * P + D_GMLP, P)
    load_stage(nc, [(w_sgu, a["sgu_w"][0].rearrange("g i j -> i g j")),
                    (gain_row, a["sgu_norm"][0].partition_broadcast(P)),
                    (keep, a["upper"]), (row_valid, a["row_valid"])])
    flip(core, [([w_sgu[:, g, :]], w_T[:, g, :], 1.0) for g in range(SGU_GROUPS)], ident)
    spatial_stage(core, pr, w_T, keep, gain_row, cols[:, 2 * KD:2 * KD + SGU_GROUPS], mixed, D_Q)

    pair_T = [core.work(scratch_at + KV * T * kind, KV, T) for kind in range(2)]
    jobs = []
    for kind, lo in enumerate((KC_COL, VC_COL)):
        for g in range(KV):
            src = [pr[:, t, lo + g * DH:lo + (g + 1) * DH] for t in range(TT)]
            jobs.append((src, pair_T[kind][0:DH, g, :], 1.0))
            jobs.append((src, pair_T[kind][DH:P, g, 0:T - 1], 1.0))
    flip(core, jobs, ident)
    compress_stage(core, a, pair_T, cols[:, PE_AT:PE_AT + CMP_BLOCK], cols[:, B1_AT:B1_AT + 4], [kc, vc], ob_at)
    head_norms(core, [kc[0:CMP_N].unsqueeze(1)], scratch_at)

    with stage(nc, "scaled") as (block, scaled):
        @block.vector
        def _(dve):
            nc.vector.tensor_scalar(heads_cols[0:DH, 4:5], heads_cols[0:DH, 0:1], DH ** -0.5, None,
                                    ALU.mult).then_inc(scaled, 1)
    jobs = [([pr[:, t, Q_COL + h * DH:Q_COL + (h + 1) * DH] for t in range(TT)], qT[0:DH, h, :],
             heads_cols[0:DH, 4:5]) for h in range(Q_HEADS)]
    for b, lo in enumerate((KS_COL, KW_COL)):
        jobs += [([pr[:, t, lo + g * DH:lo + (g + 1) * DH] for t in range(TT)], kT[0:DH, b * KV + g, :],
                  heads_cols[0:DH, 2 + b:3 + b]) for g in range(KV)]
    jobs += [([kc[0:CMP_N, g, :]], kc_T[0:DH, g, :], heads_cols[0:DH, 1:2]) for g in range(KV)]
    flip(core, jobs, ident)

    attend(core, scratch_at, ident, KV, 2 * GROUP,
           q_of=lambda i, u: qT[0:DH, i * GROUP + u % GROUP, :],
           k_of=lambda i, u, n: kT[0:DH, i + u // GROUP * KV, 0:n],
           v_of=lambda i, u, kt, n: pr[0:n, kt, bass.ds((VS_COL, VW_COL)[u // GROUP] + i * DH, DH)],
           bias_of=lambda i, u, t, n: bias[:, i * GROUP + u % GROUP, T - P - P * t:T - P - P * t + n],
           out_of=lambda i, u, t: outs[1 + u // GROUP][:, t, bass.ds((i * GROUP + u % GROUP) * DH, DH)],
           width=DH, keys=lambda t: P * (t + 1))
    first_end = CMP_BLOCK - 1
    attend(core, scratch_at, ident, KV, GROUP,
           q_of=lambda i, u: qT[0:DH, i * GROUP + u, :],
           k_of=lambda i, u, n: kc_T[0:DH, i, 0:n],
           v_of=lambda i, u, kt, n: vc[0:n, i, :],
           bias_of=lambda i, u, t, n: bias[:, i * GROUP + u, T - P - P * t + first_end:
                                           T - P - P * t + first_end + CMP_STRIDE * (n - 1) + 1:CMP_STRIDE],
           out_of=lambda i, u, t: outs[0][:, t, bass.ds((i * GROUP + u) * DH, DH)],
           width=DH, keys=lambda t: (P * (t + 1) - CMP_BLOCK) // CMP_STRIDE + 1)
    branches_stage(core, outs, gates, row_valid, mixed)

    flip(core, [([mixed[:, t, k * P:(k + 1) * P] for t in range(TT)], mixed_T[:, k, :], 1.0) for k in range(KD)], ident)
    rows_product(core, mixed_T, KD, rows_of(a["w_out"][0]), add_to_residual(core))
    norm_stage(core, ones, cols[:, KD:2 * KD])
    hidden = core.work(0, KF, T)
    up = columns_of(a["w_up"][0])
    gated_hidden(core, lambda lo, n: up(lo + D_FF, n), up, hidden,
                 conv=(taps[:, 0:6 * KF], 3, taps[:, 6 * KF:8 * KF]))
    rows_product(core, hidden, KF, rows_of(a["w_down"][0]), add_to_residual(core))


LAYERS_2 = 2
A_HEADS, IDX_HEADS, IDX_DIM, B_HEADS = 8, 8, 32, 4
D_A = A_HEADS * DH
D_B = B_HEADS * 2 * DH
TOPK = min(256, T // 4)
QA_AT, KA_AT, VA_AT = 0, D_A, 2 * D_A
IQ_AT = 3 * D_A
IK_AT = IQ_AT + IDX_HEADS * IDX_DIM
IW_AT = IK_AT + IDX_DIM
QB_AT = IW_AT + IDX_HEADS
KB_AT = QB_AT + D_B
VB_AT = KB_AT + D_B
D_IN_2 = VB_AT + D_B
PICKED = -3e38


def rotate(engine, steps, x, cos, sin, tmp):
    heads, d = x.shape[1], x.shape[2]
    half = d // 2
    a, b = tmp[:, 0, 0:heads * d], tmp[:, 1, 0:heads * d]
    a = a.rearrange("p (h d) -> p h d", h=heads)
    b = b.rearrange("p (h d) -> p h d", h=heads)
    c = cos.unsqueeze(1).broadcast_to([P, heads, d])
    s = sin.unsqueeze(1).broadcast_to([P, heads, d])
    steps.step(engine.tensor_tensor(a, x, c, ALU.mult))
    steps.step(engine.tensor_tensor(b[:, :, 0:half], x[:, :, half:d], s[:, :, 0:half], ALU.mult))
    steps.link(engine.tensor_tensor(b[:, :, half:d], x[:, :, 0:half], s[:, :, half:d], ALU.mult))
    steps.link(engine.tensor_tensor(x, a, b, ALU.add))


def rope_stage(core, pr, tables, tmp_at):
    nc = core.nc
    cos64, sin64, cos32, sin32 = tables
    tmp_dve = core.work(tmp_at, 2, 2 * D_A)
    tmp_pool = core.work(tmp_at + 4 * D_A, 2, 2 * D_B)
    with stage(nc, "dve_steps", "pool_steps") as (block, dve_steps, pool_steps):
        @block.vector
        def _(dve):
            steps = Count(dve, dve_steps)
            for t in range(TT):
                x = pr[:, t, QA_AT:QA_AT + 2 * D_A].rearrange("p (h d) -> p h d", d=DH)
                rotate(nc.vector, steps, x, cos64[:, t, :], sin64[:, t, :], tmp_dve)
                x = pr[:, t, IQ_AT:IQ_AT + (IDX_HEADS + 1) * IDX_DIM].rearrange("p (h d) -> p h d", d=IDX_DIM)
                rotate(nc.vector, steps, x, cos32[:, t, :], sin32[:, t, :], tmp_dve)

        @block.gpsimd
        def _(pool):
            steps = Count(pool, pool_steps)
            for t in range(TT):
                x = pr[:, t, QB_AT:QB_AT + 2 * D_B].rearrange("p (h d) -> p h d", d=DH)
                rotate(nc.gpsimd, steps, x, cos64[:, t, :], sin64[:, t, :], tmp_pool)


def pick_stage(core, pr, iq, ik, picks, chunk_mask, scratch_at):
    nc = core.nc
    relu = core.work(scratch_at, 2, T)
    scores = core.work(scratch_at + 2 * T, 2, T)
    best = core.work(scratch_at + 4 * T, 2, 8)
    iw = core.work(scratch_at + 4 * T + 16, TT, IDX_HEADS)
    with stage(nc, "dotted", "relued", "weighed", "pick_steps") as (block, dotted, relued, weighed, pick_steps):
        @block.tensor
        def _(pe):
            for n in range((TT - 1) * IDX_HEADS):
                t, h, b = 1 + n // IDX_HEADS, n % IDX_HEADS, n % 4
                if n >= 4:
                    pe.wait_ge(relued, n - 3)
                nk = P * (t + 1)
                nc.tensor.matmul(core.bank(b)[:, 0:nk], iq[0:IDX_DIM, h, t * P:(t + 1) * P],
                                 ik[0:IDX_DIM, 0:nk], start=True, stop=True).then_inc(dotted, 1)

        @block.scalar
        def _(act):
            for n in range((TT - 1) * IDX_HEADS):
                t, b = 1 + n // IDX_HEADS, n % 4
                nk = P * (t + 1)
                act.wait_ge(dotted, n + 1)
                if n >= 2:
                    act.wait_ge(weighed, n - 1)
                nc.scalar.activation(relu[:, n % 2, 0:nk], core.bank(b)[:, 0:nk], ACT.Relu).then_inc(relued, 1)

        @block.vector
        def _(dve):
            steps = Count(dve, pick_steps)
            steps.step(nc.vector.tensor_scalar(iw, pr[:, :, IW_AT:IW_AT + IDX_HEADS],
                                               IDX_DIM ** -0.5 * IDX_HEADS ** -0.5, None, ALU.mult))
            steps.link(nc.vector.tensor_copy(picks[:, 0, 0:P], chunk_mask))
            for t in range(1, TT):
                nk = P * (t + 1)
                acc, work = scores[:, 0, 0:nk], scores[:, 1, 0:nk]
                for h in range(IDX_HEADS):
                    n = (t - 1) * IDX_HEADS + h
                    dve.wait_ge(relued, n + 1)
                    if h == 0:
                        nc.vector.tensor_scalar(acc, relu[:, n % 2, 0:nk], iw[:, t, h:h + 1], None,
                                                ALU.mult).then_inc(weighed, 1)
                    else:
                        nc.vector.scalar_tensor_tensor(out=acc, in0=relu[:, n % 2, 0:nk],
                                                       scalar=iw[:, t, h:h + 1], in1=acc,
                                                       op0=ALU.mult, op1=ALU.add).then_inc(weighed, 1)
                    dve.wait_ge(weighed, n + 1)
                last = acc[:, nk - P:nk]
                steps.link(nc.vector.tensor_tensor(last, last, chunk_mask, ALU.add))
                now, then = acc, work
                for r in range(TOPK // 8):
                    steps.link(nc.vector.max(best[:, r % 2, :], now))
                    steps.link(nc.vector.match_replace(then, best[:, r % 2, :], now, PICKED))
                    now, then = then, now
                steps.link(nc.vector.tensor_scalar(picks[:, t, 0:nk], now, PICKED / 2, NEG, ALU.is_gt, ALU.mult))


def difference_stage(core, ob, mixed, lam, lam_stats, scratch_at):
    nc = core.nc
    W = 2 * DH
    sq = core.work(scratch_at, TT, B_HEADS * W)
    ms = core.work(scratch_at + TT * B_HEADS * W, 3, TT * B_HEADS)
    lam_v, steps_words = lam, lam_stats
    with stage(nc, "steps_done", "mean_ready", "root_ready", "exponents", "exps") as (
            block, steps_done, mean_ready, root_ready, exponents, exps):
        @block.scalar
        def _(act):
            act.wait_ge(exponents, 2)
            nc.scalar.activation(steps_words[:, 2:4], steps_words[:, 0:2], ACT.Exp).then_inc(exps, 1)
            act.wait_ge(mean_ready, 1)
            nc.scalar.activation(ms[:, 1, :], ms[:, 0, :], ACT.Sqrt).then_inc(root_ready, 1)

        @block.vector
        def _(dve):
            steps = Count(dve, steps_done)
            for n in range(2):
                nc.vector.tensor_tensor_reduce(lam_v[:, 2 * n, :], lam_v[:, 2 * n, :], lam_v[:, 2 * n + 1, :],
                                               1.0, 0.0, ALU.mult, ALU.add,
                                               steps_words[:, n:n + 1]).then_inc(exponents, 1)
            dve.wait_ge(exps, 1)
            steps.link(nc.vector.tensor_tensor(steps_words[:, 4:5], steps_words[:, 3:4], steps_words[:, 2:3], ALU.subtract))
            steps.link(nc.vector.tensor_tensor(steps_words[:, 5:6], steps_words[:, 4:5], steps_words[:, 6:7], ALU.subtract))
            for t in range(TT):
                o = ob[:, t, :].rearrange("p (h c w) -> p h c w", h=B_HEADS, c=2)
                m = mixed[:, t, D_A:D_A + D_B].rearrange("p (h w) -> p h w", h=B_HEADS)
                steps.link(nc.vector.scalar_tensor_tensor(out=m, in0=o[:, :, 1, :], scalar=steps_words[:, 5:6],
                                                          in1=o[:, :, 0, :], op0=ALU.mult, op1=ALU.add))
                s = sq[:, t, :].rearrange("p (h w) -> p h w", h=B_HEADS)
                steps.link(nc.vector.tensor_tensor(s, m, m, ALU.mult))
                steps.link(nc.vector.tensor_reduce(ms[:, 0, t * B_HEADS:(t + 1) * B_HEADS], s, AX_X, ALU.add))
            nc.vector.tensor_scalar(ms[:, 0, :], ms[:, 0, :], 1.0 / W, EPS, ALU.mult, ALU.add).then_inc(mean_ready, 1)
            dve.wait_ge(root_ready, 1)
            steps.link(nc.vector.reciprocal(ms[:, 2, :], ms[:, 1, :]))
            for t in range(TT):
                m = mixed[:, t, D_A:D_A + D_B].rearrange("p (h w) -> p h w", h=B_HEADS)
                r = ms[:, 2, t * B_HEADS:(t + 1) * B_HEADS].unsqueeze(2).broadcast_to([P, B_HEADS, W])
                steps.step(nc.vector.tensor_tensor(m, m, r, ALU.mult))


def swiglu(core, gate_w, up_w, down_w):
    hidden = core.work(0, KF, T)
    gated_hidden(core, gate_w, up_w, hidden)
    rows_product(core, hidden, KF, down_w, add_to_residual(core))


def columns_of(w):
    w = w.rearrange("(k p) n -> p k n", p=P)
    return lambda lo, n: w[:, :, bass.ds(lo, n)]


def rows_of(w):
    w = w.rearrange("(k p) n -> p k n", p=P)
    return lambda k: w[:, bass.ds(k, 2), :]


def second_block(core, a, tables, chunk_mask, ident, ones):
    nc = core.nc
    pr = core.work(0, TT, D_IN_2)
    at = TT * D_IN_2
    qT, kT = core.work(at, A_HEADS, T), core.work(at + 8 * T, A_HEADS, T)
    picks = core.work(at + 16 * T, TT, T)
    scratch_at = at + 20 * T
    ob_at = scratch_at + ATTEND_WORDS
    ob = core.work(ob_at, TT, B_HEADS * 4 * DH)
    mixed = core.cut(H_AT, TT, D)
    mixed_T = core.work(at, KD, T)
    cols = core.const(2 * KD + 1)
    lam = core.const(4, DH)
    lam_words = core.const(8)
    sub_gain = core.const(1)
    one_minus = core.const(1)

    with nc.Fori(0, LAYERS_2) as layer:
        row = lambda v, n: v[layer].rearrange("(k p) -> k p", k=n)
        load_columns(core, 0, [row(a["g_mix_2"], KD), row(a["g_ffn_2"], KD), row(a["g_subln_2"], 1)], cols, ident)
        everywhere = lambda v: v.partition_broadcast(P)
        load_stage(nc, [(lam[:, n, :], everywhere(a[name][layer])) for n, name in
                        enumerate(["lam_q1_2", "lam_k1_2", "lam_q2_2", "lam_k2_2"])]
                   + [(lam_words[:, 6:8], everywhere(a["lam_init"][layer]))])
        norm_stage(core, ones, cols[:, 0:KD])
        project_tokens(core, columns_of(a["w_in_2"][layer]), D_IN_2, pr)
        rope_stage(core, pr, tables, at)

        def turned(lo, n, width, dst, scale=1.0):
            return [([pr[:, t, lo + width * h:lo + width * (h + 1)] for t in range(TT)],
                     dst[0:width, h, :], scale) for h in range(n)]
        flip(core, turned(IQ_AT, IDX_HEADS, IDX_DIM, qT) + turned(IK_AT, 1, IDX_DIM, kT), ident)
        pick_stage(core, pr, qT, kT[:, 0, :], picks, chunk_mask, scratch_at)
        flip(core, turned(QA_AT, A_HEADS, DH, qT, DH ** -0.5) + turned(KA_AT, A_HEADS, DH, kT), ident)
        U = 4
        attend(core, scratch_at, ident, A_HEADS // U, U,
               q_of=lambda i, u: qT[0:DH, i * U + u, :],
               k_of=lambda i, u, n: kT[0:DH, i * U + u, 0:n],
               v_of=lambda i, u, kt, n: pr[0:n, kt, bass.ds(VA_AT + (i * U + u) * DH, DH)],
               bias_of=lambda i, u, t, n: picks[:, t, 0:n],
               out_of=lambda i, u, t: mixed[:, t, bass.ds((i * U + u) * DH, DH)],
               width=DH, keys=lambda t: P * (t + 1))

        flip(core, turned(QB_AT, 2 * B_HEADS, DH, qT, DH ** -0.5) + turned(KB_AT, 2 * B_HEADS, DH, kT), ident)
        load_bias(core, picks, chunk_mask)
        attend(core, scratch_at, ident, 2 * B_HEADS // U, U,
               q_of=lambda i, u: qT[0:DH, i * U + u, :],
               k_of=lambda i, u, n: kT[0:DH, i * U + u, 0:n],
               v_of=lambda i, u, kt, n: pr[0:n, kt, bass.ds(VB_AT + (i * (U // 2) + u // 2) * 2 * DH, 2 * DH)],
               bias_of=lambda i, u, t, n: picks[:, t, 0:n],
               out_of=lambda i, u, t: ob[:, t, bass.ds((i * U + u) * 2 * DH, 2 * DH)],
               width=2 * DH, keys=lambda t: P * (t + 1))
        difference_stage(core, ob, mixed, lam, lam_words, at)
        with stage(nc, "gain_ready") as (block, gain_ready):
            @block.vector
            def _(dve):
                nc.vector.tensor_tensor(sub_gain, cols[:, 2 * KD:2 * KD + 1], lam_words[:, 7:8],
                                        ALU.mult).then_inc(gain_ready, 1)
        flip(core, [([mixed[:, t, k * P:(k + 1) * P] for t in range(TT)], mixed_T[:, k, :],
                     1.0 if k < D_A // P else sub_gain) for k in range(KD)], ident)
        rows_product(core, mixed_T, KD, rows_of(a["w_out_2"][layer]), add_to_residual(core))
        norm_stage(core, ones, cols[:, KD:2 * KD])
        swiglu(core, columns_of(a["w_gate_2"][layer]), columns_of(a["w_up_2"][layer]),
               rows_of(a["w_down_2"][layer]))
    load_columns(core, 0, [a["g_final_2"].rearrange("(k p) -> k p", p=P)], cols[:, 0:KD], ident)
    norm_stage(core, ones, cols[:, 0:KD], out=core.x)


def load_bias(core, picks, chunk_mask):
    nc = core.nc
    with stage(nc, "cleared", "masked") as (block, cleared, masked):
        @block.gpsimd
        def _(pool):
            for t in range(1, TT):
                nc.gpsimd.memset(picks[:, t, 0:t * P], 0.0).then_inc(cleared, 1)

        @block.vector
        def _(dve):
            for t in range(TT):
                nc.vector.tensor_copy(picks[:, t, t * P:(t + 1) * P], chunk_mask).then_inc(masked, 1)


S_HEADS, S_GROUPS, S_STATE = 16, 2, 128
S_INNER = S_HEADS * DH
CONV_K = 4
G_HEADS, G_DIM = 8, 128
Z_COL = 0
XBC_COL = Z_COL + S_INNER
XBC = S_INNER + 2 * S_GROUPS * S_STATE
DT_COL = XBC_COL + XBC
QKV_COL = DT_COL + S_HEADS
QKV = 3 * G_HEADS * G_DIM
GZ_COL = QKV_COL + QKV
AB_COL = GZ_COL + G_HEADS * G_DIM
GATE_S_COL = AB_COL + 2 * G_HEADS
GATE_G_COL = GATE_S_COL + D
ROWS = 40
G_ROW = 32
SPANS = [(sum(T - P * m for m in range(j)), T - P * j) for j in range(TT)]
SPAN_WORDS = sum(w for _, w in SPANS)
LOG_TERMS = 8


def project_features(core, weight, tiles, dst, func, conv=None):
    nc, h = core.nc, core.h
    bodies, odd = pairs(tiles // 4)
    with stage(nc, "weights0", "weights1", "products0", "products1", "based", "convolved", "conv_steps",
               "done0", "done1", from_one=("products0", "products1", "done0", "done1")) as (block, *sems):
        weights, products, based, convolved, conv_steps, done = (
            sems[0:2], sems[2:4], sems[4], sems[5], sems[6], sems[7:9])

        def each(engine, unit):
            with engine.Fori(0, bodies) as i:
                for j in range(2):
                    unit(i, j)
            if odd:
                unit(bodies, 0)

        def tile(i, j, m):
            return (2 * i + j) * 4 + m

        @block.sync
        def _(sp):
            def load(i, j):
                sp.wait_ge(products[j], 4 * i + 1)
                sp.dma_start(core.slot(j, KD, BANK), weight((2 * i + j) * BANK, BANK)).then_inc(weights[j], 16)
            each(sp, load)

        @block.tensor
        def _(pe):
            def multiply(i, j):
                pe.wait_ge(weights[j], 16 * i + 16)
                pe.wait_ge(done[j], 4 * i + 1)
                w = core.slot(j, KD, BANK)
                for m in range(4):
                    for k in range(KD):
                        mm = nc.tensor.matmul(core.bank(4 * j + m), w[:, k, m * P:(m + 1) * P], h[:, k, :],
                                              start=(k == 0), stop=(k == KD - 1))
                    mm.then_inc(products[j], 1)
            each(pe, multiply)

        @block.scalar
        def _(act):
            def work(i, j):
                for m in range(4):
                    hold(act, products[j], 4 * i + m + 2)
                    to = dst[:, tile(i, j, m), :]
                    if conv is None:
                        nc.scalar.activation(to, core.bank(4 * j + m), func).then_inc(done[j], 1)
                    else:
                        nc.scalar.activation(to, core.bank(4 * j + m), ACT.Identity,
                                             scale=conv[0][:, bass.ds((CONV_K - 1) * tiles + tile(i, j, m), 1)],
                                             bias=conv[1][:, bass.ds(tile(i, j, m), 1)]).then_inc(based, 1)
                for m in range(4 if conv else 0):
                    hold(act, convolved, tile(i, j, m) + 1)
                    to = dst[:, tile(i, j, m), :]
                    nc.scalar.activation(to, to, func).then_inc(done[j], 1)
            each(act, work)

        @block.vector
        def _(dve):
            def work(i, j):
                for m in range(4):
                    n = tile(i, j, m)
                    dve.wait_ge(based, n + 1)
                    for back in range(1, CONV_K):
                        ins = nc.vector.scalar_tensor_tensor(
                            out=dst[:, n, back:T], in0=core.bank(4 * j + m)[:, 0:T - back],
                            scalar=conv[0][:, bass.ds((CONV_K - 1 - back) * tiles + n, 1)],
                            in1=dst[:, n, back:T], op0=ALU.mult, op1=ALU.add)
                        if back < CONV_K - 1:
                            ins.then_inc(conv_steps, 1)
                            dve.wait_ge(conv_steps, (CONV_K - 2) * n + back)
                    ins.then_inc(convolved, 1)
            if conv is not None:
                each(dve, work)


def small_projections(core, w, small):
    nc, h = core.nc, core.h
    n = S_HEADS
    with stage(nc, "weights_in", "projected", "stored") as (block, weights_in, projected, stored):
        @block.sync
        def _(sp):
            for c, col in enumerate((DT_COL, AB_COL)):
                sp.dma_start(core.slot(0, KD, 2 * n)[:, :, c * n:(c + 1) * n], w[:, :, col:col + n]
                             ).then_inc(weights_in, 16)

        @block.tensor
        def _(pe):
            pe.wait_ge(weights_in, 32)
            for t in range(TT):
                for k in range(KD):
                    mm = nc.tensor.matmul(core.bank(t)[:, 0:2 * n], h[:, k, t * P:(t + 1) * P],
                                          core.slot(0, KD, 2 * n)[:, k, :], start=(k == 0), stop=(k == KD - 1))
                mm.then_inc(projected, 1)

        @block.vector
        def _(dve):
            for t in range(TT):
                dve.wait_ge(projected, t + 1)
                nc.vector.tensor_copy(small[:, t, :], core.bank(t)[:, 0:2 * n]).then_inc(stored, 1)


def decay_stage(core, raw, beta_raw, bias_col, log_col, steps_row, sums, delta_rows, at):
    nc = core.nc
    neg, e, z, z2, series, one = (core.work(at + T * n, T)[0:ROWS] for n in range(6))
    with stage(nc, "decay_steps", "ready", "exp_done", "coefficient", "beta_done") as (
            block, decay_steps, ready, exp_done, coefficient, beta_done):
        @block.scalar
        def _(act):
            nc.scalar.activation(log_col, log_col, ACT.Exp).then_inc(coefficient, 1)
            act.wait_ge(ready, 1)
            nc.scalar.activation(e, neg, ACT.Exp).then_inc(exp_done, 1)
            nc.scalar.activation(delta_rows[:, 1, :], beta_raw, ACT.Sigmoid).then_inc(beta_done, 1)

        @block.vector
        def _(dve):
            v = nc.vector
            s = Count(dve, decay_steps)
            s.step(v.memset(one, 1.0))
            s.link(v.tensor_scalar(raw, raw, bias_col, None, ALU.add))
            s.link(v.tensor_scalar(neg, raw, -1.0, None, ALU.mult))
            s.link(v.tensor_tensor(neg, neg, raw, ALU.min))
            v.tensor_scalar(raw, raw, 0.0, None, ALU.max).then_inc(ready, 1)
            dve.wait_ge(exp_done, 1)
            dve.wait_ge(ready, 1)
            s.link(v.tensor_scalar(z2, e, 2.0, None, ALU.add))
            s.link(v.reciprocal(neg, z2))
            s.link(v.tensor_tensor(z, e, neg, ALU.mult))
            s.link(v.tensor_tensor(z2, z, z, ALU.mult))
            s.link(v.tensor_scalar(series, z2, 1.0 / (2 * LOG_TERMS + 1), None, ALU.mult))
            for k in range(LOG_TERMS - 1, 0, -1):
                s.link(v.scalar_tensor_tensor(out=series, in0=series, scalar=1.0 / (2 * k + 1), in1=z2,
                                              op0=ALU.add, op1=ALU.mult))
            s.link(v.scalar_tensor_tensor(out=series, in0=series, scalar=1.0, in1=z, op0=ALU.add, op1=ALU.mult))
            s.link(v.scalar_tensor_tensor(out=steps_row, in0=series, scalar=2.0, in1=raw, op0=ALU.mult, op1=ALU.add))
            dve.wait_ge(coefficient, 1)
            s.link(v.tensor_scalar(neg, steps_row, log_col, -1.0, ALU.mult, ALU.mult))
            for j, (lo, w) in enumerate(SPANS):
                s.step(v.tensor_tensor_scan(sums[:, lo:lo + w], one[:, 0:w], neg[:, T - w:T], 0.0,
                                            ALU.mult, ALU.add))
            s.settle()
            for j, (lo, w) in enumerate(SPANS):
                s.step(v.tensor_copy(delta_rows[:, 0, j * P:(j + 1) * P], sums[G_ROW:G_ROW + G_HEADS, lo:lo + P]))


def ssd_stage(core, ones, pick, b_T, c_T, xs, xdt, sums, sums_tok, d_skip, keep, y, at):
    nc = core.nc
    gram = core.work(at, S_GROUPS, SPAN_WORDS)
    decay = core.work(at + 2 * SPAN_WORDS, 2, SPAN_WORDS)
    one_row = core.work(at + 4 * SPAN_WORDS, 2, SPAN_WORDS)[0:S_HEADS]
    per_group = S_HEADS // S_GROUPS
    with stage(nc, "gram_ready", "gram_stored", "gram_masked") as (block, gram_ready, gram_stored, gram_masked):
        @block.tensor
        def _(pe):
            for g in range(S_GROUPS):
                for j, (lo, w) in enumerate(SPANS):
                    nc.tensor.matmul(core.bank(g * TT + j)[:, 0:w], b_T[:, g, j * P:(j + 1) * P],
                                     c_T[:, g, j * P:T], start=True, stop=True).then_inc(gram_ready, 1)

        @block.vector
        def _(dve):
            for g in range(S_GROUPS):
                for j, (lo, w) in enumerate(SPANS):
                    dve.wait_ge(gram_ready, g * TT + j + 1)
                    if w > P:
                        nc.vector.tensor_copy(gram[:, g, lo + P:lo + w], core.bank(g * TT + j)[:, P:w]
                                              ).then_inc(gram_stored, 1)
                    nc.vector.tensor_tensor(gram[:, g, lo:lo + P], core.bank(g * TT + j)[:, 0:P], keep,
                                            ALU.mult).then_inc(gram_masked, 1)

    with stage(nc, "row_ready", "spread", "spread_read", "decayed", "weighted", "output", "output_stored",
               from_one=("spread", "spread_read", "output", "output_stored")) as (
            block, row_ready, spread, spread_read, decayed, weighted, output, output_stored):
        bodies = S_HEADS // 2

        @block.gpsimd
        def _(pool):
            with pool.Fori(0, bodies) as i:
                for u in range(2):
                    hold(pool, spread, TT * (2 * i + u) + 1)
                    own = pick[0:S_HEADS, bass.ds(2 * i + u, 1)].broadcast_to([S_HEADS, SPAN_WORDS])
                    nc.gpsimd.tensor_tensor(one_row[:, u, :], sums[0:S_HEADS, :], own, ALU.mult).then_inc(row_ready, 1)

        @block.tensor
        def _(pe):
            with pe.Fori(0, bodies) as i:
                for u in range(2):
                    h = 2 * i + u
                    pe.wait_ge(row_ready, h + 1)
                    pe.wait_ge(spread_read, TT * h + 1)
                    for j, (lo, w) in enumerate(SPANS):
                        nc.tensor.matmul(core.bank(j)[:, 0:w], ones[0:S_HEADS, :], one_row[:, u, lo:lo + w],
                                         start=True, stop=True).then_inc(spread, 1)
                for u in range(2):
                    h = 2 * i + u
                    pe.wait_ge(weighted, h + 1)
                    pe.wait_ge(output_stored, 2 * i + 1)
                    for t in range(TT):
                        for j in range(t + 1):
                            at_j = SPANS[j][0] + (t - j) * P
                            mm = nc.tensor.matmul(core.bank(4 + u)[:, t * DH:(t + 1) * DH],
                                                  decay[:, u, at_j:at_j + P], xdt[:, j, bass.ds(h * DH, DH)],
                                                  start=(j == 0), stop=(j == t))
                    mm.then_inc(output, 1)

        @block.scalar
        def _(act):
            with act.Fori(0, bodies) as i:
                for u in range(2):
                    h = 2 * i + u
                    act.wait_ge(output, 2 * i + 1)
                    for j, (lo, w) in enumerate(SPANS):
                        hold(act, spread, TT * h + j + 2)
                        nc.scalar.activation(decay[:, u, lo:lo + w], core.bank(j)[:, 0:w], ACT.Relu, scale=-1.0,
                                             bias=sums_tok[:, j, bass.ds(h, 1)]).then_inc(spread_read, 1)
                    act.wait_ge(spread_read, TT * h + TT + 1)
                    nc.scalar.activation(decay[:, u, :], decay[:, u, :], ACT.Exp, scale=-1.0).then_inc(decayed, 1)

        @block.vector
        def _(dve):
            with dve.Fori(0, bodies) as i:
                for u in range(2):
                    h = 2 * i + u
                    dve.wait_ge(decayed, h + 1)
                    nc.vector.tensor_tensor(decay[:, u, :], decay[:, u, :], gram[:, i // (per_group // 2), :],
                                            ALU.mult).then_inc(weighted, 1)
                for u in range(2):
                    h = 2 * i + u
                    dve.wait_ge(output, h + 2)
                    nc.vector.scalar_tensor_tensor(
                        out=y[:, :, bass.ds(h * DH, DH)], in0=xs[:, :, bass.ds(h * DH, DH)],
                        scalar=d_skip[:, bass.ds(h, 1)],
                        in1=core.bank(4 + u)[:, 0:TT * DH].rearrange("p (t d) -> p t d", t=TT),
                        op0=ALU.mult, op1=ALU.add).then_inc(output_stored, 1)


def multiply_stage(core, jobs):
    nc = core.nc
    with stage(nc, "multiplied") as (block, multiplied):
        @block.vector
        def _(dve):
            for out, a, b in jobs:
                nc.vector.tensor_tensor(out, a, b, ALU.mult).then_inc(multiplied, 1)


def unit_stage(core, ones, x, n, queries, at):
    nc = core.nc
    sq = core.cut(RING_AT, 2, T)
    root = core.cut(RING_AT + 2 * T, 4, T)
    with stage(nc, "squared", "summed", "mean_ready", "root_ready", "inverted", "scaled") as (
            block, squared, summed, mean_ready, root_ready, inverted, scaled):
        @block.gpsimd
        def _(pool):
            for m in range(n):
                if m >= 2:
                    pool.wait_ge(summed, m - 1)
                nc.gpsimd.tensor_tensor(sq[:, m % 2, :], x[:, m, :], x[:, m, :], ALU.mult).then_inc(squared, 1)

        @block.tensor
        def _(pe):
            for m in range(n):
                pe.wait_ge(squared, m + 1)
                if m >= 4:
                    pe.wait_ge(mean_ready, m - 3)
                nc.tensor.matmul(core.bank(m % 4), ones, sq[:, m % 2, :], start=True, stop=True).then_inc(summed, 1)

        @block.scalar
        def _(act):
            for m in range(n):
                r = root[:, m % 4, :]
                act.wait_ge(mean_ready, m + 1)
                nc.scalar.activation(r, r, ACT.Sqrt).then_inc(root_ready, 1)

        @block.vector
        def _(dve):
            def scale(m):
                r = root[:, m % 4, :]
                dve.wait_ge(root_ready, m + 1)
                nc.vector.reciprocal(r, r).then_inc(inverted, 1)
                dve.wait_ge(inverted, m + 1)
                factor = G_DIM ** -0.5 if m < queries else 1.0
                nc.vector.scalar_tensor_tensor(out=x[:, m, :], in0=x[:, m, :], scalar=factor, in1=r,
                                               op0=ALU.mult, op1=ALU.mult).then_inc(scaled, 1)
            for m in range(n):
                dve.wait_ge(summed, m + 1)
                if m >= 4:
                    dve.wait_ge(scaled, m - 3)
                nc.vector.tensor_scalar(root[:, m % 4, :], core.bank(m % 4), EPS, None, ALU.add).then_inc(mean_ready, 1)
                if m >= 2:
                    scale(m - 2)
            scale(n - 2)
            scale(n - 1)


def delta_prepare(core, ones, pick, q_T, k_T, delta_rows, sums_tok, keep, couple_T, attn_T, last_sum, last_decay):
    nc = core.nc
    one_row = core.cut(RING_AT, 2, 2 * T)[0:G_HEADS]
    kb = core.cut(RING_AT + 4 * T, 2, T)
    dec = core.cut(RING_AT + 6 * T, 2, T)
    eg = core.cut(RING_AT + 8 * T, 2, T)
    k_static = core.cut(RING_AT + 10 * T, 2, T)
    with stage(nc, "row_ready", "spread", "sums_read", "exp_ready", "keys_scaled", "products", "differences", "decay_ready",
               "decay_kept", "used", "lasts", from_one=("spread", "used", "products")) as (
            block, row_ready, spread, sums_read, exp_ready, keys_scaled, products, differences, decay_ready, decay_kept, used, lasts):
        bodies = G_HEADS // 2

        @block.gpsimd
        def _(pool):
            with pool.Fori(0, bodies) as i:
                for u in range(2):
                    h = 2 * i + u
                    hold(pool, spread, 4 * i + 1)
                    own = pick[0:G_HEADS, bass.ds(h, 1)].broadcast_to([G_HEADS, 2 * T])
                    nc.gpsimd.tensor_tensor(one_row[:, u, :], delta_rows.rearrange("p a b -> p (a b)"), own,
                                            ALU.mult).then_inc(row_ready, 1)
                for u in range(2):
                    h = 2 * i + u
                    pool.wait_ge(decay_ready, h + 1)
                    d = dec[:, u, :].rearrange("p (t i) -> p t i", t=TT)
                    nc.gpsimd.tensor_tensor(d, d, keep.unsqueeze(1).broadcast_to([P, TT, P]), ALU.mult).then_inc(decay_kept, 1)

        @block.tensor
        def _(pe):
            with pe.Fori(0, bodies) as i:
                for u in range(2):
                    h = 2 * i + u
                    pe.wait_ge(row_ready, h + 1)
                    pe.wait_ge(used, 6 * i + 1)
                    for c in range(2):
                        nc.tensor.matmul(core.bank(4 * u + c), ones[0:G_HEADS, :], one_row[:, u, c * T:(c + 1) * T],
                                         start=True, stop=True).then_inc(spread, 1)
                for u in range(2):
                    h = 2 * i + u
                    pe.wait_ge(keys_scaled, 2 * h + 2)
                    for c in range(2):
                        for t in range(TT):
                            s = slice(t * P, (t + 1) * P)
                            mm = nc.tensor.matmul(core.bank(4 * u + 2 + c)[:, s], k_static[:, u, s],
                                                  q_T[:, h, s] if c else kb[:, u, s], start=True, stop=True)
                        mm.then_inc(products, 1)

        @block.scalar
        def _(act):
            with act.Fori(0, bodies) as i:
                for u in range(2):
                    h = 2 * i + u
                    act.wait_ge(spread, 4 * i + 2 * u + 2)
                    hold(act, used, 6 * i + 1)
                    for t in range(TT):
                        nc.scalar.activation(dec[:, u, t * P:(t + 1) * P], core.bank(4 * u)[:, t * P:(t + 1) * P],
                                             ACT.Relu, scale=-1.0, bias=sums_tok[:, t, bass.ds(G_ROW + h, 1)]
                                             ).then_inc(differences, 1)
                    act.wait_ge(differences, TT * h + TT)
                    nc.scalar.activation(dec[:, u, :], dec[:, u, :], ACT.Exp, scale=-1.0).then_inc(decay_ready, 1)
                    nc.scalar.copy(last_sum[:, h, :], core.bank(4 * u)[:, P - 1:T:P]).then_inc(exp_ready, 1)
                    nc.scalar.activation(eg[:, u, :], core.bank(4 * u), ACT.Exp).then_inc(exp_ready, 1)

        @block.vector
        def _(dve):
            with dve.Fori(0, bodies) as i:
                for u in range(2):
                    h = 2 * i + u
                    dve.wait_ge(spread, 4 * i + 2 * u + 3)
                    dve.wait_ge(products, 4 * i + 1)
                    nc.vector.tensor_tensor(kb[:, u, :], k_T[:, h, :], core.bank(4 * u + 1), ALU.mult).then_inc(keys_scaled, 1)
                    nc.vector.tensor_copy(k_static[:, u, :], k_T[:, h, :]).then_inc(keys_scaled, 1)
                for u in range(2):
                    h = 2 * i + u
                    dve.wait_ge(decay_kept, h + 1)
                    dve.wait_ge(products, 2 * h + 2)
                    nc.vector.tensor_tensor(couple_T[:, h, :], dec[:, u, :], core.bank(4 * u + 2), ALU.mult).then_inc(used, 1)
                    dve.wait_ge(products, 2 * h + 3)
                    nc.vector.tensor_tensor(attn_T[:, h, :], dec[:, u, :], core.bank(4 * u + 3), ALU.mult).then_inc(used, 1)
                    dve.wait_ge(exp_ready, 2 * h + 2)
                    nc.vector.tensor_copy(last_decay[:, h, :], eg[:, u, P - 1:T:P]).then_inc(lasts, 1)
                    nc.vector.tensor_tensor(q_T[:, h, :], q_T[:, h, :], eg[:, u, :], ALU.mult).then_inc(used, 1)


def delta_solve(core, ident, level_masks, couple_T, inverse_T):
    nc = core.nc
    levels = level_masks.shape[1]
    inv = core.cut(RING_AT, 2, T)
    inv_T = core.cut(RING_AT + 2 * T, 2, T)
    join = core.cut(RING_AT + 4 * T, 4, T)
    part = core.cut(RING_AT + 8 * T, 2, T)
    with stage(nc, "begun", "joined", "part_ready", "part_stored", "updates", "updated", from_one=("part_ready",)) as (
            block, begun, joined, part_ready, part_stored, updates, updated):
        bodies = G_HEADS // 2

        @block.gpsimd
        def _(pool):
            with pool.Fori(0, bodies) as i:
                for n in range(2 * levels):
                    l, u = n // 2, n % 2
                    hold(pool, part_ready, 2 * levels * i + max(n - 3, 0) + 1)
                    h = 2 * i + u
                    e = join[:, 2 * u + l % 2, :].rearrange("p (t i) -> p t i", t=TT)
                    nc.gpsimd.tensor_tensor(e, couple_T[:, h, :].rearrange("p (t i) -> p t i", t=TT),
                                            level_masks[:, l, :].unsqueeze(1).broadcast_to([P, TT, P]),
                                            ALU.mult).then_inc(joined, 1)

        @block.tensor
        def _(pe):
            def product(bank, left, right):
                for t in range(TT):
                    s = slice(t * P, (t + 1) * P)
                    mm = nc.tensor.matmul(core.bank(bank)[:, s], left[:, s], right[:, s], start=True, stop=True)
                return mm
            with pe.Fori(0, bodies) as i:
                base = 2 * levels * i
                for l in range(levels):
                    for u in range(2):
                        n = 2 * l + u
                        pe.wait_ge(joined, base + n + 1)
                        if l == 0:
                            pe.wait_ge(begun, 4 * i + 2 * u + 2)
                        else:
                            pe.wait_ge(updated, 2 * (base + n - 1))
                        product(4 * u, join[:, 2 * u + l % 2, :], inv[:, u, :]).then_inc(part_ready, 1)
                    for u in range(2):
                        n = 2 * l + u
                        pe.wait_ge(part_stored, base + n + 1)
                        product(4 * u + 1, inv_T[:, u, :], part[:, u, :]).then_inc(updates, 1)
                        product(4 * u + 2, part[:, u, :], inv_T[:, u, :]).then_inc(updates, 1)

        @block.scalar
        def _(act):
            with act.Fori(0, bodies) as i:
                base = 2 * levels * i
                for n in range(2 * levels):
                    u = n % 2
                    act.wait_ge(part_ready, base + n + 2)
                    nc.scalar.copy(part[:, u, :], core.bank(4 * u)).then_inc(part_stored, 1)

        @block.vector
        def _(dve):
            eye = ident.unsqueeze(1).broadcast_to([P, TT, P])
            with dve.Fori(0, bodies) as i:
                base = 2 * levels * i
                for u in range(2):
                    for m in (inv, inv_T):
                        nc.vector.tensor_copy(m[:, u, :].rearrange("p (t i) -> p t i", t=TT), eye).then_inc(begun, 1)
                for l in range(levels):
                    for u in range(2):
                        n = 2 * l + u
                        dve.wait_ge(updates, 2 * (base + n) + 2)
                        if l == 0:
                            dve.wait_ge(begun, 4 * i + 4)
                        else:
                            dve.wait_ge(updated, 2 * (base + n - 1))
                        nc.vector.tensor_tensor(inv[:, u, :], inv[:, u, :], core.bank(4 * u + 1),
                                                ALU.subtract).then_inc(updated, 1)
                        to = inverse_T[:, 2 * i + u, :] if l == levels - 1 else inv_T[:, u, :]
                        nc.vector.tensor_tensor(to, inv_T[:, u, :], core.bank(4 * u + 2), ALU.subtract).then_inc(updated, 1)
                dve.wait_ge(updated, 2 * (base + 2 * levels))


def delta_inputs(core, k_tok, v_tok, beta_tok, sums_tok, last_sum, inverse_T, minus_w_T, tail_k):
    nc = core.nc
    k_in = core.cut(RING_AT, TT, D)
    factor = core.cut(RING_AT + SLOT, 3, TT * G_HEADS)
    heads = lambda x: x.rearrange("p t (h d) -> p t h d", h=G_HEADS)
    wide = lambda f: f.rearrange("p (t h) -> p t h", t=TT).unsqueeze(3).broadcast_to([P, TT, G_HEADS, G_DIM])
    with stage(nc, "exp_sum", "rest", "exp_rest", "input_ready", "factor_ready", "scaled", "w_ready", "w_stored") as (
            block, exp_sum, rest, exp_rest, input_ready, factor_ready, scaled, w_ready, w_stored):
        f = lambda n: factor[:, n, :].rearrange("p (t h) -> p t h", t=TT)
        gsum = sums_tok[:, :, G_ROW:G_ROW + G_HEADS]

        @block.scalar
        def _(act):
            nc.scalar.activation(f(0), gsum, ACT.Exp).then_inc(exp_sum, 1)
            act.wait_ge(rest, 1)
            nc.scalar.activation(f(1), f(1), ACT.Exp).then_inc(exp_rest, 1)
            for h in range(G_HEADS):
                act.wait_ge(w_ready, h + 1)
                nc.scalar.activation(minus_w_T[:, h, :], core.bank(h), ACT.Copy, scale=-1.0).then_inc(w_stored, 1)

        @block.vector
        def _(dve):
            nc.vector.tensor_tensor(f(1), last_sum.rearrange("p h t -> p t h"), gsum, ALU.subtract).then_inc(rest, 1)
            dve.wait_ge(exp_sum, 1)
            nc.vector.tensor_tensor(f(2), f(0), beta_tok, ALU.mult).then_inc(factor_ready, 1)
            dve.wait_ge(factor_ready, 1)
            nc.vector.tensor_tensor(heads(k_in), heads(k_tok), wide(factor[:, 2, :]), ALU.mult).then_inc(input_ready, 1)
            nc.vector.tensor_tensor(heads(v_tok), heads(v_tok),
                                    beta_tok.unsqueeze(3).broadcast_to([P, TT, G_HEADS, G_DIM]),
                                    ALU.mult).then_inc(scaled, 1)

        @block.gpsimd
        def _(pool):
            pool.wait_ge(exp_rest, 1)
            nc.gpsimd.tensor_tensor(heads(tail_k), heads(k_tok), wide(factor[:, 1, :]), ALU.mult).then_inc(scaled, 1)

        @block.tensor
        def _(pe):
            pe.wait_ge(input_ready, 1)
            for h in range(G_HEADS):
                for t in range(TT):
                    mm = nc.tensor.matmul(core.bank(h)[:, t * P:(t + 1) * P], k_in[:, t, h * G_DIM:(h + 1) * G_DIM],
                                          inverse_T[:, h, t * P:(t + 1) * P], start=True, stop=True)
                mm.then_inc(w_ready, 1)


def delta_scan(core, q_T, v_tok, tail_k, inverse_T, minus_w_T, attn_T, last_decay, out):
    nc = core.nc
    state = core.cut(RING_AT, G_HEADS, G_DIM)
    fresh = core.cut(RING_AT + G_HEADS * G_DIM, 2, G_DIM)
    with stage(nc, "cleared", "fresh_ready", "fresh_stored", "out_ready", "step_ready", "out_stored", "state_ready") as (
            block, cleared, fresh_ready, fresh_stored, out_ready, step_ready, out_stored, state_ready):
        order = [(t, h) for t in range(TT) for h in range(G_HEADS)]

        @block.gpsimd
        def _(pool):
            nc.gpsimd.memset(state, 0.0).then_inc(cleared, 1)

        @block.tensor
        def _(pe):
            pe.wait_ge(cleared, 1)

            def finish(n):
                t, h = order[n]
                s = slice(t * P, (t + 1) * P)
                pe.wait_ge(fresh_stored, n + 1)
                if n >= 2:
                    pe.wait_ge(out_stored, n - 1)
                    pe.wait_ge(state_ready, n - 1)
                b = core.bank(2 + n % 2)[:, 0:G_DIM]
                nc.tensor.matmul(b, q_T[:, h, s], state[:, h, :], start=True, stop=False)
                nc.tensor.matmul(b, attn_T[:, h, s], fresh[:, n % 2, :], start=False, stop=True).then_inc(out_ready, 1)
                nc.tensor.matmul(core.bank(4 + n % 2)[:, 0:G_DIM], tail_k[:, t, h * G_DIM:(h + 1) * G_DIM],
                                 fresh[:, n % 2, :], start=True, stop=True).then_inc(step_ready, 1)

            for n, (t, h) in enumerate(order):
                s = slice(t * P, (t + 1) * P)
                if n >= 2:
                    pe.wait_ge(fresh_stored, n - 1)
                if n >= G_HEADS:
                    pe.wait_ge(state_ready, n - G_HEADS + 1)
                b = core.bank(n % 2)[:, 0:G_DIM]
                nc.tensor.matmul(b, inverse_T[:, h, s], v_tok[:, t, h * G_DIM:(h + 1) * G_DIM], start=True, stop=False)
                nc.tensor.matmul(b, minus_w_T[:, h, s], state[:, h, :], start=False, stop=True).then_inc(fresh_ready, 1)
                if n:
                    finish(n - 1)
            finish(len(order) - 1)

        @block.scalar
        def _(act):
            for n in range(len(order)):
                act.wait_ge(fresh_ready, n + 1)
                if n >= 2:
                    act.wait_ge(step_ready, n - 1)
                nc.scalar.copy(fresh[:, n % 2, :], core.bank(n % 2)[:, 0:G_DIM]).then_inc(fresh_stored, 1)

        @block.vector
        def _(dve):
            for n, (t, h) in enumerate(order):
                dve.wait_ge(step_ready, n + 1)
                dve.wait_ge(out_ready, n + 1)
                nc.vector.scalar_tensor_tensor(out=state[:, h, :], in0=state[:, h, :],
                                               scalar=last_decay[:, h, t:t + 1],
                                               in1=core.bank(4 + n % 2)[:, 0:G_DIM],
                                               op0=ALU.mult, op1=ALU.add).then_inc(state_ready, 1)
                nc.vector.tensor_copy(out[:, t, h * G_DIM:(h + 1) * G_DIM], core.bank(2 + n % 2)[:, 0:G_DIM]
                                      ).then_inc(out_stored, 1)


def third_block(core, a, ident, ones):
    nc = core.nc
    KX, KQ = XBC // P, QKV // P
    cols = core.const(4 * KD + 1)
    conv_s = core.const(CONV_K * KX + KX)
    conv_g = core.const(CONV_K * KQ + KQ)
    keep = core.const(P)
    masks = core.const(7, P)
    d_skip = core.const(S_HEADS)
    bias_col, log_col = core.const(1)[0:ROWS], core.const(1)[0:ROWS]
    sums_tok = core.const(TT, ROWS)
    steps_tok = core.const(TT, S_HEADS)
    beta_tok = core.const(TT, G_HEADS)
    last_sum, last_decay = core.const(G_HEADS, TT), core.const(G_HEADS, TT)
    w_in = columns_of(a["w_in_3"][0])
    section = lambda col: lambda lo, n: w_in(lo + col, n)
    rows = lambda v: v.rearrange("(k p) -> k p", p=P)
    load_columns(core, 0, [rows(a["norm_mix_w_3"][0]), rows(a["ssm_norm_w_3"][0]), rows(a["norm_ffn_w_3"][0]),
                           rows(a["final_norm_w_3"]), a["gdn_norm_w_3"]], cols, ident)
    load_columns(core, 0, [a["ssm_conv_w_3"][0].rearrange("w (f p) -> (w f) p", p=P), rows(a["ssm_conv_b_3"][0])],
                 conv_s, ident)
    load_columns(core, 0, [a["gdn_conv_w_3"][0].rearrange("w (f p) -> (w f) p", p=P)], conv_g[:, 0:CONV_K * KQ], ident)
    with stage(nc, "cleared") as (block, cleared):
        @block.gpsimd
        def _(pool):
            nc.gpsimd.memset(conv_g[:, CONV_K * KQ:(CONV_K + 1) * KQ], 0.0).then_inc(cleared, 1)
            nc.gpsimd.memset(bias_col, 0.0).then_inc(cleared, 1)
            nc.gpsimd.memset(log_col, 0.0).then_inc(cleared, 1)
    column = lambda v: v.unsqueeze(1)
    load_stage(nc, [(keep, a["upper"]), (masks, a["levels"].rearrange("l p i -> p l i")),
                    (d_skip, a["ssm_d_3"][0].partition_broadcast(P)),
                    (bias_col[0:S_HEADS], column(a["ssm_dt_bias_3"][0])),
                    (bias_col[G_ROW:G_ROW + G_HEADS], column(a["gdn_dt_bias_3"][0])),
                    (log_col[0:S_HEADS], column(a["ssm_a_log_3"][0])),
                    (log_col[G_ROW:G_ROW + G_HEADS], column(a["gdn_a_log_3"][0]))])
    norm_stage(core, ones, cols[:, 0:KD])

    merged = core.work(0, KD, T)
    small = core.work(4096, TT, 2 * S_HEADS)
    delta_rows = core.work(WORK_WORDS - 2 * T, 2, T)[0:G_HEADS]
    raw, steps_row = core.work(8192, T)[0:ROWS], core.work(8192 + T, T)[0:ROWS]
    beta_raw = core.work(8192 + 2 * T, T)[0:G_HEADS]
    sums = core.work(28672, SPAN_WORDS)[0:ROWS]
    small_projections(core, a["w_in_3"][0].rearrange("(k p) n -> p k n", p=P), small)
    with stage(nc, "cleared") as (block, cleared):
        @block.gpsimd
        def _(pool):
            nc.gpsimd.memset(raw, 0.0).then_inc(cleared, 1)
    flip(core, [([small[:, t, lo:lo + n] for t in range(TT)], dst, 1.0) for lo, n, dst in (
        (0, S_HEADS, raw[0:S_HEADS, :]), (S_HEADS, G_HEADS, raw[G_ROW:G_ROW + G_HEADS, :]),
        (S_HEADS + G_HEADS, G_HEADS, beta_raw))], ident)
    decay_stage(core, raw, beta_raw, bias_col, log_col, steps_row, sums, delta_rows, 8192 + 3 * T)
    flip(core, [([sums[:, lo:lo + P] for lo, _ in SPANS], sums_tok.rearrange("p t h -> p (t h)"), 1.0),
                ([steps_row[0:S_HEADS, t * P:(t + 1) * P] for t in range(TT)],
                 steps_tok.rearrange("p t h -> p (t h)"), 1.0),
                ([delta_rows[:, 1, t * P:(t + 1) * P] for t in range(TT)],
                 beta_tok.rearrange("p t h -> p (t h)"), 1.0)], ident)

    xbc = core.work(0, KX, T)
    xs, xdt = core.work(6144, TT, S_INNER), core.work(10240, TT, S_INNER)
    y = core.work(14336, TT, S_INNER)
    project_features(core, section(XBC_COL), KX, xbc, ACT.Silu,
                     conv=(conv_s[:, 0:CONV_K * KX], conv_s[:, CONV_K * KX:(CONV_K + 1) * KX]))
    flip(core, [([xbc[:, 4 * g + k, t * P:(t + 1) * P] for k in range(4)], xs[:, t, g * 4 * P:(g + 1) * 4 * P], 1.0)
                for t in range(TT) for g in range(2)], ident)
    by_head = lambda v: v.rearrange("p t (h d) -> p t h d", h=S_HEADS)
    multiply_stage(core, [(by_head(xdt)[:, t], by_head(xs)[:, t],
                           steps_tok[:, t, :].unsqueeze(2).broadcast_to([P, S_HEADS, DH])) for t in range(TT)])
    ssd_stage(core, ones, ident, xbc[:, 8:10, :], xbc[:, 10:12, :], xs, xdt, sums, sums_tok, d_skip, keep, y, 18432)
    z = core.work(0, TT, S_INNER)
    project_tokens(core, section(Z_COL), S_INNER, z, func=ACT.Silu)
    multiply_stage(core, [(y[:, t], y[:, t], z[:, t]) for t in range(TT)])
    head_norms(core, [y.rearrange("p t (g w) -> p t g w", g=S_GROUPS)], 18432, TT * S_INNER)
    y_T = core.work(4096, KD, T)
    flip(core, [([y[:, t, k * P:(k + 1) * P] for t in range(TT)], y_T[:, k, :], cols[:, KD + k:KD + k + 1])
                for k in range(KD)], ident)
    gate = core.work(8192, KD, T)
    project_features(core, section(GATE_S_COL), KD, gate, ACT.Sigmoid)
    rows_product(core, y_T, KD, rows_of(a["w_proj_ssm_3"][0]),
                 lambda m: nc.vector.tensor_tensor(merged[:, m, :], gate[:, m, :], core.bank(m), ALU.mult))

    qkv = core.work(4096, KQ, T)
    q_T, k_T, v_T = (qkv[:, n * G_HEADS:(n + 1) * G_HEADS, :] for n in range(3))
    k_tok, v_tok = core.work(16384, TT, D), core.work(20480, TT, D)
    couple_T, attn_T = core.work(24576, G_HEADS, T), core.work(28672, G_HEADS, T)
    project_features(core, section(QKV_COL), KQ, qkv, ACT.Silu,
                     conv=(conv_g[:, 0:CONV_K * KQ], conv_g[:, CONV_K * KQ:(CONV_K + 1) * KQ]))
    unit_stage(core, ones, qkv, 2 * G_HEADS, G_HEADS, 0)
    flip(core, [([src[:, 4 * g + k, t * P:(t + 1) * P] for k in range(4)], dst[:, t, g * 4 * P:(g + 1) * 4 * P], 1.0)
                for src, dst in ((k_T, k_tok), (v_T, v_tok)) for t in range(TT) for g in range(2)], ident)
    delta_prepare(core, ones, ident, q_T, k_T, delta_rows, sums_tok, keep, couple_T, attn_T, last_sum, last_decay)
    inverse_T = v_T
    delta_solve(core, ident, masks, couple_T, inverse_T)
    minus_w_T, tail_k = k_T, core.work(24576, TT, D)
    delta_inputs(core, k_tok, v_tok, beta_tok, sums_tok, last_sum, inverse_T, minus_w_T, tail_k)
    o = k_tok
    delta_scan(core, q_T, v_tok, tail_k, inverse_T, minus_w_T, attn_T, last_decay, o)
    gz = core.work(20480, TT, D)
    project_tokens(core, section(GZ_COL), D, gz, func=ACT.Silu)
    head_norms(core, [o.rearrange("p t (h d) -> p t h d", h=G_HEADS)], 24576, TT * D)
    multiply_stage(core, [(o[:, t], o[:, t], gz[:, t]) for t in range(TT)])
    o_T = core.work(4096, KD, T)
    flip(core, [([o[:, t, k * P:(k + 1) * P] for t in range(TT)], o_T[:, k, :], cols[:, 4 * KD:4 * KD + 1])
                for k in range(KD)], ident)
    project_features(core, section(GATE_G_COL), KD, gate, ACT.Sigmoid)
    rows_product(core, o_T, KD, rows_of(a["w_proj_gdn_3"][0]),
                 lambda m: nc.vector.tensor_tensor(gate[:, m, :], gate[:, m, :], core.bank(m), ALU.mult))
    with stage(nc, "added") as (block, added):
        @block.vector
        def _(dve):
            for m in range(KD):
                nc.vector.tensor_tensor(merged[:, m, :], merged[:, m, :], gate[:, m, :], ALU.add).then_inc(added, 1)
    rows_product(core, merged, KD, rows_of(a["w_out_3"][0]), add_to_residual(core))
    norm_stage(core, ones, cols[:, 2 * KD:3 * KD])
    ffn = columns_of(a["w_ffn_in_3"][0])
    swiglu(core, ffn, lambda lo, n: ffn(lo + D_FF, n), rows_of(a["w_ffn_down_3"][0]))
    norm_stage(core, ones, cols[:, 3 * KD:4 * KD], out=core.x)


def shape_constants():
    pos = np.arange(T, dtype=np.float32)

    def rope(dim):
        inv = np.float32(10000.0) ** (-np.arange(0, dim, 2, dtype=np.float32) / np.float32(dim))
        ang = pos[:, None] * inv[None, :].astype(np.float32)
        c, s = np.cos(ang), np.sin(ang)
        return np.concatenate([c, c], 1), np.concatenate([-s, s], 1)

    def tiles(m):
        return m.reshape(TT, P, -1).transpose(1, 0, 2).reshape(P, -1)

    c64, s64 = rope(64)
    c32, s32 = rope(32)
    dist = T - 1 - np.arange(BIAS_ROW)
    exact = REL_BUCKETS // 2
    d = np.maximum(dist, 1).astype(np.float32)
    log_b = exact + (np.log(d / np.float32(exact)) / np.float32(math.log(REL_MAX_DIST / exact))
                     * np.float32(REL_BUCKETS - exact)).astype(np.int32)
    bucket = np.where(dist < exact, dist, np.clip(log_b, exact, REL_BUCKETS - 1))
    bucket = np.where(dist < 0, REL_BUCKETS, bucket)
    q = np.arange(P)[:, None]
    k = np.arange(P)[None, :]
    chunk = np.where(k // 64 <= q // 64, 0.0, NEG)
    out = {
        "ident": np.eye(P), "ones": np.ones((P, P)), "chunk_mask": chunk,
        "cos64": tiles(c64), "sin64": tiles(s64), "cos32": tiles(c32), "sin32": tiles(s32),
        "buckets": bucket[None, :] == np.arange(REL_BUCKETS + 1)[:, None],
        "levels": np.stack([(q // (2 * b) == k // (2 * b)) & (q // b % 2 == 0) & (k // b % 2 == 1)
                            for b in (1, 2, 4, 8, 16, 32, 64)]),
        "reversed": np.eye(P)[::-1], "upper": q <= k, "row_valid": q >= CMP_BLOCK - 1,
        "lam_init": np.array([[0.8 - 0.6 * math.exp(-0.3 * n), 1.0 - (0.8 - 0.6 * math.exp(-0.3 * n))]
                              for n in range(2)]),
    }
    return {n: np.ascontiguousarray(v, dtype=np.float32) for n, v in out.items()}


def common_constants(core, a):
    names = ["ident", "ones", "chunk_mask", "cos64", "sin64", "cos32", "sin32"]
    views = {n: core.const(a[n].shape[1]) for n in names}
    load_stage(core.nc, [(views[n], a[n]) for n in names])
    tables = [views[n].rearrange("p (t d) -> p t d", t=TT) for n in names[3:]]
    return views["ident"], views["ones"], views["chunk_mask"], tables


def build(nc, a, bias_rows, out):
    core = Core(nc)
    ident, ones, chunk_mask, tables = common_constants(core, a)
    resident = core.const_used
    load_input(core, a["x"][0], ident)
    first_block(core, a, bias_rows, ident, ones)
    core.const_used = resident
    second_block(core, a, tables, chunk_mask, ident, ones)
    core.const_used = CONST_AT + 2 * P
    third_block(core, a, ident, ones)
    store_output(core, core.x, out[0], ident)


def kernel(**inputs):
    import concourse.bacc as bacc
    from concourse.bass_utils import run_bass_kernel_spmd

    nc = bacc.Bacc("TRN2", target_bir_lowering=False, num_devices=1)
    arrays, views = {}, {}
    for name, value in {**inputs, **shape_constants()}.items():
        array = np.ascontiguousarray(value)
        arrays[f"in_{name}"] = array
        views[name] = nc.dram_tensor(f"in_{name}", array.shape, F32, kind="ExternalInput").ap()
    bias_rows = nc.dram_tensor("bias_rows", (Q_HEADS, BIAS_ROW), F32).ap()
    out = nc.dram_tensor("out_0", (1, T, D), F32, kind="ExternalOutput").ap()
    build(nc, views, bias_rows, out)
    result = run_bass_kernel_spmd(nc, [arrays], core_ids=[0])
    return result.results[0]["out_0"]
```

```python
import math
from contextlib import ExitStack, contextmanager

import numpy as np

import concourse.bass as bass
from concourse import mybir
from concourse.alu_op_type import AluOpType as ALU

F32 = mybir.dt.float32
ACT = mybir.ActivationFunctionType
AX_X = mybir.AxisListType.X

P = 128
T = 512
TT = T // P
D = 1024
KD = D // P
BANK = 512
BANKS = 8
D_FF = 2816
KF = D_FF // P
CONV_K = 4
EPS = 1e-6
NEG = -1e30


F32R = mybir.dt.float32r
UNIT = 2048
X_AT = 0
H_AT = X_AT + KD * T
RING_AT = H_AT + 2 * KD * T
RING_WORDS = 6 * UNIT
CONST_AT = RING_AT + RING_WORDS
CONST_WORDS = 2000
WORK_AT = CONST_AT + CONST_WORDS
ARENA = 52176
WORK_WORDS = ARENA - WORK_AT
SOURCE_AT = 16384


class Core:

    def __init__(self, nc):
        self.nc = nc
        start = -(-nc.sbuf_base // 32) * 32
        self.regions = []
        for name, at, end in (("residual", X_AT, H_AT), ("normed", H_AT, RING_AT), ("ring", RING_AT, CONST_AT),
                              ("constants", CONST_AT, WORK_AT), ("work", WORK_AT, ARENA)):
            tensor = nc.alloc_sbuf_tensor_at(name, [P, end - at], F32, offset=start + 4 * at)
            self.regions.append((tensor, at, end))

        def over(name, at, *dims):
            tensor = nc.alloc_sbuf_tensor_at(name, [P, *dims], F32R, offset=start + 4 * at)
            return tensor[tuple([slice(None)] * (1 + len(dims)))]

        self.psum = nc.alloc_psum_tensor("psum", [P, BANKS, BANK], F32)
        self.x = self.cut(X_AT, KD, T)
        self.h_hi, self.h_lo = over("h_hi", H_AT, KD, T), over("h_lo", H_AT + KD * T, KD, T)
        self.w_hi, self.w_lo = over("w_hi", RING_AT + 2 * UNIT, 2, UNIT), over("w_lo", RING_AT + 4 * UNIT, 2, UNIT)
        self.s_hi = over("s_hi", WORK_AT + SOURCE_AT, 2, 2, T)
        self.s_lo = over("s_lo", WORK_AT + SOURCE_AT + 4 * T, 2, 2, T)
        self.const_used = CONST_AT

    def cut(self, at, *dims):
        n = int(np.prod(dims))
        tensor, first = next((r, a) for r, a, end in self.regions if a <= at and at + n <= end)
        v = tensor[:, at - first:at - first + n]
        if len(dims) == 2:
            v = v.rearrange("p (a b) -> p a b", a=dims[0])
        elif len(dims) == 3:
            v = v.rearrange("p (a b c) -> p a b c", a=dims[0], b=dims[1])
        return v

    def work(self, at, *dims):
        return self.cut(WORK_AT + at, *dims)

    def ring(self, at, *dims):
        assert at + int(np.prod(dims)) <= RING_WORDS
        return self.cut(RING_AT + at, *dims)

    def const(self, *dims):
        at = self.const_used
        self.const_used += int(np.prod(dims))
        assert self.const_used <= WORK_AT
        return self.cut(at, *dims)

    def raw(self, half, a):
        return self.cut(RING_AT + half * UNIT, a, UNIT // a)

    def bank(self, b):
        return self.psum[:, b, :]


@contextmanager
def stage(nc, *names, starts={}, from_one=()):
    mark = nc.get_next_instruction_name()
    sems = [nc.alloc_semaphore(f"{n}_{mark}") for n in names]
    for n, value in {**dict.fromkeys(from_one, 1), **starts}.items():
        nc.sync.sem_inc(sems[names.index(n)], value)
    with nc.Block() as block:
        yield (block, *sems)
    nc.clear_and_free_semaphores(sems)
    nc.all_engine_barrier()


class Count:

    def __init__(self, engine, sem, base=0):
        self.engine, self.sem, self.base, self.n = engine, sem, base, 0

    def step(self, ins):
        self.n += 1
        ins.then_inc(self.sem, 1)

    def settle(self):
        self.engine.wait_ge(self.sem, self.base + self.n)

    def link(self, ins):
        self.step(ins)
        self.settle()


def hold(engine, sem, value):
    engine.wait_ge(sem, value)
    engine.nop(nofuse=True)


def pairs(n):
    return n // 2, n % 2


def norm_stage(core, ones, gain, out=None, following=None):
    nc, x = core.nc, core.x
    sq = core.cut(H_AT + KD * T, KD, T)
    rstd = core.ring(5 * UNIT, 2, T)
    whole = sq if out is None else out
    total = core.bank(0)
    with stage(nc, *UNIT_SEMS, "squared_act", "squared_dve", "summed", "mean_ready", "root_ready", "inverted", "normed",
               "rounded", "rests", starts=UNIT_STARTS) as (block, *sems):
        squared_act, squared_dve, summed, mean_ready, root_ready, inverted, normed, rounded, rests = sems[8:]

        def rest(dve, k):
            dve.wait_ge(rounded, k + 1)
            nc.vector.tensor_tensor(core.h_lo[:, k, :], whole[:, k, :], core.h_hi[:, k, :].bitcast(F32),
                                    ALU.subtract).then_inc(rests, 1)

        @block.sync
        def _(sp):
            load_following(core, sp, sems, following, (0, 0))

        @block.scalar
        def _(act):
            for k in range(0, KD, 2):
                nc.scalar.activation(sq[:, k, :], x[:, k, :], ACT.Square).then_inc(squared_act, 1)
            round_following(core, act, sems, following, 0, 1)
            act.wait_ge(mean_ready, 1)
            nc.scalar.activation(rstd[:, 1, :], rstd[:, 0, :], ACT.Sqrt).then_inc(root_ready, 1)
            for k in range(KD if out is None else 0):
                act.wait_ge(normed, k + 1)
                nc.scalar.activation(core.h_hi[:, k, :], whole[:, k, :], ACT.Copy).then_inc(rounded, 1)

        @block.tensor
        def _(pe):
            for k in range(KD):
                pe.wait_ge((squared_act, squared_dve)[k % 2], k // 2 + 1)
                mm = nc.tensor.matmul(total, ones, sq[:, k, :], start=(k == 0), stop=(k == KD - 1))
            mm.then_inc(summed, 1)

        @block.vector
        def _(dve):
            for k in range(1, KD, 2):
                nc.vector.tensor_tensor(sq[:, k, :], x[:, k, :], x[:, k, :], ALU.mult).then_inc(squared_dve, 1)
            dve.wait_ge(summed, 1)
            nc.vector.tensor_scalar(rstd[:, 0, :], total, 1.0 / D, EPS, ALU.mult, ALU.add).then_inc(mean_ready, 1)
            rest_following(core, dve, sems, following, 0)
            dve.wait_ge(root_ready, 1)
            nc.vector.reciprocal(rstd[:, 0, :], rstd[:, 1, :]).then_inc(inverted, 1)
            dve.wait_ge(inverted, 1)
            for k in range(KD):
                nc.vector.scalar_tensor_tensor(out=whole[:, k, :], in0=x[:, k, :], scalar=gain[:, k:k + 1],
                                               in1=rstd[:, 0, :], op0=ALU.mult, op1=ALU.mult).then_inc(normed, 1)
                if out is None and k >= 1:
                    rest(dve, k - 1)
            if out is None:
                rest(dve, KD - 1)


UNIT_SEMS = ("loaded0", "loaded1", "rounded0", "rounded1", "split0", "split1", "used0", "used1")
UNIT_STARTS = {"split0": 1, "split1": 1, "used0": 1, "used1": 1}


def load_unit(core, sp, sems, c, half, a, src):
    loaded, split = sems[0:2], sems[4:6]
    hold(sp, split[half], c + 1)
    sp.dma_start(core.raw(half, a)[:, :, 0:src.shape[2]], src).then_inc(loaded[half], 16)


def round_unit(core, act, sems, c, half, per, a=1, n=UNIT):
    loaded, rounded, used = sems[0:2], sems[2:4], sems[6:8]
    act.wait_ge(loaded[half], 16 * c + 16)
    act.wait_ge(used[half], per * c + 1)
    hi = core.w_hi[:, half, :].rearrange("p (a b) -> p a b", a=a)[:, :, 0:n]
    core.nc.scalar.activation(hi, core.raw(half, a)[:, :, 0:n], ACT.Copy).then_inc(rounded[half], 1)


def rest_unit(core, dve, sems, c, half, a=1, n=UNIT):
    rounded, split = sems[2:4], sems[4:6]
    dve.wait_ge(rounded[half], c + 1)
    hi, lo = (w[:, half, :].rearrange("p (a b) -> p a b", a=a)[:, :, 0:n] for w in (core.w_hi, core.w_lo))
    core.nc.vector.tensor_tensor(lo, core.raw(half, a)[:, :, 0:n], hi.bitcast(F32), ALU.subtract
                                 ).then_inc(split[half], 1)


def load_following(core, sp, sems, following, done):
    for half, (a, src) in enumerate(following or ()):
        load_unit(core, sp, sems, done[half], half, a, src)
    for half in range(2 if following else 0):
        sp.wait_ge(sems[half], 16 * done[half] + 16)


def round_following(core, act, sems, following, done, per):
    if following:
        a, src = following[0]
        round_unit(core, act, sems, done, 0, per, a, src.shape[2])


def rest_following(core, dve, sems, following, done):
    if following:
        a, src = following[0]
        rest_unit(core, dve, sems, done, 0, a, src.shape[2])


def first_columns(weight, cols):
    return [(KD // 2, weight(half * KD // 2, 0, min(cols, BANK))) for half in range(2)]


def first_rows(weight):
    return [(2, weight(2 * half)) for half in range(2)]


LOADED, SPLIT = 1, 2


def prepared_starts(prepared):
    starts = dict(UNIT_STARTS)
    if prepared:
        starts.update(loaded0=16, loaded1=16)
    if prepared == SPLIT:
        starts.update(rounded0=1, split0=2)
    return starts


def walk_loads(sp, n, load, prepared):
    if prepared:
        walk(sp, n - 1, lambda c, j: load(c + 1, j))
    else:
        walk(sp, n, load)


def unsplit(c, prepared):
    return range(1 if isinstance(c, int) and c == 0 and prepared == SPLIT else 0, 2)


def walk(engine, n, visit, ahead=None):
    bodies = max(n - 2, 0) // 2
    if ahead:
        ahead(0)
    if bodies:
        with engine.Fori(0, bodies) as i:
            for j in range(2):
                if ahead:
                    ahead(2 * i + j + 1)
                visit(2 * i + j, j)
    for c in range(2 * bodies, n):
        if ahead:
            ahead(c + 1)
        visit(c, c % 2)


def three_passes(nc, bank, left, right, start, stop):
    (l_hi, l_lo), (r_hi, r_lo) = left, right
    nc.tensor.matmul(bank, l_hi, r_hi, start=start, stop=False)
    nc.tensor.matmul(bank, l_hi, r_lo, start=False, stop=False)
    return nc.tensor.matmul(bank, l_lo, r_hi, start=False, stop=stop)


def seen(core, half, a, k, lo, hi):
    b = UNIT // a
    return [w[:, half, k * b + lo:k * b + hi] for w in (core.w_hi, core.w_lo)]


def project(core, weight, cols, dst, func, conv=None, to_tokens=False, prepared=0, following=None):
    nc = core.nc
    chunks = -(-cols // BANK)
    tiles = cols // P
    KH = KD // 2

    def width(c):
        return cols - c * BANK if isinstance(c, int) and c == chunks - 1 else BANK

    with stage(nc, *UNIT_SEMS, "based", "convolved", "conv_steps", "stored",
               starts={**prepared_starts(prepared), "stored": 5}) as (block, *sems):
        used = sems[6:8]
        based, convolved, conv_steps, stored = sems[8:12]

        @block.sync
        def _(sp):
            def load(c, j):
                for half in range(2):
                    load_unit(core, sp, sems, c, half, KH, weight(half * KH, c * BANK, width(c)))
            walk_loads(sp, chunks, load, prepared)
            load_following(core, sp, sems, following, (chunks, chunks))

        @block.tensor
        def _(pe):
            def multiply(c, j):
                n = width(c)
                pe.wait_ge(stored, 4 * c + 1)
                for half in range(2):
                    pe.wait_ge(sems[4 + half], c + 2)
                    for m in range(4):
                        s = slice(m * P, (m + 1) * P)
                        for k in range(KH):
                            f = half * KH + k
                            ends = dict(start=(f == 0), stop=(f == KD - 1))
                            if to_tokens:
                                mm = three_passes(nc, core.bank(4 * j + m)[:, 0:n],
                                                  (core.h_hi[:, f, s], core.h_lo[:, f, s]),
                                                  seen(core, half, KH, k, 0, n), **ends)
                            else:
                                mm = three_passes(nc, core.bank(4 * j + m), seen(core, half, KH, k, m * P, (m + 1) * P),
                                                  (core.h_hi[:, f, :], core.h_lo[:, f, :]), **ends)
                        if half or m == 3:
                            mm.then_inc(used[half], 1)
            walk(pe, chunks, multiply)

        @block.scalar
        def _(act):
            def ahead(c):
                if isinstance(c, int) and c == chunks:
                    round_following(core, act, sems, following, c, 1)
                    return
                for half in unsplit(c, prepared):
                    round_unit(core, act, sems, c, half, (1, 4)[half], KH, width(c))

            def finish(c, j):
                n = width(c)
                for m in range(4 if func is not None else 0):
                    hold(act, used[1], 4 * c + m + 2)
                    to = dst[:, m, bass.ds(c * BANK, n)] if to_tokens else dst[:, 4 * c + m, :]
                    bank = core.bank(4 * j + m)[:, 0:n]
                    if conv is None:
                        nc.scalar.activation(to, bank, func).then_inc(stored, 1)
                    else:
                        tap = conv[0][:, bass.ds((CONV_K - 1) * tiles + 4 * c + m, 1)]
                        nc.scalar.activation(to, bank, ACT.Identity, scale=tap,
                                             bias=conv[1][:, bass.ds(4 * c + m, 1)]).then_inc(based, 1)
                for m in range(4 if conv else 0):
                    hold(act, convolved, 4 * c + m + 1)
                    to = dst[:, 4 * c + m, :]
                    nc.scalar.activation(to, to, func).then_inc(stored, 1)
            walk(act, chunks, finish, ahead)

        @block.vector
        def _(dve):
            def ahead(c):
                if isinstance(c, int) and c == chunks:
                    rest_following(core, dve, sems, following, c)
                    return
                for half in unsplit(c, prepared):
                    rest_unit(core, dve, sems, c, half, KH, width(c))

            def finish(c, j):
                n = width(c)
                for m in range(4 if func is None else 0):
                    dve.wait_ge(used[1], 4 * c + m + 2)
                    nc.vector.tensor_copy(dst[:, m, bass.ds(c * BANK, n)], core.bank(4 * j + m)[:, 0:n]
                                          ).then_inc(stored, 1)
                for m in range(4 if conv else 0):
                    t = 4 * c + m
                    dve.wait_ge(based, t + 1)
                    for back in range(1, CONV_K):
                        ins = nc.vector.scalar_tensor_tensor(
                            out=dst[:, t, back:T], in0=core.bank(4 * j + m)[:, 0:T - back],
                            scalar=conv[0][:, bass.ds((CONV_K - 1 - back) * tiles + t, 1)],
                            in1=dst[:, t, back:T], op0=ALU.mult, op1=ALU.add)
                        if back < CONV_K - 1:
                            ins.then_inc(conv_steps, 1)
                            dve.wait_ge(conv_steps, (CONV_K - 2) * t + back)
                    ins.then_inc(convolved, 1)
            walk(dve, chunks, finish, ahead)


def rows_product(core, src, tiles, weight, finish, prepared=0, following=None):
    nc = core.nc
    units = tiles // 2
    chunks = -(-units // 2)
    assert units % 2 == 0 or following is None

    def halves(c):
        return range(1 if isinstance(c, int) and 2 * c + 1 == units else 2)

    with stage(nc, *UNIT_SEMS, "source_rounded", "banks_full", "finished",
               starts={**prepared_starts(prepared), "split0": 1}) as (block, *sems):
        used = sems[6:8]
        source_rounded, banks_full, finished = sems[8:11]

        @block.sync
        def _(sp):
            def load(c, j):
                for half in halves(c):
                    load_unit(core, sp, sems, c, half, 2, weight(4 * c + 2 * half))
            walk_loads(sp, chunks, load, prepared)
            load_following(core, sp, sems, following, (chunks, chunks))

        @block.tensor
        def _(pe):
            def multiply(c, j):
                for half in halves(c):
                    last = isinstance(c, int) and 2 * c + half == units - 1
                    pe.wait_ge(sems[4 + half], c + 2)
                    for a in range(2):
                        for m in range(KD):
                            mm = three_passes(nc, core.bank(m), seen(core, half, 2, a, m * P, (m + 1) * P),
                                              (core.s_hi[:, half, a, :], core.s_lo[:, half, a, :]),
                                              start=(isinstance(c, int) and c + half + a == 0), stop=(last and a == 1))
                            if last and a == 1:
                                mm.then_inc(banks_full, 1)
                    if not last:
                        mm.then_inc(used[half], 1)
            multiply(0, 0)
            if chunks > 2:
                with pe.Fori(1, chunks - 1) as c:
                    multiply(c, 0)
            multiply(chunks - 1, 0)

        @block.scalar
        def _(act):
            def split(c, j):
                for half in halves(c):
                    hold(act, used[half], c + 1)
                    nc.scalar.activation(core.s_hi[:, half, :, :], src[:, bass.ds(4 * c + 2 * half, 2), :],
                                         ACT.Copy).then_inc(source_rounded, 1)
                    if half in unsplit(c, prepared):
                        round_unit(core, act, sems, c, half, 1)
            split(0, 0)
            walk(act, chunks - 1, lambda c, j: split(c + 1, j))
            round_following(core, act, sems, following, chunks, 1)

        @block.vector
        def _(dve):
            def split(c, j):
                for half in halves(c):
                    dve.wait_ge(source_rounded, 2 * c + half + 1)
                    source_rest = nc.vector.tensor_tensor(
                        core.s_lo[:, half, :, :], src[:, bass.ds(4 * c + 2 * half, 2), :],
                        core.s_hi[:, half, :, :].bitcast(F32), ALU.subtract)
                    if half in unsplit(c, prepared):
                        rest_unit(core, dve, sems, c, half)
                    else:
                        source_rest.then_inc(sems[4], 1)
            split(0, 0)
            walk(dve, chunks - 1, lambda c, j: split(c + 1, j))
            rest_following(core, dve, sems, following, chunks)
            for m in range(KD):
                dve.wait_ge(banks_full, m + 1)
                finish(m).then_inc(finished, 1)


def add_to_residual(core):
    def finish(m):
        return core.nc.vector.tensor_tensor(core.x[:, m, :], core.x[:, m, :], core.bank(m), ALU.add)
    return finish


CHUNK_COLS = UNIT // KD
FF_CHUNKS = D_FF // CHUNK_COLS
CT = CHUNK_COLS // P


def first_gates(gate_w, up_w):
    return [(KD, w(0, 0, CHUNK_COLS, KD)) for w in (gate_w, up_w)]


def gated_hidden(core, gate_w, up_w, hidden, conv=None, prepared=0, following=None):
    nc = core.nc
    scratch = core.work(KF * T, 4 * CT, T)
    taps, width, bias = conv if conv else (None, 0, None)
    with stage(nc, *UNIT_SEMS, "silus", "made", "biased", "convolved", "conv_steps",
               starts={**prepared_starts(prepared), "made": CT + 1}) as (block, *sems):
        used = sems[6:8]
        silus, made, biased, convolved, conv_steps = sems[8:13]

        @block.sync
        def _(sp):
            def load(c, j):
                for half, w in enumerate((gate_w, up_w)):
                    load_unit(core, sp, sems, c, half, KD, w(0, c * CHUNK_COLS, CHUNK_COLS, KD))
            walk_loads(sp, FF_CHUNKS, load, prepared)
            load_following(core, sp, sems, following, (FF_CHUNKS, FF_CHUNKS))

        @block.tensor
        def _(pe):
            def multiply(c, j):
                pe.wait_ge(made, CT * c + 1)
                for half in range(2):
                    pe.wait_ge(sems[4 + half], c + 2)
                    for m in range(CT):
                        for k in range(KD):
                            mm = three_passes(nc, core.bank(4 * j + CT * half + m),
                                              seen(core, half, KD, k, m * P, (m + 1) * P),
                                              (core.h_hi[:, k, :], core.h_lo[:, k, :]),
                                              start=(k == 0), stop=(k == KD - 1))
                        mm.then_inc(used[half], 1)
            walk(pe, FF_CHUNKS, multiply)

        @block.scalar
        def _(act):
            def ahead(c):
                if isinstance(c, int) and c == FF_CHUNKS:
                    round_following(core, act, sems, following, c, CT)
                    return
                for half in unsplit(c, prepared):
                    round_unit(core, act, sems, c, half, CT)

            def work(c, j):
                act.wait_ge(made, CT * c + 1)
                for n in range(2 * CT if conv else CT):
                    half, m = n // CT, n % CT
                    hold(act, used[half], CT * c + m + 2)
                    to = scratch[:, 2 * CT * j + n, :]
                    if conv is None:
                        nc.scalar.activation(to, core.bank(4 * j + n), ACT.Silu).then_inc(silus, 1)
                    else:
                        f = (1 - half) * KF
                        nc.scalar.activation(to, core.bank(4 * j + n), ACT.Identity,
                                             scale=taps[:, bass.ds(2 * KF * (width - 1) + f + CT * c + m, 1)],
                                             bias=bias[:, bass.ds(f + CT * c + m, 1)]).then_inc(biased, 1)
                for m in range(CT if conv else 0):
                    act.wait_ge(convolved, 2 * CT * c + m + 1)
                    to = scratch[:, 2 * CT * j + m, :]
                    nc.scalar.activation(to, to, ACT.Silu).then_inc(silus, 1)
            walk(act, FF_CHUNKS, work, ahead)

        @block.vector
        def _(dve):
            def ahead(c):
                if isinstance(c, int) and c == FF_CHUNKS:
                    rest_following(core, dve, sems, following, c)
                    return
                for half in unsplit(c, prepared):
                    rest_unit(core, dve, sems, c, half)

            def work(c, j):
                for n in range(2 * CT if conv else 0):
                    half, m = n // CT, n % CT
                    dve.wait_ge(biased, 2 * CT * c + n + 1)
                    s = scratch[:, 2 * CT * j + n, :]
                    for back in range(1, width):
                        tap = taps[:, bass.ds(2 * KF * (width - 1 - back) + (1 - half) * KF + CT * c + m, 1)]
                        ins = nc.vector.scalar_tensor_tensor(
                            out=s[:, back:T], in0=core.bank(4 * j + n)[:, 0:T - back], scalar=tap,
                            in1=s[:, back:T], op0=ALU.mult, op1=ALU.add)
                        if back < width - 1:
                            ins.then_inc(conv_steps, 1)
                            dve.wait_ge(conv_steps, (width - 2) * (2 * CT * c + n) + back)
                    ins.then_inc(convolved, 1)
                for m in range(CT):
                    dve.wait_ge(silus, CT * c + m + 1)
                    if conv is None:
                        dve.wait_ge(used[1], CT * c + m + 2)
                        up = core.bank(4 * j + CT + m)
                    else:
                        dve.wait_ge(convolved, 2 * CT * c + CT + m + 1)
                        up = scratch[:, 2 * CT * j + CT + m, :]
                    nc.vector.tensor_tensor(hidden[:, CT * c + m, :], scratch[:, 2 * CT * j + m, :], up,
                                            ALU.mult).then_inc(made, 1)
            walk(dve, FF_CHUNKS, work, ahead)


def flip(core, jobs, ident, following=None):
    nc = core.nc
    with stage(nc, "turned", "stored_act", "stored_dve", "following_in") as (
            block, turned, stored_act, stored_dve, following_in):
        stored = [stored_act, stored_dve]

        @block.sync
        def _(sp):
            for half, (a, src) in enumerate(following or ()):
                sp.dma_start(core.raw(half, a)[:, :, 0:src.shape[2]], src).then_inc(following_in, 16)
            if following:
                sp.wait_ge(following_in, 32)

        @block.tensor
        def _(pe):
            for n, (sources, dst, scale) in enumerate(jobs):
                if n >= BANKS:
                    pe.wait_ge(stored[n % 2], (n - BANKS) // 2 + 1)
                at = 0
                for src in sources:
                    p, c = src.shape
                    mm = nc.tensor.transpose(core.bank(n % BANKS)[0:c, at:at + p], src, ident[0:p, 0:p])
                    at += p
                mm.then_inc(turned, 1)

        def store(engine, parity, put):
            for n, (sources, dst, scale) in enumerate(jobs):
                if n % 2 == parity:
                    c, w = dst.shape
                    all_w = sum(src.shape[0] for src in sources)
                    engine.wait_ge(turned, n + 1)
                    put(dst, core.bank(n % BANKS)[0:c, all_w - w:all_w], scale).then_inc(stored[parity], 1)

        @block.scalar
        def _(act):
            store(act, 0, lambda to, what, scale: nc.scalar.activation(to, what, ACT.Copy, scale=scale))

        @block.vector
        def _(dve):
            store(dve, 1, lambda to, what, scale: nc.vector.tensor_scalar(to, what, scale, None, ALU.mult))


DH = 64
ATTEND_WORDS = 8 * T + 16


def attend(core, scratch_at, ident, loops, unroll, q_of, k_of, v_of, bias_of, out_of, width, keys):
    nc = core.nc
    qs = core.cut(scratch_at, 2, T)
    sb = core.cut(scratch_at + 2 * T, 2, T)
    pb = core.cut(scratch_at + 4 * T, 2, T)
    pt = core.cut(scratch_at + 6 * T, 2, T)
    stats = core.cut(scratch_at + 8 * T, 4, 4)
    steps = unroll * TT

    def cuts(n):
        return [(k, min(P, n - k)) for k in range(0, n, P)]

    with stage(nc, "q_ready", "scored", "biased", "max_ready", "exp_done", "turned", "turned_stored",
               "weighed", "sum_inverted", "out_done",
               from_one=("scored", "biased", "max_ready", "exp_done", "turned", "turned_stored", "weighed",
                         "sum_inverted", "out_done")) as (
            block, q_ready, scored, biased, max_ready, exp_done, turned, turned_stored,
            weighed, sum_inverted, out_done):

        @block.gpsimd
        def _(pool):
            with pool.Fori(0, loops) as i:
                base = i * steps + 1
                for u in range(unroll):
                    if u >= 2:
                        hold(pool, scored, base + TT * (u - 1))
                    else:
                        hold(pool, weighed, base)
                    nc.gpsimd.tensor_copy(qs[0:DH, u % 2, :], q_of(i, u)).then_inc(q_ready, 1)

        @block.tensor
        def _(pe):
            with pe.Fori(0, loops) as i:
                base = i * steps + 1
                for n in range(steps + 2):
                    if n < steps:
                        u, t, b = n // TT, n % TT, n % 2
                        nk = keys(t)
                        if t == 0:
                            pe.wait_ge(q_ready, i * unroll + u + 1)
                        if n >= 2:
                            pe.wait_ge(biased, base + n - 1)
                        pe.nop(nofuse=True)
                        nc.tensor.matmul(core.bank(b)[:, 0:nk], qs[0:DH, u % 2, t * P:(t + 1) * P],
                                         k_of(i, u, nk), start=True, stop=True).then_inc(scored, 1)
                    if 1 <= n <= steps:
                        s = n - 1
                        t, b = s % TT, s % 2
                        pe.wait_ge(exp_done, base + s + 1)
                        if s >= 2:
                            pe.wait_ge(turned_stored, base + s - 1)
                        for k, kn in cuts(keys(t)):
                            mm = nc.tensor.transpose(core.bank(2 + b)[0:kn, k:k + P], pb[:, b, k:k + kn], ident)
                        mm.then_inc(turned, 1)
                    if n >= 2:
                        s = n - 2
                        u, t, b = s // TT, s % TT, s % 2
                        pe.wait_ge(turned_stored, base + s + 1)
                        pe.wait_ge(out_done, base + (s - 1 if s >= 2 else 0))
                        pe.nop(nofuse=True)
                        parts = cuts(keys(t))
                        for c, (k, kn) in enumerate(parts):
                            mm = nc.tensor.matmul(core.bank(4 + b)[:, 0:width], pt[0:kn, b, k:k + P],
                                                  v_of(i, u, c, kn), start=(c == 0), stop=(c == len(parts) - 1))
                        mm.then_inc(weighed, 1)

        @block.vector
        def _(dve):
            with dve.Fori(0, loops) as i:
                base = i * steps + 1
                for n in range(steps + 2):
                    if n < steps:
                        u, t, b = n // TT, n % TT, n % 2
                        nk = keys(t)
                        dve.wait_ge(scored, base + n + 1)
                        dve.wait_ge(exp_done, base + (n - 1 if n >= 2 else 0))
                        nc.vector.tensor_tensor(sb[:, b, 0:nk], core.bank(b)[:, 0:nk], bias_of(i, u, t, nk),
                                                ALU.add).then_inc(biased, 1)
                        dve.wait_ge(biased, base + n + 1)
                        nc.vector.tensor_reduce(stats[:, n % 4, 1:2], sb[:, b, 0:nk], AX_X, ALU.max,
                                                negate=True).then_inc(max_ready, 1)
                    if n >= 2:
                        s = n - 2
                        u, t, b = s // TT, s % TT, s % 2
                        dve.wait_ge(exp_done, base + s + 1)
                        nc.vector.reciprocal(stats[:, s % 4, 3:4], stats[:, s % 4, 2:3]).then_inc(sum_inverted, 1)
                        dve.wait_ge(sum_inverted, base + s + 1)
                        dve.wait_ge(weighed, base + s + 1)
                        nc.vector.tensor_scalar(out_of(i, u, t), core.bank(4 + b)[:, 0:width],
                                                stats[:, s % 4, 3:4], None, ALU.mult).then_inc(out_done, 1)

        @block.scalar
        def _(act):
            with act.Fori(0, loops) as i:
                base = i * steps + 1
                for n in range(steps + 1):
                    if n < steps:
                        t, b = n % TT, n % 2
                        nk = keys(t)
                        act.wait_ge(max_ready, base + n + 1)
                        act.wait_ge(turned, base + (n - 1 if n >= 2 else 0))
                        nc.scalar.activation(pb[:, b, 0:nk], sb[:, b, 0:nk], ACT.Exp,
                                             bias=stats[:, n % 4, 1:2],
                                             accum_out=stats[:, n % 4, 2:3]).then_inc(exp_done, 1)
                    if n >= 1:
                        s = n - 1
                        t, b = s % TT, s % 2
                        act.wait_ge(turned, base + s + 1)
                        act.wait_ge(weighed, base + (s - 1 if s >= 2 else 0))
                        parts = cuts(keys(t))
                        kn, kw = parts[0][1], P * len(parts)
                        nc.scalar.copy(pt[0:kn, b, 0:kw], core.bank(2 + b)[0:kn, 0:kw]).then_inc(turned_stored, 1)


def load_stage(nc, pairs_of):
    with stage(nc, "small_loaded") as (block, small_loaded):
        @block.sync
        def _(sp):
            for dst, src in pairs_of:
                sp.dma_start(dst, src).then_inc(small_loaded, 16)
            sp.wait_ge(small_loaded, 16 * len(pairs_of))


def load_input(core, x, ident):
    nc = core.nc
    xt = core.work(0, TT, D)
    load_stage(nc, [(xt, x.rearrange("(t p) d -> p t d", p=P))])
    flip(core, [([xt[:, t, k * P:(k + 1) * P] for t in range(TT)], core.x[:, k, :], 1.0) for k in range(KD)], ident)


def store_output(core, src, y, ident):
    nc = core.nc
    yt = core.work(0, TT, D)
    flip(core, [([src[:, 4 * g + k, t * P:(t + 1) * P] for k in range(4)],
                 yt[:, t, g * 4 * P:(g + 1) * 4 * P], 1.0) for t in range(TT) for g in range(KD // 4)], ident)
    with stage(nc, "written") as (block, written):
        @block.sync
        def _(sp):
            sp.dma_start(y.rearrange("(t p) d -> p t d", p=P), yt).then_inc(written, 16)
            sp.wait_ge(written, 16)


def load_columns(core, rows_at, entries, dst, ident, width=P):
    parts, at = [], 0
    for src in entries:
        r = src.shape[0]
        done = 0
        while done < r:
            n = min(r - done, P - at % P)
            parts.append((at // P, at % P, n, src[done:done + n, :]))
            at += n
            done += n
    tiles = -(-at // P)
    rows = core.work(rows_at, tiles, P)
    load_stage(core.nc, [(rows[p:p + n, tile, 0:width], src) for tile, p, n, src in parts])
    flip(core, [([rows[0:min(P, at - P * c), c, 0:width] for c in range(tiles)], dst[0:width, 0:at], 1.0)], ident)


Q_HEADS, KV = 8, 2
GROUP = Q_HEADS // KV
D_Q, D_KV = Q_HEADS * DH, KV * DH
Q_COL = 0
KC_COL = Q_COL + D_Q
VC_COL, KS_COL, VS_COL, KW_COL, VW_COL = (KC_COL + D_KV * n for n in range(1, 6))
GATE_COL = VW_COL + D_KV
BRANCHES = 3
U_COL = GATE_COL + Q_HEADS * BRANCHES
D_GMLP = 512
V_COL = U_COL + D_GMLP
D_PROJ = V_COL + D_GMLP
CMP_BLOCK, CMP_STRIDE, CMP_HIDDEN = 32, 16, 256
CMP_N = (T - CMP_BLOCK) // CMP_STRIDE + 1
REL_BUCKETS, REL_MAX_DIST = 32, 128
SGU_GROUPS = 8
BIAS_ROW = T + P


def head_norms(core, views, at, sq_words=4 * T):
    nc = core.nc
    sizes = [v.shape[1] * v.shape[2] for v in views]
    total = sum(sizes)
    p = views[0].shape[0]
    sq = core.work(at, sq_words)
    ms = core.work(at + sq_words, 3, total)
    with stage(nc, "norm_steps", "mean_ready", "root_ready") as (block, norm_steps, mean_ready, root_ready):
        @block.scalar
        def _(act):
            act.wait_ge(mean_ready, len(views))
            nc.scalar.activation(ms[0:p, 1, :], ms[0:p, 0, :], ACT.Sqrt).then_inc(root_ready, 1)

        @block.vector
        def _(dve):
            steps = Count(dve, norm_steps)
            lo = 0
            for v, n in zip(views, sizes):
                a, heads, width = v.shape[1:]
                s = sq[0:p, 0:n * width].rearrange("p (a h w) -> p a h w", a=a, h=heads)
                m = ms[0:p, 0, lo:lo + n].rearrange("p (a h) -> p a h", a=a)
                steps.link(nc.vector.tensor_tensor(s, v, v, ALU.mult))
                steps.link(nc.vector.tensor_reduce(m, s, AX_X, ALU.add))
                nc.vector.tensor_scalar(m, m, 1.0 / width, EPS, ALU.mult, ALU.add).then_inc(mean_ready, 1)
                lo += n
            dve.wait_ge(root_ready, 1)
            steps.link(nc.vector.reciprocal(ms[0:p, 2, :], ms[0:p, 1, :]))
            lo = 0
            for v, n in zip(views, sizes):
                a, heads, width = v.shape[1:]
                r = ms[0:p, 2, lo:lo + n].rearrange("p (a h) -> p a h", a=a)
                steps.step(nc.vector.tensor_tensor(v, v, r.unsqueeze(3).broadcast_to([p, a, heads, width]), ALU.mult))
                lo += n


def bias_stage(core, a, bias, scratch_dram, at):
    nc = core.nc
    table = core.work(at, Q_HEADS)
    buckets = core.work(at + Q_HEADS, BIAS_ROW)
    rows = core.work(at + Q_HEADS + BIAS_ROW, BIAS_ROW)
    back = core.work(at + Q_HEADS + 2 * BIAS_ROW, P)
    shifted = core.ring(0, Q_HEADS, T)
    with stage(nc, "small_loaded", "table_ready", "rows_ready", "rows_stored", "shifted_ready", "round_ready",
               "rows_saved", "bias_stored") as (
            block, small_loaded, table_ready, rows_ready, rows_stored, shifted_ready, round_ready, rows_saved,
            bias_stored):
        @block.gpsimd
        def _(pool):
            nc.gpsimd.memset(table[REL_BUCKETS:REL_BUCKETS + 1, :], NEG).then_inc(table_ready, 1)

        @block.sync
        def _(sp):
            sp.dma_start(table[0:REL_BUCKETS, :], a["rel_bias"]).then_inc(small_loaded, 16)
            sp.dma_start(buckets[0:REL_BUCKETS + 1, :], a["buckets"]).then_inc(small_loaded, 16)
            sp.dma_start(back, a["reversed"]).then_inc(small_loaded, 16)
            sp.wait_ge(rows_stored, 2)
            sp.dma_start(scratch_dram, rows[0:Q_HEADS, :]).then_inc(rows_saved, 16)
            sp.wait_ge(rows_saved, 16)
            for h in range(Q_HEADS):
                sp.dma_start(shifted[:, h, :], bass.AP(scratch_dram.tensor, h * BIAS_ROW, [[1, P], [1, T]])
                             ).then_inc(shifted_ready, 16)

        @block.tensor
        def _(pe):
            pe.wait_ge(small_loaded, 48)
            pe.wait_ge(table_ready, 1)
            n = REL_BUCKETS + 1
            for c, (lo, w) in enumerate([(0, T), (T, BIAS_ROW - T)]):
                nc.tensor.matmul(core.bank(c)[0:Q_HEADS, 0:w], table[0:n, :], buckets[0:n, lo:lo + w],
                                 start=True, stop=True).then_inc(rows_ready, 1)
            pe.wait_ge(rows_stored, 2)
            pe.wait_ge(shifted_ready, 16 * Q_HEADS)
            for h in range(Q_HEADS):
                nc.tensor.matmul(core.bank(h), back, shifted[:, h, :], start=True, stop=True).then_inc(round_ready, 1)

        @block.vector
        def _(dve):
            for c, (lo, w) in enumerate([(0, T), (T, BIAS_ROW - T)]):
                dve.wait_ge(rows_ready, c + 1)
                nc.vector.tensor_copy(rows[0:Q_HEADS, lo:lo + w], core.bank(c)[0:Q_HEADS, 0:w]).then_inc(rows_stored, 1)
            for h in range(Q_HEADS):
                dve.wait_ge(round_ready, h + 1)
                nc.vector.tensor_copy(bias[:, h, :], core.bank(h)).then_inc(bias_stored, 1)


def activation_stage(core, jobs):
    nc = core.nc
    with stage(nc, "activated") as (block, activated):
        @block.scalar
        def _(act):
            for out, x, func in jobs:
                nc.scalar.activation(out, x, func).then_inc(activated, 1)


def compress_stage(core, a, turned, pe_cols, b1_cols, out, at):
    nc = core.nc
    pairs_n = CMP_BLOCK // 2
    N = KV * CMP_N
    blocks = core.work(at, 2 * pairs_n, N)
    hid = core.work(at + 2 * pairs_n * N, 4, N)
    w2 = core.work(at + 2 * pairs_n * N + 4 * N, 4, DH)
    hid_tiles = CMP_HIDDEN // P
    with stage(nc, "weights_in", "blocks_ready", "hidden_ready", "hidden_stored", "compressed", "out_stored") as (
            block, weights_in, blocks_ready, hidden_ready, hidden_stored, compressed, out_stored):
        @block.sync
        def _(sp):
            for kind, name in enumerate("kv"):
                w1 = a[f"cmp_w1_{name}"][0].rearrange("(c p) n -> p c n", p=P)
                sp.dma_start(core.ring(kind * pairs_n * CMP_HIDDEN, pairs_n, CMP_HIDDEN), w1).then_inc(weights_in, 16)
                sp.dma_start(w2[:, 2 * kind:2 * kind + 2, :],
                             a[f"cmp_w2_{name}"][0].rearrange("(k p) n -> p k n", p=P)).then_inc(weights_in, 16)

        @block.vector
        def _(dve):
            half = pairs_n // 2
            for kind in range(2):
                for g in range(KV):
                    x = turned[kind][:, g, :].rearrange("p (n s) -> p s n", s=CMP_STRIDE)
                    for hh in range(2):
                        c = kind * pairs_n + half * hh
                        pe_v = pe_cols[:, c:c + half].unsqueeze(2).broadcast_to([P, half, CMP_N])
                        nc.vector.tensor_tensor(blocks[:, c:c + half, g * CMP_N:(g + 1) * CMP_N],
                                                x[:, 0:CMP_STRIDE:2, hh:hh + CMP_N], pe_v,
                                                ALU.add).then_inc(blocks_ready, 1)
            for kind in range(2):
                for g in range(KV):
                    n = kind * KV + g
                    dve.wait_ge(compressed, n + 1)
                    nc.vector.tensor_copy(out[kind][0:CMP_N, g, :], core.bank(4 + n)[0:CMP_N, 0:DH]).then_inc(out_stored, 1)

        @block.tensor
        def _(pe):
            pe.wait_ge(weights_in, 64)
            pe.wait_ge(blocks_ready, 8)
            for kind in range(2):
                w1 = core.ring(kind * pairs_n * CMP_HIDDEN, pairs_n, CMP_HIDDEN)
                for m in range(hid_tiles):
                    for c in range(pairs_n):
                        mm = nc.tensor.matmul(core.bank(2 * kind + m)[:, 0:N], w1[:, c, m * P:(m + 1) * P],
                                              blocks[:, kind * pairs_n + c, :], start=(c == 0), stop=(c == pairs_n - 1))
                    mm.then_inc(hidden_ready, 1)
            for kind in range(2):
                pe.wait_ge(hidden_stored, 2 * kind + 2)
                for g in range(KV):
                    for k in range(hid_tiles):
                        mm = nc.tensor.matmul(core.bank(4 + kind * KV + g)[0:CMP_N, 0:DH],
                                              hid[:, 2 * kind + k, g * CMP_N:(g + 1) * CMP_N],
                                              w2[:, 2 * kind + k, :], start=(k == 0), stop=(k == hid_tiles - 1))
                    mm.then_inc(compressed, 1)

        @block.scalar
        def _(act):
            for n in range(4):
                act.wait_ge(hidden_ready, n + 1)
                nc.scalar.activation(hid[:, n, :], core.bank(n)[:, 0:N], ACT.Gelu_apprx_tanh,
                                     bias=b1_cols[:, n:n + 1]).then_inc(hidden_stored, 1)


def spatial_stage(core, pr, w_T, keep, gain_row, bias_cols, mixed, col):
    nc = core.nc
    width = D_GMLP // SGU_GROUPS
    v = pr[:, :, V_COL:V_COL + D_GMLP]
    with stage(nc, "masked", "gained", "mixed_ready", "gated") as (block, masked, gained, mixed_ready, gated):
        @block.gpsimd
        def _(pool):
            nc.gpsimd.tensor_tensor(w_T, w_T, keep.unsqueeze(1).broadcast_to([P, SGU_GROUPS, P]),
                                    ALU.mult).then_inc(masked, 1)

        @block.tensor
        def _(pe):
            pe.wait_ge(masked, 1)
            pe.wait_ge(gained, 1)
            for g in range(SGU_GROUPS):
                nc.tensor.matmul(core.bank(g)[:, 0:TT * width], w_T[:, g, :], v[:, :, g * width:(g + 1) * width],
                                 start=True, stop=True).then_inc(mixed_ready, 1)

        @block.vector
        def _(dve):
            nc.vector.tensor_tensor(v, v, gain_row.unsqueeze(1).broadcast_to([P, TT, D_GMLP]),
                                    ALU.mult).then_inc(gained, 1)
            for g in range(SGU_GROUPS):
                dve.wait_ge(mixed_ready, g + 1)
                nc.vector.scalar_tensor_tensor(
                    out=mixed[:, :, col + g * width:col + (g + 1) * width],
                    in0=core.bank(g)[:, 0:TT * width].rearrange("p (t w) -> p t w", t=TT),
                    scalar=bias_cols[:, g:g + 1],
                    in1=pr[:, :, U_COL + g * width:U_COL + (g + 1) * width],
                    op0=ALU.add, op1=ALU.mult).then_inc(gated, 1)


def branches_stage(core, outs, gates, row_valid, mixed):
    nc = core.nc
    with stage(nc, "valid_ready", "scaled", "summed") as (block, valid_ready, scaled, summed):
        def scale(engine, n):
            o = outs[n].rearrange("p t (h w) -> p t h w", h=Q_HEADS)
            g = gates[:, :, n:Q_HEADS * BRANCHES:BRANCHES].unsqueeze(3).broadcast_to([P, TT, Q_HEADS, DH])
            engine.tensor_tensor(o, o, g, ALU.mult).then_inc(scaled, 1)

        @block.gpsimd
        def _(pool):
            scale(nc.gpsimd, 2)

        @block.vector
        def _(dve):
            nc.vector.tensor_scalar(gates[:, 0, 0:Q_HEADS * BRANCHES:BRANCHES],
                                    gates[:, 0, 0:Q_HEADS * BRANCHES:BRANCHES], row_valid, None,
                                    ALU.mult).then_inc(valid_ready, 1)
            scale(nc.vector, 1)
            dve.wait_ge(valid_ready, 1)
            scale(nc.vector, 0)
            dve.wait_ge(scaled, 3)
            m = mixed[:, :, 0:D_Q]
            nc.vector.tensor_tensor(m, outs[0], outs[1], ALU.add).then_inc(summed, 1)
            dve.wait_ge(summed, 1)
            nc.vector.tensor_tensor(m, m, outs[2], ALU.add).then_inc(summed, 1)


def first_block(core, a, scratch_dram, ident, ones):
    nc = core.nc
    cols = core.const(2 * KD + SGU_GROUPS + CMP_BLOCK + 4)
    heads_cols = core.const(5)
    taps = core.const(3 * 2 * KF + 2 * KF)
    row_valid = core.const(1)
    kc_T = core.const(KV, CMP_N)
    kc = core.const(KV, DH)
    vc = core.const(KV, DH)
    PE_AT, B1_AT = 2 * KD + SGU_GROUPS, 2 * KD + SGU_GROUPS + CMP_BLOCK
    pr = core.work(0, TT, D_PROJ)
    at = TT * D_PROJ
    bias = core.work(at, Q_HEADS, T)
    kT = core.work(at + 8 * T, 2 * KV, T)
    scratch_at = at + 12 * T
    qT = core.ring(0, Q_HEADS, T)
    outs = [core.ring(8 * T + n * TT * D_Q, TT, D_Q) for n in range(BRANCHES)]
    mixed = core.cut(H_AT, TT, D)
    mixed_T = core.work(0, KD, T)

    rows = lambda v: v.rearrange("(k p) -> k p", p=P)
    pe_rows = lambda v: v.rearrange("(c a) d -> c (a d)", a=2)
    load_columns(core, 0, [rows(a["attn_norm"][0]), rows(a["ffn_norm"][0]), a["sgu_b"][0],
                           pe_rows(a["cmp_pe_k"][0]), pe_rows(a["cmp_pe_v"][0]),
                           rows(a["cmp_b1_k"][0]), rows(a["cmp_b1_v"][0])], cols, ident)
    load_columns(core, 0, [a[n] for n in ("q_norm", "k_norm_cmp", "k_norm_slc", "k_norm_win")], heads_cols,
                 ident, width=DH)
    load_columns(core, 0, [a["conv_w"][0].rearrange("w (f p) -> (w f) p", p=P), rows(a["conv_b"][0])], taps, ident)
    w_in = columns_of(a["w_in"][0])
    norm_stage(core, ones, cols[:, 0:KD], following=first_columns(w_in, D_PROJ))
    project(core, w_in, D_PROJ, pr, None, to_tokens=True, prepared=SPLIT)
    bias_stage(core, a, bias, scratch_dram, scratch_at)

    gates = pr[:, :, GATE_COL:GATE_COL + Q_HEADS * BRANCHES]
    activation_stage(core, [(pr[:, t, U_COL:U_COL + 2 * D_GMLP],) * 2 + (ACT.Gelu_apprx_tanh,) for t in range(TT)]
                     + [(gates, gates, ACT.Sigmoid)])
    by_head = lambda lo, heads, w: pr[:, :, lo:lo + heads * w].rearrange("p t (h w) -> p t h w", h=heads)
    head_norms(core, [by_head(Q_COL, Q_HEADS, DH), by_head(KS_COL, KV, DH), by_head(KW_COL, KV, DH),
                      by_head(V_COL, 1, D_GMLP)], scratch_at)

    w_sgu = core.work(scratch_at, SGU_GROUPS, P)
    w_T = core.work(scratch_at + SGU_GROUPS * P, SGU_GROUPS, P)
    gain_row = core.work(scratch_at + 2 * SGU_GROUPS * P, D_GMLP)
    keep = core.work(scratch_at + 2 * SGU_GROUPS * P + D_GMLP, P)
    load_stage(nc, [(w_sgu, a["sgu_w"][0].rearrange("g i j -> i g j")),
                    (gain_row, a["sgu_norm"][0].partition_broadcast(P)),
                    (keep, a["upper"]), (row_valid, a["row_valid"])])
    flip(core, [([w_sgu[:, g, :]], w_T[:, g, :], 1.0) for g in range(SGU_GROUPS)], ident)
    spatial_stage(core, pr, w_T, keep, gain_row, cols[:, 2 * KD:2 * KD + SGU_GROUPS], mixed, D_Q)

    pair_T = [core.work(scratch_at + KV * T * kind, KV, T) for kind in range(2)]
    jobs = []
    for kind, lo in enumerate((KC_COL, VC_COL)):
        for g in range(KV):
            src = [pr[:, t, lo + g * DH:lo + (g + 1) * DH] for t in range(TT)]
            jobs.append((src, pair_T[kind][0:DH, g, :], 1.0))
            jobs.append((src, pair_T[kind][DH:P, g, 0:T - 1], 1.0))
    flip(core, jobs, ident)
    compress_stage(core, a, pair_T, cols[:, PE_AT:PE_AT + CMP_BLOCK], cols[:, B1_AT:B1_AT + 4], [kc, vc], scratch_at + ATTEND_WORDS)
    head_norms(core, [kc[0:CMP_N].unsqueeze(1)], scratch_at)

    with stage(nc, "scaled") as (block, scaled):
        @block.vector
        def _(dve):
            nc.vector.tensor_scalar(heads_cols[0:DH, 4:5], heads_cols[0:DH, 0:1], DH ** -0.5, None,
                                    ALU.mult).then_inc(scaled, 1)
    jobs = [([pr[:, t, Q_COL + h * DH:Q_COL + (h + 1) * DH] for t in range(TT)], qT[0:DH, h, :],
             heads_cols[0:DH, 4:5]) for h in range(Q_HEADS)]
    for b, lo in enumerate((KS_COL, KW_COL)):
        jobs += [([pr[:, t, lo + g * DH:lo + (g + 1) * DH] for t in range(TT)], kT[0:DH, b * KV + g, :],
                  heads_cols[0:DH, 2 + b:3 + b]) for g in range(KV)]
    jobs += [([kc[0:CMP_N, g, :]], kc_T[0:DH, g, :], heads_cols[0:DH, 1:2]) for g in range(KV)]
    flip(core, jobs, ident)

    attend(core, WORK_AT + scratch_at, ident, KV, 2 * GROUP,
           q_of=lambda i, u: qT[0:DH, i * GROUP + u % GROUP, :],
           k_of=lambda i, u, n: kT[0:DH, i + u // GROUP * KV, 0:n],
           v_of=lambda i, u, kt, n: pr[0:n, kt, bass.ds((VS_COL, VW_COL)[u // GROUP] + i * DH, DH)],
           bias_of=lambda i, u, t, n: bias[:, i * GROUP + u % GROUP, T - P - P * t:T - P - P * t + n],
           out_of=lambda i, u, t: outs[1 + u // GROUP][:, t, bass.ds((i * GROUP + u % GROUP) * DH, DH)],
           width=DH, keys=lambda t: P * (t + 1))
    first_end = CMP_BLOCK - 1
    attend(core, WORK_AT + scratch_at, ident, KV, GROUP,
           q_of=lambda i, u: qT[0:DH, i * GROUP + u, :],
           k_of=lambda i, u, n: kc_T[0:DH, i, 0:n],
           v_of=lambda i, u, kt, n: vc[0:n, i, :],
           bias_of=lambda i, u, t, n: bias[:, i * GROUP + u, T - P - P * t + first_end:
                                           T - P - P * t + first_end + CMP_STRIDE * (n - 1) + 1:CMP_STRIDE],
           out_of=lambda i, u, t: outs[0][:, t, bass.ds((i * GROUP + u) * DH, DH)],
           width=DH, keys=lambda t: (P * (t + 1) - CMP_BLOCK) // CMP_STRIDE + 1)
    branches_stage(core, outs, gates, row_valid, mixed)

    flip(core, [([mixed[:, t, k * P:(k + 1) * P] for t in range(TT)], mixed_T[:, k, :], 1.0) for k in range(KD)], ident,
         following=first_rows(rows_of(a["w_out"][0])))
    rows_product(core, mixed_T, KD, rows_of(a["w_out"][0]), add_to_residual(core), prepared=LOADED)
    hidden = core.work(0, KF, T)
    up = columns_of(a["w_up"][0])
    gate = lambda k, lo, n, tiles: up(k, lo + D_FF, n, tiles)
    down = rows_of(a["w_down"][0])
    norm_stage(core, ones, cols[:, KD:2 * KD], following=first_gates(gate, up))
    gated_hidden(core, gate, up, hidden, conv=(taps[:, 0:6 * KF], 3, taps[:, 6 * KF:8 * KF]),
                 prepared=SPLIT, following=first_rows(down))
    rows_product(core, hidden, KF, down, add_to_residual(core), prepared=SPLIT)


LAYERS_2 = 2
A_HEADS, IDX_HEADS, IDX_DIM, B_HEADS = 8, 8, 32, 4
D_A = A_HEADS * DH
D_B = B_HEADS * 2 * DH
TOPK = min(256, T // 4)
QA_AT, KA_AT, VA_AT = 0, D_A, 2 * D_A
IQ_AT = 3 * D_A
IK_AT = IQ_AT + IDX_HEADS * IDX_DIM
IW_AT = IK_AT + IDX_DIM
QB_AT = IW_AT + IDX_HEADS
KB_AT = QB_AT + D_B
VB_AT = KB_AT + D_B
D_IN_2 = VB_AT + D_B
PICKED = -3e38


def rotate(engine, steps, x, cos, sin, tmp):
    heads, d = x.shape[1], x.shape[2]
    half = d // 2
    a, b = tmp[:, 0, 0:heads * d], tmp[:, 1, 0:heads * d]
    a = a.rearrange("p (h d) -> p h d", h=heads)
    b = b.rearrange("p (h d) -> p h d", h=heads)
    c = cos.unsqueeze(1).broadcast_to([P, heads, d])
    s = sin.unsqueeze(1).broadcast_to([P, heads, d])
    steps.step(engine.tensor_tensor(a, x, c, ALU.mult))
    steps.step(engine.tensor_tensor(b[:, :, 0:half], x[:, :, half:d], s[:, :, 0:half], ALU.mult))
    steps.link(engine.tensor_tensor(b[:, :, half:d], x[:, :, 0:half], s[:, :, half:d], ALU.mult))
    steps.link(engine.tensor_tensor(x, a, b, ALU.add))


def rope_stage(core, pr, tables, tmp_at):
    nc = core.nc
    cos64, sin64, cos32, sin32 = tables
    tmp_dve = core.cut(tmp_at, 2, 2 * D_A)
    tmp_pool = core.cut(tmp_at + 4 * D_A, 2, 2 * D_B)
    with stage(nc, "dve_steps", "pool_steps") as (block, dve_steps, pool_steps):
        @block.vector
        def _(dve):
            steps = Count(dve, dve_steps)
            for t in range(TT):
                x = pr[:, t, QA_AT:QA_AT + 2 * D_A].rearrange("p (h d) -> p h d", d=DH)
                rotate(nc.vector, steps, x, cos64[:, t, :], sin64[:, t, :], tmp_dve)
                x = pr[:, t, IQ_AT:IQ_AT + (IDX_HEADS + 1) * IDX_DIM].rearrange("p (h d) -> p h d", d=IDX_DIM)
                rotate(nc.vector, steps, x, cos32[:, t, :], sin32[:, t, :], tmp_dve)

        @block.gpsimd
        def _(pool):
            steps = Count(pool, pool_steps)
            for t in range(TT):
                x = pr[:, t, QB_AT:QB_AT + 2 * D_B].rearrange("p (h d) -> p h d", d=DH)
                rotate(nc.gpsimd, steps, x, cos64[:, t, :], sin64[:, t, :], tmp_pool)


def pick_stage(core, pr, iq, ik, picks, chunk_mask, scratch_at):
    nc = core.nc
    relu = core.cut(scratch_at, 2, T)
    scores = core.cut(scratch_at + 2 * T, 2, T)
    best = core.cut(scratch_at + 4 * T, 2, 8)
    iw = core.cut(scratch_at + 4 * T + 16, TT, IDX_HEADS)
    with stage(nc, "dotted", "relued", "weighed", "pick_steps") as (block, dotted, relued, weighed, pick_steps):
        @block.tensor
        def _(pe):
            for n in range((TT - 1) * IDX_HEADS):
                t, h, b = 1 + n // IDX_HEADS, n % IDX_HEADS, n % 4
                if n >= 4:
                    pe.wait_ge(relued, n - 3)
                nk = P * (t + 1)
                nc.tensor.matmul(core.bank(b)[:, 0:nk], iq[0:IDX_DIM, h, t * P:(t + 1) * P],
                                 ik[0:IDX_DIM, 0:nk], start=True, stop=True).then_inc(dotted, 1)

        @block.scalar
        def _(act):
            for n in range((TT - 1) * IDX_HEADS):
                t, b = 1 + n // IDX_HEADS, n % 4
                nk = P * (t + 1)
                act.wait_ge(dotted, n + 1)
                if n >= 2:
                    act.wait_ge(weighed, n - 1)
                nc.scalar.activation(relu[:, n % 2, 0:nk], core.bank(b)[:, 0:nk], ACT.Relu).then_inc(relued, 1)

        @block.vector
        def _(dve):
            steps = Count(dve, pick_steps)
            steps.step(nc.vector.tensor_scalar(iw, pr[:, :, IW_AT:IW_AT + IDX_HEADS],
                                               IDX_DIM ** -0.5 * IDX_HEADS ** -0.5, None, ALU.mult))
            steps.link(nc.vector.tensor_copy(picks[:, 0, 0:P], chunk_mask))
            for t in range(1, TT):
                nk = P * (t + 1)
                acc, work = scores[:, 0, 0:nk], scores[:, 1, 0:nk]
                for h in range(IDX_HEADS):
                    n = (t - 1) * IDX_HEADS + h
                    dve.wait_ge(relued, n + 1)
                    if h == 0:
                        nc.vector.tensor_scalar(acc, relu[:, n % 2, 0:nk], iw[:, t, h:h + 1], None,
                                                ALU.mult).then_inc(weighed, 1)
                    else:
                        nc.vector.scalar_tensor_tensor(out=acc, in0=relu[:, n % 2, 0:nk],
                                                       scalar=iw[:, t, h:h + 1], in1=acc,
                                                       op0=ALU.mult, op1=ALU.add).then_inc(weighed, 1)
                    dve.wait_ge(weighed, n + 1)
                last = acc[:, nk - P:nk]
                steps.link(nc.vector.tensor_tensor(last, last, chunk_mask, ALU.add))
                now, then = acc, work
                for r in range(TOPK // 8):
                    steps.link(nc.vector.max(best[:, r % 2, :], now))
                    steps.link(nc.vector.match_replace(then, best[:, r % 2, :], now, PICKED))
                    now, then = then, now
                steps.link(nc.vector.tensor_scalar(picks[:, t, 0:nk], now, PICKED / 2, NEG, ALU.is_gt, ALU.mult))


def difference_stage(core, ob, mixed, lam, lam_stats, scratch_at):
    nc = core.nc
    W = 2 * DH
    sq = core.cut(scratch_at, TT, B_HEADS * W)
    ms = core.cut(scratch_at + TT * B_HEADS * W, 3, TT * B_HEADS)
    lam_v, steps_words = lam, lam_stats
    with stage(nc, "steps_done", "mean_ready", "root_ready", "exponents", "exps") as (
            block, steps_done, mean_ready, root_ready, exponents, exps):
        @block.scalar
        def _(act):
            act.wait_ge(exponents, 2)
            nc.scalar.activation(steps_words[:, 2:4], steps_words[:, 0:2], ACT.Exp).then_inc(exps, 1)
            act.wait_ge(mean_ready, 1)
            nc.scalar.activation(ms[:, 1, :], ms[:, 0, :], ACT.Sqrt).then_inc(root_ready, 1)

        @block.vector
        def _(dve):
            steps = Count(dve, steps_done)
            for n in range(2):
                nc.vector.tensor_tensor_reduce(lam_v[:, 2 * n, :], lam_v[:, 2 * n, :], lam_v[:, 2 * n + 1, :],
                                               1.0, 0.0, ALU.mult, ALU.add,
                                               steps_words[:, n:n + 1]).then_inc(exponents, 1)
            dve.wait_ge(exps, 1)
            steps.link(nc.vector.tensor_tensor(steps_words[:, 4:5], steps_words[:, 3:4], steps_words[:, 2:3], ALU.subtract))
            steps.link(nc.vector.tensor_tensor(steps_words[:, 5:6], steps_words[:, 4:5], steps_words[:, 6:7], ALU.subtract))
            for t in range(TT):
                o = ob[:, t, :].rearrange("p (h c w) -> p h c w", h=B_HEADS, c=2)
                m = mixed[:, t, D_A:D_A + D_B].rearrange("p (h w) -> p h w", h=B_HEADS)
                steps.link(nc.vector.scalar_tensor_tensor(out=m, in0=o[:, :, 1, :], scalar=steps_words[:, 5:6],
                                                          in1=o[:, :, 0, :], op0=ALU.mult, op1=ALU.add))
                s = sq[:, t, :].rearrange("p (h w) -> p h w", h=B_HEADS)
                steps.link(nc.vector.tensor_tensor(s, m, m, ALU.mult))
                steps.link(nc.vector.tensor_reduce(ms[:, 0, t * B_HEADS:(t + 1) * B_HEADS], s, AX_X, ALU.add))
            nc.vector.tensor_scalar(ms[:, 0, :], ms[:, 0, :], 1.0 / W, EPS, ALU.mult, ALU.add).then_inc(mean_ready, 1)
            dve.wait_ge(root_ready, 1)
            steps.link(nc.vector.reciprocal(ms[:, 2, :], ms[:, 1, :]))
            for t in range(TT):
                m = mixed[:, t, D_A:D_A + D_B].rearrange("p (h w) -> p h w", h=B_HEADS)
                r = ms[:, 2, t * B_HEADS:(t + 1) * B_HEADS].unsqueeze(2).broadcast_to([P, B_HEADS, W])
                steps.step(nc.vector.tensor_tensor(m, m, r, ALU.mult))


def swiglu(core, gate_w, up_w, down_w):
    hidden = core.work(0, KF, T)
    gated_hidden(core, gate_w, up_w, hidden, prepared=SPLIT, following=first_rows(down_w))
    rows_product(core, hidden, KF, down_w, add_to_residual(core), prepared=SPLIT)


def columns_of(w):
    w = w.rearrange("(k p) n -> p k n", p=P)
    return lambda k, lo, n, tiles=KD // 2: w[:, k:k + tiles, bass.ds(lo, n)]


def rows_of(w):
    w = w.rearrange("(k p) n -> p k n", p=P)
    return lambda k: w[:, bass.ds(k, 2), :]


def second_block(core, a, tables, chunk_mask, ident, ones):
    nc = core.nc
    pr = core.work(0, TT, D_IN_2)
    picks = core.work(TT * D_IN_2, TT, T)
    scratch_at = WORK_AT + TT * D_IN_2 + TT * T
    qT, kT = core.ring(0, A_HEADS, T), core.ring(8 * T, A_HEADS, T)
    mixed = core.cut(H_AT, TT, D)
    ob = core.cut(H_AT + TT * D, TT, B_HEADS * 4 * DH)
    mixed_T = core.work(0, KD, T)
    cols = core.const(2 * KD + 1)
    lam = core.const(4, DH)
    lam_words = core.const(8)
    sub_gain = core.const(1)
    one_minus = core.const(1)

    with nc.Fori(0, LAYERS_2) as layer:
        row = lambda v, n: v[layer].rearrange("(k p) -> k p", k=n)
        load_columns(core, 0, [row(a["g_mix_2"], KD), row(a["g_ffn_2"], KD), row(a["g_subln_2"], 1)], cols, ident)
        everywhere = lambda v: v.partition_broadcast(P)
        load_stage(nc, [(lam[:, n, :], everywhere(a[name][layer])) for n, name in
                        enumerate(["lam_q1_2", "lam_k1_2", "lam_q2_2", "lam_k2_2"])]
                   + [(lam_words[:, 6:8], everywhere(a["lam_init"][layer]))])
        w_in = columns_of(a["w_in_2"][layer])
        norm_stage(core, ones, cols[:, 0:KD], following=first_columns(w_in, D_IN_2))
        project(core, w_in, D_IN_2, pr, None, to_tokens=True, prepared=SPLIT)
        rope_stage(core, pr, tables, RING_AT)

        def turned(lo, n, width, dst, scale=1.0):
            return [([pr[:, t, lo + width * h:lo + width * (h + 1)] for t in range(TT)],
                     dst[0:width, h, :], scale) for h in range(n)]
        flip(core, turned(IQ_AT, IDX_HEADS, IDX_DIM, qT) + turned(IK_AT, 1, IDX_DIM, kT), ident)
        pick_stage(core, pr, qT, kT[:, 0, :], picks, chunk_mask, scratch_at)
        flip(core, turned(QA_AT, A_HEADS, DH, qT, DH ** -0.5) + turned(KA_AT, A_HEADS, DH, kT), ident)
        U = 4
        attend(core, scratch_at, ident, A_HEADS // U, U,
               q_of=lambda i, u: qT[0:DH, i * U + u, :],
               k_of=lambda i, u, n: kT[0:DH, i * U + u, 0:n],
               v_of=lambda i, u, kt, n: pr[0:n, kt, bass.ds(VA_AT + (i * U + u) * DH, DH)],
               bias_of=lambda i, u, t, n: picks[:, t, 0:n],
               out_of=lambda i, u, t: mixed[:, t, bass.ds((i * U + u) * DH, DH)],
               width=DH, keys=lambda t: P * (t + 1))

        flip(core, turned(QB_AT, 2 * B_HEADS, DH, qT, DH ** -0.5) + turned(KB_AT, 2 * B_HEADS, DH, kT), ident)
        load_bias(core, picks, chunk_mask)
        attend(core, scratch_at, ident, 2 * B_HEADS // U, U,
               q_of=lambda i, u: qT[0:DH, i * U + u, :],
               k_of=lambda i, u, n: kT[0:DH, i * U + u, 0:n],
               v_of=lambda i, u, kt, n: pr[0:n, kt, bass.ds(VB_AT + (i * (U // 2) + u // 2) * 2 * DH, 2 * DH)],
               bias_of=lambda i, u, t, n: picks[:, t, 0:n],
               out_of=lambda i, u, t: ob[:, t, bass.ds((i * U + u) * 2 * DH, 2 * DH)],
               width=2 * DH, keys=lambda t: P * (t + 1))
        difference_stage(core, ob, mixed, lam, lam_words, RING_AT)
        with stage(nc, "gain_ready") as (block, gain_ready):
            @block.vector
            def _(dve):
                nc.vector.tensor_tensor(sub_gain, cols[:, 2 * KD:2 * KD + 1], lam_words[:, 7:8],
                                        ALU.mult).then_inc(gain_ready, 1)
        flip(core, [([mixed[:, t, k * P:(k + 1) * P] for t in range(TT)], mixed_T[:, k, :],
                     1.0 if k < D_A // P else sub_gain) for k in range(KD)], ident,
             following=first_rows(rows_of(a["w_out_2"][layer])))
        rows_product(core, mixed_T, KD, rows_of(a["w_out_2"][layer]), add_to_residual(core), prepared=LOADED)
        gate, up = columns_of(a["w_gate_2"][layer]), columns_of(a["w_up_2"][layer])
        norm_stage(core, ones, cols[:, KD:2 * KD], following=first_gates(gate, up))
        swiglu(core, gate, up, rows_of(a["w_down_2"][layer]))
    load_columns(core, 0, [a["g_final_2"].rearrange("(k p) -> k p", p=P)], cols[:, 0:KD], ident)
    norm_stage(core, ones, cols[:, 0:KD], out=core.x)


def load_bias(core, picks, chunk_mask):
    nc = core.nc
    with stage(nc, "cleared", "masked") as (block, cleared, masked):
        @block.gpsimd
        def _(pool):
            for t in range(1, TT):
                nc.gpsimd.memset(picks[:, t, 0:t * P], 0.0).then_inc(cleared, 1)

        @block.vector
        def _(dve):
            for t in range(TT):
                nc.vector.tensor_copy(picks[:, t, t * P:(t + 1) * P], chunk_mask).then_inc(masked, 1)


S_HEADS, S_GROUPS, S_STATE = 16, 2, 128
S_INNER = S_HEADS * DH
G_HEADS, G_DIM = 8, 128
Z_COL = 0
XBC_COL = Z_COL + S_INNER
XBC = S_INNER + 2 * S_GROUPS * S_STATE
DT_COL = XBC_COL + XBC
QKV_COL = DT_COL + S_HEADS
QKV = 3 * G_HEADS * G_DIM
GZ_COL = QKV_COL + QKV
AB_COL = GZ_COL + G_HEADS * G_DIM
GATE_S_COL = AB_COL + 2 * G_HEADS
GATE_G_COL = GATE_S_COL + D
ROWS = 40
G_ROW = 32
SPANS = [(sum(T - P * m for m in range(j)), T - P * j) for j in range(TT)]
SPAN_WORDS = sum(w for _, w in SPANS)
LOG_TERMS = 8


def small_projections(core, w, small):
    nc = core.nc
    n = S_HEADS
    weights = core.ring(0, KD, 2 * n)
    with stage(nc, "weights_in", "projected", "stored") as (block, weights_in, projected, stored):
        @block.sync
        def _(sp):
            for c, col in enumerate((DT_COL, AB_COL)):
                sp.dma_start(weights[:, :, c * n:(c + 1) * n], w[:, :, col:col + n]).then_inc(weights_in, 16)

        @block.tensor
        def _(pe):
            pe.wait_ge(weights_in, 32)
            for t in range(TT):
                for k in range(KD):
                    for h in (core.h_hi, core.h_lo):
                        mm = nc.tensor.matmul(core.bank(t)[:, 0:2 * n], h[:, k, t * P:(t + 1) * P].bitcast(F32),
                                              weights[:, k, :], start=(k == 0 and h is core.h_hi),
                                              stop=(k == KD - 1 and h is core.h_lo))
                mm.then_inc(projected, 1)

        @block.vector
        def _(dve):
            for t in range(TT):
                dve.wait_ge(projected, t + 1)
                nc.vector.tensor_copy(small[:, t, :], core.bank(t)[:, 0:2 * n]).then_inc(stored, 1)


def decay_stage(core, raw, beta_raw, bias_col, log_col, steps_row, sums, delta_rows, at):
    nc = core.nc
    neg, e, z, z2, series, one = (core.work(at + T * n, T)[0:ROWS] for n in range(6))
    with stage(nc, "decay_steps", "ready", "exp_done", "coefficient", "beta_done") as (
            block, decay_steps, ready, exp_done, coefficient, beta_done):
        @block.scalar
        def _(act):
            nc.scalar.activation(log_col, log_col, ACT.Exp).then_inc(coefficient, 1)
            act.wait_ge(ready, 1)
            nc.scalar.activation(e, neg, ACT.Exp).then_inc(exp_done, 1)
            nc.scalar.activation(delta_rows[:, 1, :], beta_raw, ACT.Sigmoid).then_inc(beta_done, 1)

        @block.vector
        def _(dve):
            v = nc.vector
            s = Count(dve, decay_steps)
            s.step(v.memset(one, 1.0))
            s.link(v.tensor_scalar(raw, raw, bias_col, None, ALU.add))
            s.link(v.tensor_scalar(neg, raw, -1.0, None, ALU.mult))
            s.link(v.tensor_tensor(neg, neg, raw, ALU.min))
            v.tensor_scalar(raw, raw, 0.0, None, ALU.max).then_inc(ready, 1)
            dve.wait_ge(exp_done, 1)
            dve.wait_ge(ready, 1)
            s.link(v.tensor_scalar(z2, e, 2.0, None, ALU.add))
            s.link(v.reciprocal(neg, z2))
            s.link(v.tensor_tensor(z, e, neg, ALU.mult))
            s.link(v.tensor_tensor(z2, z, z, ALU.mult))
            s.link(v.tensor_scalar(series, z2, 1.0 / (2 * LOG_TERMS + 1), None, ALU.mult))
            for k in range(LOG_TERMS - 1, 0, -1):
                s.link(v.scalar_tensor_tensor(out=series, in0=series, scalar=1.0 / (2 * k + 1), in1=z2,
                                              op0=ALU.add, op1=ALU.mult))
            s.link(v.scalar_tensor_tensor(out=series, in0=series, scalar=1.0, in1=z, op0=ALU.add, op1=ALU.mult))
            s.link(v.scalar_tensor_tensor(out=steps_row, in0=series, scalar=2.0, in1=raw, op0=ALU.mult, op1=ALU.add))
            dve.wait_ge(coefficient, 1)
            s.link(v.tensor_scalar(neg, steps_row, log_col, -1.0, ALU.mult, ALU.mult))
            for j, (lo, w) in enumerate(SPANS):
                s.step(v.tensor_tensor_scan(sums[:, lo:lo + w], one[:, 0:w], neg[:, T - w:T], 0.0,
                                            ALU.mult, ALU.add))
            s.settle()
            for j, (lo, w) in enumerate(SPANS):
                s.step(v.tensor_copy(delta_rows[:, 0, j * P:(j + 1) * P], sums[G_ROW:G_ROW + G_HEADS, lo:lo + P]))


def ssd_stage(core, ones, pick, b_T, c_T, xs, xdt, sums, sums_tok, d_skip, keep, y, at, following):
    nc = core.nc
    gram = core.work(at, S_GROUPS, SPAN_WORDS)
    decay = core.ring(2 * UNIT, 2, SPAN_WORDS)
    one_row = core.ring(2 * UNIT + 2 * SPAN_WORDS, 2, SPAN_WORDS)[0:S_HEADS]
    per_group = S_HEADS // S_GROUPS
    with stage(nc, "gram_ready", "gram_stored", "gram_masked") as (block, gram_ready, gram_stored, gram_masked):
        @block.tensor
        def _(pe):
            for g in range(S_GROUPS):
                for j, (lo, w) in enumerate(SPANS):
                    nc.tensor.matmul(core.bank(g * TT + j)[:, 0:w], b_T[:, g, j * P:(j + 1) * P],
                                     c_T[:, g, j * P:T], start=True, stop=True).then_inc(gram_ready, 1)

        @block.vector
        def _(dve):
            for g in range(S_GROUPS):
                for j, (lo, w) in enumerate(SPANS):
                    dve.wait_ge(gram_ready, g * TT + j + 1)
                    if w > P:
                        nc.vector.tensor_copy(gram[:, g, lo + P:lo + w], core.bank(g * TT + j)[:, P:w]
                                              ).then_inc(gram_stored, 1)
                    nc.vector.tensor_tensor(gram[:, g, lo:lo + P], core.bank(g * TT + j)[:, 0:P], keep,
                                            ALU.mult).then_inc(gram_masked, 1)

    with stage(nc, "row_ready", "spread", "spread_read", "decayed", "weighted", "output", "output_stored", "following_in",
               from_one=("spread", "spread_read", "output", "output_stored")) as (
            block, row_ready, spread, spread_read, decayed, weighted, output, output_stored, following_in):
        bodies = S_HEADS // 2

        @block.sync
        def _(sp):
            for half, (rows, src) in enumerate(following):
                sp.dma_start(core.raw(half, rows)[:, :, 0:src.shape[2]], src).then_inc(following_in, 16)
            sp.wait_ge(following_in, 32)

        @block.gpsimd
        def _(pool):
            with pool.Fori(0, bodies) as i:
                for u in range(2):
                    hold(pool, spread, TT * (2 * i + u) + 1)
                    own = pick[0:S_HEADS, bass.ds(2 * i + u, 1)].broadcast_to([S_HEADS, SPAN_WORDS])
                    nc.gpsimd.tensor_tensor(one_row[:, u, :], sums[0:S_HEADS, :], own, ALU.mult).then_inc(row_ready, 1)

        @block.tensor
        def _(pe):
            with pe.Fori(0, bodies) as i:
                for u in range(2):
                    h = 2 * i + u
                    pe.wait_ge(row_ready, h + 1)
                    pe.wait_ge(spread_read, TT * h + 1)
                    for j, (lo, w) in enumerate(SPANS):
                        nc.tensor.matmul(core.bank(j)[:, 0:w], ones[0:S_HEADS, :], one_row[:, u, lo:lo + w],
                                         start=True, stop=True).then_inc(spread, 1)
                for u in range(2):
                    h = 2 * i + u
                    pe.wait_ge(weighted, h + 1)
                    pe.wait_ge(output_stored, 2 * i + 1)
                    for t in range(TT):
                        for j in range(t + 1):
                            at_j = SPANS[j][0] + (t - j) * P
                            mm = nc.tensor.matmul(core.bank(4 + u)[:, t * DH:(t + 1) * DH],
                                                  decay[:, u, at_j:at_j + P], xdt[:, j, bass.ds(h * DH, DH)],
                                                  start=(j == 0), stop=(j == t))
                    mm.then_inc(output, 1)

        @block.scalar
        def _(act):
            with act.Fori(0, bodies) as i:
                for u in range(2):
                    h = 2 * i + u
                    act.wait_ge(output, 2 * i + 1)
                    for j, (lo, w) in enumerate(SPANS):
                        hold(act, spread, TT * h + j + 2)
                        nc.scalar.activation(decay[:, u, lo:lo + w], core.bank(j)[:, 0:w], ACT.Relu, scale=-1.0,
                                             bias=sums_tok[:, j, bass.ds(h, 1)]).then_inc(spread_read, 1)
                    act.wait_ge(spread_read, TT * h + TT + 1)
                    nc.scalar.activation(decay[:, u, :], decay[:, u, :], ACT.Exp, scale=-1.0).then_inc(decayed, 1)

        @block.vector
        def _(dve):
            with dve.Fori(0, bodies) as i:
                for u in range(2):
                    h = 2 * i + u
                    dve.wait_ge(decayed, h + 1)
                    nc.vector.tensor_tensor(decay[:, u, :], decay[:, u, :], gram[:, i // (per_group // 2), :],
                                            ALU.mult).then_inc(weighted, 1)
                for u in range(2):
                    h = 2 * i + u
                    dve.wait_ge(output, h + 2)
                    nc.vector.scalar_tensor_tensor(
                        out=y[:, :, bass.ds(h * DH, DH)], in0=xs[:, :, bass.ds(h * DH, DH)],
                        scalar=d_skip[:, bass.ds(h, 1)],
                        in1=core.bank(4 + u)[:, 0:TT * DH].rearrange("p (t d) -> p t d", t=TT),
                        op0=ALU.mult, op1=ALU.add).then_inc(output_stored, 1)


def multiply_stage(core, jobs):
    nc = core.nc
    with stage(nc, "multiplied") as (block, multiplied):
        @block.vector
        def _(dve):
            for out, a, b in jobs:
                nc.vector.tensor_tensor(out, a, b, ALU.mult).then_inc(multiplied, 1)


def unit_stage(core, ones, x, n, queries, at):
    nc = core.nc
    sq = core.ring(0, 2, T)
    root = core.ring(2 * T, 4, T)
    with stage(nc, "squared", "summed", "mean_ready", "root_ready", "inverted", "scaled") as (
            block, squared, summed, mean_ready, root_ready, inverted, scaled):
        @block.gpsimd
        def _(pool):
            for m in range(n):
                if m >= 2:
                    pool.wait_ge(summed, m - 1)
                nc.gpsimd.tensor_tensor(sq[:, m % 2, :], x[:, m, :], x[:, m, :], ALU.mult).then_inc(squared, 1)

        @block.tensor
        def _(pe):
            for m in range(n):
                pe.wait_ge(squared, m + 1)
                if m >= 4:
                    pe.wait_ge(mean_ready, m - 3)
                nc.tensor.matmul(core.bank(m % 4), ones, sq[:, m % 2, :], start=True, stop=True).then_inc(summed, 1)

        @block.scalar
        def _(act):
            for m in range(n):
                r = root[:, m % 4, :]
                act.wait_ge(mean_ready, m + 1)
                nc.scalar.activation(r, r, ACT.Sqrt).then_inc(root_ready, 1)

        @block.vector
        def _(dve):
            def scale(m):
                r = root[:, m % 4, :]
                dve.wait_ge(root_ready, m + 1)
                nc.vector.reciprocal(r, r).then_inc(inverted, 1)
                dve.wait_ge(inverted, m + 1)
                factor = G_DIM ** -0.5 if m < queries else 1.0
                nc.vector.scalar_tensor_tensor(out=x[:, m, :], in0=x[:, m, :], scalar=factor, in1=r,
                                               op0=ALU.mult, op1=ALU.mult).then_inc(scaled, 1)
            for m in range(n):
                dve.wait_ge(summed, m + 1)
                if m >= 4:
                    dve.wait_ge(scaled, m - 3)
                nc.vector.tensor_scalar(root[:, m % 4, :], core.bank(m % 4), EPS, None, ALU.add).then_inc(mean_ready, 1)
                if m >= 2:
                    scale(m - 2)
            scale(n - 2)
            scale(n - 1)


def delta_prepare(core, ones, pick, q_T, k_T, delta_rows, sums_tok, keep, couple_T, attn_T, last_sum, last_decay):
    nc = core.nc
    one_row = core.ring(0, 2, 2 * T)[0:G_HEADS]
    kb = core.ring(4 * T, 2, T)
    dec = core.ring(6 * T, 2, T)
    eg = core.ring(8 * T, 2, T)
    k_static = core.ring(10 * T, 2, T)
    with stage(nc, "row_ready", "spread", "sums_read", "exp_ready", "keys_scaled", "products", "differences", "decay_ready",
               "decay_kept", "used", "lasts", from_one=("spread", "used", "products")) as (
            block, row_ready, spread, sums_read, exp_ready, keys_scaled, products, differences, decay_ready, decay_kept, used, lasts):
        bodies = G_HEADS // 2

        @block.gpsimd
        def _(pool):
            with pool.Fori(0, bodies) as i:
                for u in range(2):
                    h = 2 * i + u
                    hold(pool, spread, 4 * i + 1)
                    own = pick[0:G_HEADS, bass.ds(h, 1)].broadcast_to([G_HEADS, 2 * T])
                    nc.gpsimd.tensor_tensor(one_row[:, u, :], delta_rows.rearrange("p a b -> p (a b)"), own,
                                            ALU.mult).then_inc(row_ready, 1)
                for u in range(2):
                    h = 2 * i + u
                    pool.wait_ge(decay_ready, h + 1)
                    d = dec[:, u, :].rearrange("p (t i) -> p t i", t=TT)
                    nc.gpsimd.tensor_tensor(d, d, keep.unsqueeze(1).broadcast_to([P, TT, P]), ALU.mult).then_inc(decay_kept, 1)

        @block.tensor
        def _(pe):
            with pe.Fori(0, bodies) as i:
                for u in range(2):
                    h = 2 * i + u
                    pe.wait_ge(row_ready, h + 1)
                    pe.wait_ge(used, 6 * i + 1)
                    for c in range(2):
                        nc.tensor.matmul(core.bank(4 * u + c), ones[0:G_HEADS, :], one_row[:, u, c * T:(c + 1) * T],
                                         start=True, stop=True).then_inc(spread, 1)
                for u in range(2):
                    h = 2 * i + u
                    pe.wait_ge(keys_scaled, 2 * h + 2)
                    for c in range(2):
                        for t in range(TT):
                            s = slice(t * P, (t + 1) * P)
                            mm = nc.tensor.matmul(core.bank(4 * u + 2 + c)[:, s], k_static[:, u, s],
                                                  q_T[:, h, s] if c else kb[:, u, s], start=True, stop=True)
                        mm.then_inc(products, 1)

        @block.scalar
        def _(act):
            with act.Fori(0, bodies) as i:
                for u in range(2):
                    h = 2 * i + u
                    act.wait_ge(spread, 4 * i + 2 * u + 2)
                    hold(act, used, 6 * i + 1)
                    for t in range(TT):
                        nc.scalar.activation(dec[:, u, t * P:(t + 1) * P], core.bank(4 * u)[:, t * P:(t + 1) * P],
                                             ACT.Relu, scale=-1.0, bias=sums_tok[:, t, bass.ds(G_ROW + h, 1)]
                                             ).then_inc(differences, 1)
                    act.wait_ge(differences, TT * h + TT)
                    nc.scalar.activation(dec[:, u, :], dec[:, u, :], ACT.Exp, scale=-1.0).then_inc(decay_ready, 1)
                    nc.scalar.copy(last_sum[:, h, :], core.bank(4 * u)[:, P - 1:T:P]).then_inc(exp_ready, 1)
                    nc.scalar.activation(eg[:, u, :], core.bank(4 * u), ACT.Exp).then_inc(exp_ready, 1)

        @block.vector
        def _(dve):
            with dve.Fori(0, bodies) as i:
                for u in range(2):
                    h = 2 * i + u
                    dve.wait_ge(spread, 4 * i + 2 * u + 3)
                    dve.wait_ge(products, 4 * i + 1)
                    nc.vector.tensor_tensor(kb[:, u, :], k_T[:, h, :], core.bank(4 * u + 1), ALU.mult).then_inc(keys_scaled, 1)
                    nc.vector.tensor_copy(k_static[:, u, :], k_T[:, h, :]).then_inc(keys_scaled, 1)
                for u in range(2):
                    h = 2 * i + u
                    dve.wait_ge(decay_kept, h + 1)
                    dve.wait_ge(products, 2 * h + 2)
                    nc.vector.tensor_tensor(couple_T[:, h, :], dec[:, u, :], core.bank(4 * u + 2), ALU.mult).then_inc(used, 1)
                    dve.wait_ge(products, 2 * h + 3)
                    nc.vector.tensor_tensor(attn_T[:, h, :], dec[:, u, :], core.bank(4 * u + 3), ALU.mult).then_inc(used, 1)
                    dve.wait_ge(exp_ready, 2 * h + 2)
                    nc.vector.tensor_copy(last_decay[:, h, :], eg[:, u, P - 1:T:P]).then_inc(lasts, 1)
                    nc.vector.tensor_tensor(q_T[:, h, :], q_T[:, h, :], eg[:, u, :], ALU.mult).then_inc(used, 1)


def delta_solve(core, ident, level_masks, couple_T, inverse_T):
    nc = core.nc
    levels = level_masks.shape[1]
    inv = core.ring(0, 2, T)
    inv_T = core.ring(2 * T, 2, T)
    join = core.ring(4 * T, 4, T)
    part = core.ring(8 * T, 2, T)
    with stage(nc, "begun", "joined", "part_ready", "part_stored", "updates", "updated", from_one=("part_ready",)) as (
            block, begun, joined, part_ready, part_stored, updates, updated):
        bodies = G_HEADS // 2

        @block.gpsimd
        def _(pool):
            with pool.Fori(0, bodies) as i:
                for n in range(2 * levels):
                    l, u = n // 2, n % 2
                    hold(pool, part_ready, 2 * levels * i + max(n - 3, 0) + 1)
                    h = 2 * i + u
                    e = join[:, 2 * u + l % 2, :].rearrange("p (t i) -> p t i", t=TT)
                    nc.gpsimd.tensor_tensor(e, couple_T[:, h, :].rearrange("p (t i) -> p t i", t=TT),
                                            level_masks[:, l, :].unsqueeze(1).broadcast_to([P, TT, P]),
                                            ALU.mult).then_inc(joined, 1)

        @block.tensor
        def _(pe):
            def product(bank, left, right):
                for t in range(TT):
                    s = slice(t * P, (t + 1) * P)
                    mm = nc.tensor.matmul(core.bank(bank)[:, s], left[:, s], right[:, s], start=True, stop=True)
                return mm
            with pe.Fori(0, bodies) as i:
                base = 2 * levels * i
                for l in range(levels):
                    for u in range(2):
                        n = 2 * l + u
                        pe.wait_ge(joined, base + n + 1)
                        if l == 0:
                            pe.wait_ge(begun, 4 * i + 2 * u + 2)
                        else:
                            pe.wait_ge(updated, 2 * (base + n - 1))
                        product(4 * u, join[:, 2 * u + l % 2, :], inv[:, u, :]).then_inc(part_ready, 1)
                    for u in range(2):
                        n = 2 * l + u
                        pe.wait_ge(part_stored, base + n + 1)
                        product(4 * u + 1, inv_T[:, u, :], part[:, u, :]).then_inc(updates, 1)
                        product(4 * u + 2, part[:, u, :], inv_T[:, u, :]).then_inc(updates, 1)

        @block.scalar
        def _(act):
            with act.Fori(0, bodies) as i:
                base = 2 * levels * i
                for n in range(2 * levels):
                    u = n % 2
                    act.wait_ge(part_ready, base + n + 2)
                    nc.scalar.copy(part[:, u, :], core.bank(4 * u)).then_inc(part_stored, 1)

        @block.vector
        def _(dve):
            eye = ident.unsqueeze(1).broadcast_to([P, TT, P])
            with dve.Fori(0, bodies) as i:
                base = 2 * levels * i
                for u in range(2):
                    for m in (inv, inv_T):
                        nc.vector.tensor_copy(m[:, u, :].rearrange("p (t i) -> p t i", t=TT), eye).then_inc(begun, 1)
                for l in range(levels):
                    for u in range(2):
                        n = 2 * l + u
                        dve.wait_ge(updates, 2 * (base + n) + 2)
                        if l == 0:
                            dve.wait_ge(begun, 4 * i + 4)
                        else:
                            dve.wait_ge(updated, 2 * (base + n - 1))
                        nc.vector.tensor_tensor(inv[:, u, :], inv[:, u, :], core.bank(4 * u + 1),
                                                ALU.subtract).then_inc(updated, 1)
                        to = inverse_T[:, 2 * i + u, :] if l == levels - 1 else inv_T[:, u, :]
                        nc.vector.tensor_tensor(to, inv_T[:, u, :], core.bank(4 * u + 2), ALU.subtract).then_inc(updated, 1)
                dve.wait_ge(updated, 2 * (base + 2 * levels))


def delta_inputs(core, k_tok, v_tok, beta_tok, sums_tok, last_sum, inverse_T, minus_w_T, tail_k):
    nc = core.nc
    k_in = core.ring(0, TT, D)
    factor = core.ring(TT * D, 3, TT * G_HEADS)
    heads = lambda x: x.rearrange("p t (h d) -> p t h d", h=G_HEADS)
    wide = lambda f: f.rearrange("p (t h) -> p t h", t=TT).unsqueeze(3).broadcast_to([P, TT, G_HEADS, G_DIM])
    with stage(nc, "exp_sum", "rest", "exp_rest", "input_ready", "factor_ready", "scaled", "w_ready", "w_stored") as (
            block, exp_sum, rest, exp_rest, input_ready, factor_ready, scaled, w_ready, w_stored):
        f = lambda n: factor[:, n, :].rearrange("p (t h) -> p t h", t=TT)
        gsum = sums_tok[:, :, G_ROW:G_ROW + G_HEADS]

        @block.scalar
        def _(act):
            nc.scalar.activation(f(0), gsum, ACT.Exp).then_inc(exp_sum, 1)
            act.wait_ge(rest, 1)
            nc.scalar.activation(f(1), f(1), ACT.Exp).then_inc(exp_rest, 1)
            for h in range(G_HEADS):
                act.wait_ge(w_ready, h + 1)
                nc.scalar.activation(minus_w_T[:, h, :], core.bank(h), ACT.Copy, scale=-1.0).then_inc(w_stored, 1)

        @block.vector
        def _(dve):
            nc.vector.tensor_tensor(f(1), last_sum.rearrange("p h t -> p t h"), gsum, ALU.subtract).then_inc(rest, 1)
            dve.wait_ge(exp_sum, 1)
            nc.vector.tensor_tensor(f(2), f(0), beta_tok, ALU.mult).then_inc(factor_ready, 1)
            dve.wait_ge(factor_ready, 1)
            nc.vector.tensor_tensor(heads(k_in), heads(k_tok), wide(factor[:, 2, :]), ALU.mult).then_inc(input_ready, 1)
            nc.vector.tensor_tensor(heads(v_tok), heads(v_tok),
                                    beta_tok.unsqueeze(3).broadcast_to([P, TT, G_HEADS, G_DIM]),
                                    ALU.mult).then_inc(scaled, 1)

        @block.gpsimd
        def _(pool):
            pool.wait_ge(exp_rest, 1)
            nc.gpsimd.tensor_tensor(heads(tail_k), heads(k_tok), wide(factor[:, 1, :]), ALU.mult).then_inc(scaled, 1)

        @block.tensor
        def _(pe):
            pe.wait_ge(input_ready, 1)
            for h in range(G_HEADS):
                for t in range(TT):
                    mm = nc.tensor.matmul(core.bank(h)[:, t * P:(t + 1) * P], k_in[:, t, h * G_DIM:(h + 1) * G_DIM],
                                          inverse_T[:, h, t * P:(t + 1) * P], start=True, stop=True)
                mm.then_inc(w_ready, 1)


def delta_scan(core, q_T, v_tok, tail_k, inverse_T, minus_w_T, attn_T, last_decay, out):
    nc = core.nc
    state = core.ring(0, G_HEADS, G_DIM)
    fresh = core.ring(G_HEADS * G_DIM, 2, G_DIM)
    with stage(nc, "cleared", "fresh_ready", "fresh_stored", "out_ready", "step_ready", "out_stored", "state_ready") as (
            block, cleared, fresh_ready, fresh_stored, out_ready, step_ready, out_stored, state_ready):
        order = [(t, h) for t in range(TT) for h in range(G_HEADS)]

        @block.gpsimd
        def _(pool):
            nc.gpsimd.memset(state, 0.0).then_inc(cleared, 1)

        @block.tensor
        def _(pe):
            pe.wait_ge(cleared, 1)

            def finish(n):
                t, h = order[n]
                s = slice(t * P, (t + 1) * P)
                pe.wait_ge(fresh_stored, n + 1)
                if n >= 2:
                    pe.wait_ge(out_stored, n - 1)
                    pe.wait_ge(state_ready, n - 1)
                b = core.bank(2 + n % 2)[:, 0:G_DIM]
                nc.tensor.matmul(b, q_T[:, h, s], state[:, h, :], start=True, stop=False)
                nc.tensor.matmul(b, attn_T[:, h, s], fresh[:, n % 2, :], start=False, stop=True).then_inc(out_ready, 1)
                nc.tensor.matmul(core.bank(4 + n % 2)[:, 0:G_DIM], tail_k[:, t, h * G_DIM:(h + 1) * G_DIM],
                                 fresh[:, n % 2, :], start=True, stop=True).then_inc(step_ready, 1)

            for n, (t, h) in enumerate(order):
                s = slice(t * P, (t + 1) * P)
                if n >= 2:
                    pe.wait_ge(fresh_stored, n - 1)
                if n >= G_HEADS:
                    pe.wait_ge(state_ready, n - G_HEADS + 1)
                b = core.bank(n % 2)[:, 0:G_DIM]
                nc.tensor.matmul(b, inverse_T[:, h, s], v_tok[:, t, h * G_DIM:(h + 1) * G_DIM], start=True, stop=False)
                nc.tensor.matmul(b, minus_w_T[:, h, s], state[:, h, :], start=False, stop=True).then_inc(fresh_ready, 1)
                if n:
                    finish(n - 1)
            finish(len(order) - 1)

        @block.scalar
        def _(act):
            for n in range(len(order)):
                act.wait_ge(fresh_ready, n + 1)
                if n >= 2:
                    act.wait_ge(step_ready, n - 1)
                nc.scalar.copy(fresh[:, n % 2, :], core.bank(n % 2)[:, 0:G_DIM]).then_inc(fresh_stored, 1)

        @block.vector
        def _(dve):
            for n, (t, h) in enumerate(order):
                dve.wait_ge(step_ready, n + 1)
                dve.wait_ge(out_ready, n + 1)
                nc.vector.scalar_tensor_tensor(out=state[:, h, :], in0=state[:, h, :],
                                               scalar=last_decay[:, h, t:t + 1],
                                               in1=core.bank(4 + n % 2)[:, 0:G_DIM],
                                               op0=ALU.mult, op1=ALU.add).then_inc(state_ready, 1)
                nc.vector.tensor_copy(out[:, t, h * G_DIM:(h + 1) * G_DIM], core.bank(2 + n % 2)[:, 0:G_DIM]
                                      ).then_inc(out_stored, 1)


def third_block(core, a, ident, ones):
    nc = core.nc
    KX, KQ = XBC // P, QKV // P
    cols = core.const(4 * KD + 1)
    conv_s = core.const(CONV_K * KX + KX)
    conv_g = core.const(CONV_K * KQ + KQ)
    keep = core.const(P)
    masks = core.const(7, P)
    d_skip = core.const(S_HEADS)
    bias_col, log_col = core.const(1)[0:ROWS], core.const(1)[0:ROWS]
    sums_tok = core.const(TT, ROWS)
    steps_tok = core.const(TT, S_HEADS)
    beta_tok = core.const(TT, G_HEADS)
    last_sum, last_decay = core.const(G_HEADS, TT), core.const(G_HEADS, TT)
    w_in = columns_of(a["w_in_3"][0])
    section = lambda col: lambda k, lo, n: w_in(k, lo + col, n)
    rows = lambda v: v.rearrange("(k p) -> k p", p=P)
    load_columns(core, 0, [rows(a["norm_mix_w_3"][0]), rows(a["ssm_norm_w_3"][0]), rows(a["norm_ffn_w_3"][0]),
                           rows(a["final_norm_w_3"]), a["gdn_norm_w_3"]], cols, ident)
    load_columns(core, 0, [a["ssm_conv_w_3"][0].rearrange("w (f p) -> (w f) p", p=P), rows(a["ssm_conv_b_3"][0])],
                 conv_s, ident)
    load_columns(core, 0, [a["gdn_conv_w_3"][0].rearrange("w (f p) -> (w f) p", p=P)], conv_g[:, 0:CONV_K * KQ], ident)
    with stage(nc, "cleared") as (block, cleared):
        @block.gpsimd
        def _(pool):
            nc.gpsimd.memset(conv_g[:, CONV_K * KQ:(CONV_K + 1) * KQ], 0.0).then_inc(cleared, 1)
            nc.gpsimd.memset(bias_col, 0.0).then_inc(cleared, 1)
            nc.gpsimd.memset(log_col, 0.0).then_inc(cleared, 1)
    column = lambda v: v.unsqueeze(1)
    load_stage(nc, [(keep, a["upper"]), (masks, a["levels"].rearrange("l p i -> p l i")),
                    (d_skip, a["ssm_d_3"][0].partition_broadcast(P)),
                    (bias_col[0:S_HEADS], column(a["ssm_dt_bias_3"][0])),
                    (bias_col[G_ROW:G_ROW + G_HEADS], column(a["gdn_dt_bias_3"][0])),
                    (log_col[0:S_HEADS], column(a["ssm_a_log_3"][0])),
                    (log_col[G_ROW:G_ROW + G_HEADS], column(a["gdn_a_log_3"][0]))])
    norm_stage(core, ones, cols[:, 0:KD])

    merged = core.work(0, KD, T)
    small = core.work(4096, TT, 2 * S_HEADS)
    delta_rows = core.work(24576, 2, T)[0:G_HEADS]
    raw, steps_row = core.work(8192, T)[0:ROWS], core.work(8192 + T, T)[0:ROWS]
    beta_raw = core.work(8192 + 2 * T, T)[0:G_HEADS]
    sums = core.work(18432 + 2 * SPAN_WORDS, SPAN_WORDS)[0:ROWS]
    small_projections(core, a["w_in_3"][0].rearrange("(k p) n -> p k n", p=P), small)
    with stage(nc, "cleared") as (block, cleared):
        @block.gpsimd
        def _(pool):
            nc.gpsimd.memset(raw, 0.0).then_inc(cleared, 1)
    flip(core, [([small[:, t, lo:lo + n] for t in range(TT)], dst, 1.0) for lo, n, dst in (
        (0, S_HEADS, raw[0:S_HEADS, :]), (S_HEADS, G_HEADS, raw[G_ROW:G_ROW + G_HEADS, :]),
        (S_HEADS + G_HEADS, G_HEADS, beta_raw))], ident)
    decay_stage(core, raw, beta_raw, bias_col, log_col, steps_row, sums, delta_rows, 8192 + 3 * T)
    flip(core, [([sums[:, lo:lo + P] for lo, _ in SPANS], sums_tok.rearrange("p t h -> p (t h)"), 1.0),
                ([steps_row[0:S_HEADS, t * P:(t + 1) * P] for t in range(TT)],
                 steps_tok.rearrange("p t h -> p (t h)"), 1.0),
                ([delta_rows[:, 1, t * P:(t + 1) * P] for t in range(TT)],
                 beta_tok.rearrange("p t h -> p (t h)"), 1.0)], ident,
         following=first_columns(section(XBC_COL), XBC))

    xbc = core.work(0, KX, T)
    xs, xdt = core.work(6144, TT, S_INNER), core.work(10240, TT, S_INNER)
    y = core.work(14336, TT, S_INNER)
    project(core, section(XBC_COL), XBC, xbc, ACT.Silu,
            conv=(conv_s[:, 0:CONV_K * KX], conv_s[:, CONV_K * KX:(CONV_K + 1) * KX]), prepared=LOADED)
    flip(core, [([xbc[:, 4 * g + k, t * P:(t + 1) * P] for k in range(4)], xs[:, t, g * 4 * P:(g + 1) * 4 * P], 1.0)
                for t in range(TT) for g in range(2)], ident)
    by_head = lambda v: v.rearrange("p t (h d) -> p t h d", h=S_HEADS)
    multiply_stage(core, [(by_head(xdt)[:, t], by_head(xs)[:, t],
                           steps_tok[:, t, :].unsqueeze(2).broadcast_to([P, S_HEADS, DH])) for t in range(TT)])
    ssd_stage(core, ones, ident, xbc[:, 8:10, :], xbc[:, 10:12, :], xs, xdt, sums, sums_tok, d_skip, keep, y, 18432,
              first_columns(section(Z_COL), S_INNER))
    z = core.work(0, TT, S_INNER)
    project(core, section(Z_COL), S_INNER, z, ACT.Silu, to_tokens=True, prepared=LOADED)
    multiply_stage(core, [(y[:, t], y[:, t], z[:, t]) for t in range(TT)])
    head_norms(core, [y.rearrange("p t (g w) -> p t g w", g=S_GROUPS)], 18432, TT * S_INNER)
    y_T = core.work(4096, KD, T)
    flip(core, [([y[:, t, k * P:(k + 1) * P] for t in range(TT)], y_T[:, k, :], cols[:, KD + k:KD + k + 1])
                for k in range(KD)], ident, following=first_columns(section(GATE_S_COL), D))
    gate = core.work(8192, KD, T)
    w_proj_s, w_proj_g, w_out = (rows_of(a[n][0]) for n in ("w_proj_ssm_3", "w_proj_gdn_3", "w_out_3"))
    project(core, section(GATE_S_COL), D, gate, ACT.Sigmoid, prepared=LOADED, following=first_rows(w_proj_s))
    rows_product(core, y_T, KD, w_proj_s,
                 lambda m: nc.vector.tensor_tensor(merged[:, m, :], gate[:, m, :], core.bank(m), ALU.mult),
                 prepared=SPLIT, following=first_columns(section(QKV_COL), QKV))

    qkv = core.work(4096, KQ, T)
    q_T, k_T, v_T = (qkv[:, n * G_HEADS:(n + 1) * G_HEADS, :] for n in range(3))
    k_tok, v_tok = core.work(16384, TT, D), core.work(20480, TT, D)
    couple_T, attn_T = core.cut(H_AT, G_HEADS, T), core.cut(H_AT + G_HEADS * T, G_HEADS, T)
    project(core, section(QKV_COL), QKV, qkv, ACT.Silu,
            conv=(conv_g[:, 0:CONV_K * KQ], conv_g[:, CONV_K * KQ:(CONV_K + 1) * KQ]), prepared=SPLIT)
    unit_stage(core, ones, qkv, 2 * G_HEADS, G_HEADS, 0)
    flip(core, [([src[:, 4 * g + k, t * P:(t + 1) * P] for k in range(4)], dst[:, t, g * 4 * P:(g + 1) * 4 * P], 1.0)
                for src, dst in ((k_T, k_tok), (v_T, v_tok)) for t in range(TT) for g in range(2)], ident)
    delta_prepare(core, ones, ident, q_T, k_T, delta_rows, sums_tok, keep, couple_T, attn_T, last_sum, last_decay)
    inverse_T = v_T
    delta_solve(core, ident, masks, couple_T, inverse_T)
    minus_w_T, tail_k = k_T, core.cut(H_AT, TT, D)
    delta_inputs(core, k_tok, v_tok, beta_tok, sums_tok, last_sum, inverse_T, minus_w_T, tail_k)
    o = k_tok
    delta_scan(core, q_T, v_tok, tail_k, inverse_T, minus_w_T, attn_T, last_decay, o)
    norm_stage(core, ones, cols[:, 0:KD], following=first_columns(section(GZ_COL), D))
    gz = core.work(20480, TT, D)
    project(core, section(GZ_COL), D, gz, ACT.Silu, to_tokens=True, prepared=SPLIT)
    head_norms(core, [o.rearrange("p t (h d) -> p t h d", h=G_HEADS)], 8192, TT * D)
    multiply_stage(core, [(o[:, t], o[:, t], gz[:, t]) for t in range(TT)])
    o_T = core.work(4096, KD, T)
    flip(core, [([o[:, t, k * P:(k + 1) * P] for t in range(TT)], o_T[:, k, :], cols[:, 4 * KD:4 * KD + 1])
                for k in range(KD)], ident, following=first_columns(section(GATE_G_COL), D))
    project(core, section(GATE_G_COL), D, gate, ACT.Sigmoid, prepared=LOADED, following=first_rows(w_proj_g))
    rows_product(core, o_T, KD, w_proj_g,
                 lambda m: nc.vector.tensor_tensor(gate[:, m, :], gate[:, m, :], core.bank(m), ALU.mult),
                 prepared=SPLIT, following=first_rows(w_out))
    with stage(nc, "added") as (block, added):
        @block.vector
        def _(dve):
            for m in range(KD):
                nc.vector.tensor_tensor(merged[:, m, :], merged[:, m, :], gate[:, m, :], ALU.add).then_inc(added, 1)
    rows_product(core, merged, KD, w_out, add_to_residual(core), prepared=SPLIT)
    ffn = columns_of(a["w_ffn_in_3"][0])
    up = lambda k, lo, n, tiles: ffn(k, lo + D_FF, n, tiles)
    norm_stage(core, ones, cols[:, 2 * KD:3 * KD], following=first_gates(ffn, up))
    swiglu(core, ffn, up, rows_of(a["w_ffn_down_3"][0]))
    norm_stage(core, ones, cols[:, 3 * KD:4 * KD], out=core.x)


def shape_constants():
    pos = np.arange(T, dtype=np.float32)

    def rope(dim):
        inv = np.float32(10000.0) ** (-np.arange(0, dim, 2, dtype=np.float32) / np.float32(dim))
        ang = pos[:, None] * inv[None, :].astype(np.float32)
        c, s = np.cos(ang), np.sin(ang)
        return np.concatenate([c, c], 1), np.concatenate([-s, s], 1)

    def tiles(m):
        return m.reshape(TT, P, -1).transpose(1, 0, 2).reshape(P, -1)

    c64, s64 = rope(64)
    c32, s32 = rope(32)
    dist = T - 1 - np.arange(BIAS_ROW)
    exact = REL_BUCKETS // 2
    d = np.maximum(dist, 1).astype(np.float32)
    log_b = exact + (np.log(d / np.float32(exact)) / np.float32(math.log(REL_MAX_DIST / exact))
                     * np.float32(REL_BUCKETS - exact)).astype(np.int32)
    bucket = np.where(dist < exact, dist, np.clip(log_b, exact, REL_BUCKETS - 1))
    bucket = np.where(dist < 0, REL_BUCKETS, bucket)
    q = np.arange(P)[:, None]
    k = np.arange(P)[None, :]
    chunk = np.where(k // 64 <= q // 64, 0.0, NEG)
    out = {
        "ident": np.eye(P), "ones": np.ones((P, P)), "chunk_mask": chunk,
        "cos64": tiles(c64), "sin64": tiles(s64), "cos32": tiles(c32), "sin32": tiles(s32),
        "buckets": bucket[None, :] == np.arange(REL_BUCKETS + 1)[:, None],
        "levels": np.stack([(q // (2 * b) == k // (2 * b)) & (q // b % 2 == 0) & (k // b % 2 == 1)
                            for b in (1, 2, 4, 8, 16, 32, 64)]),
        "reversed": np.eye(P)[::-1], "upper": q <= k, "row_valid": q >= CMP_BLOCK - 1,
        "lam_init": np.array([[0.8 - 0.6 * math.exp(-0.3 * n), 1.0 - (0.8 - 0.6 * math.exp(-0.3 * n))]
                              for n in range(2)]),
    }
    return {n: np.ascontiguousarray(v, dtype=np.float32) for n, v in out.items()}


def common_constants(core, a):
    names = ["ident", "ones", "chunk_mask", "cos64", "sin64", "cos32", "sin32"]
    views = {n: core.const(a[n].shape[1]) for n in names}
    load_stage(core.nc, [(views[n], a[n]) for n in names])
    tables = [views[n].rearrange("p (t d) -> p t d", t=TT) for n in names[3:]]
    return views["ident"], views["ones"], views["chunk_mask"], tables


def build(nc, a, bias_rows, out):
    core = Core(nc)
    ident, ones, chunk_mask, tables = common_constants(core, a)
    resident = core.const_used
    load_input(core, a["x"][0], ident)
    first_block(core, a, bias_rows, ident, ones)
    core.const_used = resident
    second_block(core, a, tables, chunk_mask, ident, ones)
    core.const_used = CONST_AT + 2 * P
    third_block(core, a, ident, ones)
    store_output(core, core.x, out[0], ident)


def kernel(**inputs):
    import concourse.bacc as bacc
    from concourse.bass_utils import run_bass_kernel_spmd

    nc = bacc.Bacc("TRN2", target_bir_lowering=False, num_devices=1)
    arrays, views = {}, {}
    for name, value in {**inputs, **shape_constants()}.items():
        array = np.ascontiguousarray(value)
        arrays[f"in_{name}"] = array
        views[name] = nc.dram_tensor(f"in_{name}", array.shape, F32, kind="ExternalInput").ap()
    bias_rows = nc.dram_tensor("bias_rows", (Q_HEADS, BIAS_ROW), F32).ap()
    out = nc.dram_tensor("out_0", (1, T, D), F32, kind="ExternalOutput").ap()
    build(nc, views, bias_rows, out)
    result = run_bass_kernel_spmd(nc, [arrays], core_ids=[0])
    return result.results[0]["out_0"]
```

```python
import math
from contextlib import ExitStack, contextmanager

import numpy as np

import concourse.bass as bass
from concourse import mybir
from concourse.alu_op_type import AluOpType as ALU

F32 = mybir.dt.float32
ACT = mybir.ActivationFunctionType
AX_X = mybir.AxisListType.X

P = 128
T = 512
TT = T // P
D = 1024
KD = D // P
BANK = 512
BANKS = 8
D_FF = 2816
KF = D_FF // P
CONV_K = 4
EPS = 1e-6
NEG = -1e30


F32R = mybir.dt.float32r
UNIT = 2048
X_AT = 0
H_AT = X_AT + KD * T
RING_AT = H_AT + 2 * KD * T
RING_WORDS = 6 * UNIT
CONST_AT = RING_AT + RING_WORDS
CONST_WORDS = 2000
WORK_AT = CONST_AT + CONST_WORDS
ARENA = 52176
WORK_WORDS = ARENA - WORK_AT
SOURCE_AT = 16384


class Core:

    def __init__(self, nc):
        self.nc = nc
        start = -(-nc.sbuf_base // 32) * 32
        self.regions = []
        for name, at, end in (("residual", X_AT, H_AT), ("normed", H_AT, RING_AT), ("ring", RING_AT, CONST_AT),
                              ("constants", CONST_AT, WORK_AT), ("work", WORK_AT, ARENA)):
            tensor = nc.alloc_sbuf_tensor_at(name, [P, end - at], F32, offset=start + 4 * at)
            self.regions.append((tensor, at, end))

        def over(name, at, *dims):
            tensor = nc.alloc_sbuf_tensor_at(name, [P, *dims], F32R, offset=start + 4 * at)
            return tensor[tuple([slice(None)] * (1 + len(dims)))]

        self.psum = nc.alloc_psum_tensor("psum", [P, BANKS, BANK], F32)
        self.x = self.cut(X_AT, KD, T)
        self.h_hi, self.h_lo = over("h_hi", H_AT, KD, T), over("h_lo", H_AT + KD * T, KD, T)
        self.w_hi, self.w_lo = over("w_hi", RING_AT + 2 * UNIT, 2, UNIT), over("w_lo", RING_AT + 4 * UNIT, 2, UNIT)
        self.s_hi = over("s_hi", WORK_AT + SOURCE_AT, 2, 2, T)
        self.s_lo = over("s_lo", WORK_AT + SOURCE_AT + 4 * T, 2, 2, T)
        self.const_used = CONST_AT

    def cut(self, at, *dims):
        n = int(np.prod(dims))
        tensor, first = next((r, a) for r, a, end in self.regions if a <= at and at + n <= end)
        v = tensor[:, at - first:at - first + n]
        if len(dims) == 2:
            v = v.rearrange("p (a b) -> p a b", a=dims[0])
        elif len(dims) == 3:
            v = v.rearrange("p (a b c) -> p a b c", a=dims[0], b=dims[1])
        return v

    def work(self, at, *dims):
        return self.cut(WORK_AT + at, *dims)

    def ring(self, at, *dims):
        assert at + int(np.prod(dims)) <= RING_WORDS
        return self.cut(RING_AT + at, *dims)

    def const(self, *dims):
        at = self.const_used
        self.const_used += int(np.prod(dims))
        assert self.const_used <= WORK_AT
        return self.cut(at, *dims)

    def raw(self, half, a):
        return self.cut(RING_AT + half * UNIT, a, UNIT // a)

    def bank(self, b):
        return self.psum[:, b, :]


@contextmanager
def stage(nc, *names, starts={}, from_one=()):
    mark = nc.get_next_instruction_name()
    sems = [nc.alloc_semaphore(f"{n}_{mark}") for n in names]
    for n, value in {**dict.fromkeys(from_one, 1), **starts}.items():
        if value:
            nc.sync.sem_inc(sems[names.index(n)], value)
    with nc.Block() as block:
        yield (block, *sems)
    nc.clear_and_free_semaphores(sems)
    nc.all_engine_barrier()


class Count:

    def __init__(self, engine, sem, base=0):
        self.engine, self.sem, self.base, self.n = engine, sem, base, 0

    def step(self, ins):
        self.n += 1
        ins.then_inc(self.sem, 1)

    def settle(self):
        self.engine.wait_ge(self.sem, self.base + self.n)

    def link(self, ins):
        self.step(ins)
        self.settle()


def hold(engine, sem, value):
    engine.wait_ge(sem, value)
    engine.nop(nofuse=True)


def pairs(n):
    return n // 2, n % 2


def norm_stage(core, ones, gain, out=None, following=None):
    nc, x = core.nc, core.x
    sq = core.cut(H_AT + KD * T, KD, T)
    rstd = core.ring(5 * UNIT, 2, T)
    warm_word = core.ring(5 * UNIT + 2 * T, 1)
    whole = sq if out is None else out
    total = core.bank(0)
    pool_rests = (1, 3, 5) if out is None else ()
    with stage(nc, *UNIT_SEMS, "squared_act", "squared_dve", "summed", "warm", "mean_ready", "root_ready",
               "inverted", "normed", "rounded", "rests", starts=UNIT_STARTS) as (block, *sems):
        squared_act, squared_dve, summed, warm, mean_ready, root_ready, inverted, normed, rounded, rests = sems[8:]

        def rest(engine, k):
            engine.wait_ge(rounded, k + 1)
            engine.tensor_tensor(core.h_lo[:, k, :], whole[:, k, :], core.h_hi[:, k, :].bitcast(F32),
                                 ALU.subtract).then_inc(rests, 1)

        @block.sync
        def _(sp):
            load_following(core, sp, sems, following, (0, 0))

        @block.scalar
        def _(act):
            for k in range(0, KD, 2):
                nc.scalar.activation(sq[:, k, :], x[:, k, :], ACT.Square).then_inc(squared_act, 1)
            nc.scalar.activation(warm_word, ones[:, 0:1], ACT.Sqrt).then_inc(warm, 1)
            round_following(core, act, sems, following, 0, 1)
            act.wait_ge(mean_ready, 1)
            nc.scalar.activation(rstd[:, 1, :], rstd[:, 0, :], ACT.Sqrt).then_inc(root_ready, 1)
            for k in range(KD if out is None else 0):
                act.wait_ge(normed, k + 1)
                nc.scalar.activation(core.h_hi[:, k, :], whole[:, k, :], ACT.Copy).then_inc(rounded, 1)

        @block.tensor
        def _(pe):
            for k in range(KD):
                pe.wait_ge((squared_act, squared_dve)[k % 2], k // 2 + 1)
                mm = nc.tensor.matmul(total, ones, sq[:, k, :], start=(k == 0), stop=(k == KD - 1))
            mm.then_inc(summed, 1)

        @block.gpsimd
        def _(pool):
            for k in pool_rests:
                rest(pool, k)

        @block.vector
        def _(dve):
            for k in range(1, KD, 2):
                nc.vector.tensor_tensor(sq[:, k, :], x[:, k, :], x[:, k, :], ALU.mult).then_inc(squared_dve, 1)
            rest_following(core, dve, sems, following, 0)
            dve.wait_ge(summed, 1)
            nc.vector.tensor_scalar(rstd[:, 0, :], total, 1.0 / D, EPS, ALU.mult, ALU.add).then_inc(mean_ready, 1)
            dve.wait_ge(root_ready, 1)
            nc.vector.reciprocal(rstd[:, 0, :], rstd[:, 1, :]).then_inc(inverted, 1)
            dve.wait_ge(inverted, 1)
            for k in range(KD):
                nc.vector.scalar_tensor_tensor(out=whole[:, k, :], in0=x[:, k, :], scalar=gain[:, k:k + 1],
                                               in1=rstd[:, 0, :], op0=ALU.mult, op1=ALU.mult).then_inc(normed, 1)
                if out is None and k >= 1 and k - 1 not in pool_rests:
                    rest(dve, k - 1)
            if out is None:
                rest(dve, KD - 1)


UNIT_SEMS = ("loaded0", "loaded1", "rounded0", "rounded1", "split0", "split1", "used0", "used1")
UNIT_STARTS = {"split0": 1, "split1": 1, "used0": 1, "used1": 1}


def load_unit(core, sp, sems, c, half, a, src):
    loaded, split = sems[0:2], sems[4:6]
    hold(sp, split[half], c + 1)
    sp.dma_start(core.raw(half, a)[:, :, 0:src.shape[2]], src).then_inc(loaded[half], 16)


def round_unit(core, act, sems, c, half, per, a=1, n=UNIT):
    loaded, rounded, used = sems[0:2], sems[2:4], sems[6:8]
    act.wait_ge(loaded[half], 16 * c + 16)
    act.wait_ge(used[half], per * c + 1)
    hi = core.w_hi[:, half, :].rearrange("p (a b) -> p a b", a=a)[:, :, 0:n]
    core.nc.scalar.activation(hi, core.raw(half, a)[:, :, 0:n], ACT.Copy).then_inc(rounded[half], 1)


def rest_unit(core, dve, sems, c, half, a=1, n=UNIT):
    rounded, split = sems[2:4], sems[4:6]
    dve.wait_ge(rounded[half], c + 1)
    hi, lo = (w[:, half, :].rearrange("p (a b) -> p a b", a=a)[:, :, 0:n] for w in (core.w_hi, core.w_lo))
    core.nc.vector.tensor_tensor(lo, core.raw(half, a)[:, :, 0:n], hi.bitcast(F32), ALU.subtract
                                 ).then_inc(split[half], 1)


def load_following(core, sp, sems, following, done):
    for half, (a, src) in enumerate(following or ()):
        load_unit(core, sp, sems, done[half], half, a, src)
    for half in range(2 if following else 0):
        sp.wait_ge(sems[half], 16 * done[half] + 16)


def round_following(core, act, sems, following, done, per):
    if following:
        a, src = following[0]
        round_unit(core, act, sems, done, 0, per, a, src.shape[2])


def rest_following(core, dve, sems, following, done):
    if following:
        a, src = following[0]
        rest_unit(core, dve, sems, done, 0, a, src.shape[2])


def first_columns(weight, cols):
    return [(KD // 2, weight(half * KD // 2, 0, min(cols, BANK))) for half in range(2)]


def first_rows(weight):
    return [(2, weight(2 * half)) for half in range(2)]


LOADED, SPLIT = 1, 2


def prepared_starts(prepared):
    starts = dict(UNIT_STARTS)
    if prepared:
        starts.update(loaded0=16, loaded1=16)
    if prepared == SPLIT:
        starts.update(rounded0=1, split0=2)
    return starts


def walk_loads(sp, n, load, prepared):
    if prepared:
        walk(sp, n - 1, lambda c, j: load(c + 1, j))
    else:
        walk(sp, n, load)


def unsplit(c, prepared):
    return range(1 if isinstance(c, int) and c == 0 and prepared == SPLIT else 0, 2)


def walk(engine, n, visit, ahead=None):
    bodies = max(n - 2, 0) // 2
    if ahead:
        ahead(0)
    if bodies:
        with engine.Fori(0, bodies) as i:
            for j in range(2):
                if ahead:
                    ahead(2 * i + j + 1)
                visit(2 * i + j, j)
    for c in range(2 * bodies, n):
        if ahead:
            ahead(c + 1)
        visit(c, c % 2)


def three_passes(nc, bank, left, right, start, stop):
    (l_hi, l_lo), (r_hi, r_lo) = left, right
    nc.tensor.matmul(bank, l_hi, r_hi, start=start, stop=False)
    nc.tensor.matmul(bank, l_hi, r_lo, start=False, stop=False)
    return nc.tensor.matmul(bank, l_lo, r_hi, start=False, stop=stop)


def seen(core, half, a, k, lo, hi):
    b = UNIT // a
    return [w[:, half, k * b + lo:k * b + hi] for w in (core.w_hi, core.w_lo)]


def project(core, weight, cols, dst, func, conv=None, to_tokens=False, prepared=0, following=None):
    nc = core.nc
    chunks = -(-cols // BANK)
    tiles = cols // P
    KH = KD // 2

    def width(c):
        return cols - c * BANK if isinstance(c, int) and c == chunks - 1 else BANK

    with stage(nc, *UNIT_SEMS, "based", "convolved", "conv_steps", "stored",
               starts={**prepared_starts(prepared), "stored": 5}) as (block, *sems):
        used = sems[6:8]
        based, convolved, conv_steps, stored = sems[8:12]

        @block.sync
        def _(sp):
            def load(c, j):
                for half in range(2):
                    load_unit(core, sp, sems, c, half, KH, weight(half * KH, c * BANK, width(c)))
            walk_loads(sp, chunks, load, prepared)
            load_following(core, sp, sems, following, (chunks, chunks))

        @block.tensor
        def _(pe):
            def multiply(c, j):
                n = width(c)
                pe.wait_ge(stored, 4 * c + 1)
                for half in range(2):
                    pe.wait_ge(sems[4 + half], c + 2)
                    for m in range(4):
                        s = slice(m * P, (m + 1) * P)
                        for k in range(KH):
                            f = half * KH + k
                            ends = dict(start=(f == 0), stop=(f == KD - 1))
                            if to_tokens:
                                mm = three_passes(nc, core.bank(4 * j + m)[:, 0:n],
                                                  (core.h_hi[:, f, s], core.h_lo[:, f, s]),
                                                  seen(core, half, KH, k, 0, n), **ends)
                            else:
                                mm = three_passes(nc, core.bank(4 * j + m), seen(core, half, KH, k, m * P, (m + 1) * P),
                                                  (core.h_hi[:, f, :], core.h_lo[:, f, :]), **ends)
                        if half or m == 3:
                            mm.then_inc(used[half], 1)
            walk(pe, chunks, multiply)

        @block.scalar
        def _(act):
            def ahead(c):
                if isinstance(c, int) and c == chunks:
                    round_following(core, act, sems, following, c, 1)
                    return
                for half in unsplit(c, prepared):
                    round_unit(core, act, sems, c, half, (1, 4)[half], KH, width(c))

            def finish(c, j):
                n = width(c)
                for m in range(4 if func is not None else 0):
                    hold(act, used[1], 4 * c + m + 2)
                    to = dst[:, m, bass.ds(c * BANK, n)] if to_tokens else dst[:, 4 * c + m, :]
                    bank = core.bank(4 * j + m)[:, 0:n]
                    if conv is None:
                        nc.scalar.activation(to, bank, func).then_inc(stored, 1)
                    else:
                        tap = conv[0][:, bass.ds((CONV_K - 1) * tiles + 4 * c + m, 1)]
                        nc.scalar.activation(to, bank, ACT.Identity, scale=tap,
                                             bias=conv[1][:, bass.ds(4 * c + m, 1)]).then_inc(based, 1)
                for m in range(4 if conv else 0):
                    hold(act, convolved, 4 * c + m + 1)
                    to = dst[:, 4 * c + m, :]
                    nc.scalar.activation(to, to, func).then_inc(stored, 1)
            walk(act, chunks, finish, ahead)

        @block.vector
        def _(dve):
            def ahead(c):
                if isinstance(c, int) and c == chunks:
                    rest_following(core, dve, sems, following, c)
                    return
                for half in unsplit(c, prepared):
                    rest_unit(core, dve, sems, c, half, KH, width(c))

            def finish(c, j):
                n = width(c)
                for m in range(4 if func is None else 0):
                    dve.wait_ge(used[1], 4 * c + m + 2)
                    nc.vector.tensor_copy(dst[:, m, bass.ds(c * BANK, n)], core.bank(4 * j + m)[:, 0:n]
                                          ).then_inc(stored, 1)
                for m in range(4 if conv else 0):
                    t = 4 * c + m
                    dve.wait_ge(based, t + 1)
                    for back in range(1, CONV_K):
                        ins = nc.vector.scalar_tensor_tensor(
                            out=dst[:, t, back:T], in0=core.bank(4 * j + m)[:, 0:T - back],
                            scalar=conv[0][:, bass.ds((CONV_K - 1 - back) * tiles + t, 1)],
                            in1=dst[:, t, back:T], op0=ALU.mult, op1=ALU.add)
                        if back < CONV_K - 1:
                            ins.then_inc(conv_steps, 1)
                            dve.wait_ge(conv_steps, (CONV_K - 2) * t + back)
                    ins.then_inc(convolved, 1)
            walk(dve, chunks, finish, ahead)


def rows_product(core, src, tiles, weight, finish, prepared=0, following=None):
    nc = core.nc
    units = tiles // 2
    chunks = -(-units // 2)
    assert units % 2 == 0 or following is None

    def halves(c):
        return range(1 if isinstance(c, int) and 2 * c + 1 == units else 2)

    with stage(nc, *UNIT_SEMS, "source_rounded", "banks_full", "finished",
               starts={**prepared_starts(prepared), "split0": 1}) as (block, *sems):
        used = sems[6:8]
        source_rounded, banks_full, finished = sems[8:11]

        @block.sync
        def _(sp):
            def load(c, j):
                for half in halves(c):
                    load_unit(core, sp, sems, c, half, 2, weight(4 * c + 2 * half))
            walk_loads(sp, chunks, load, prepared)
            load_following(core, sp, sems, following, (chunks, chunks))

        @block.tensor
        def _(pe):
            def multiply(c, j):
                for half in halves(c):
                    last = isinstance(c, int) and 2 * c + half == units - 1
                    pe.wait_ge(sems[4 + half], c + 2)
                    for a in range(2):
                        for m in range(KD):
                            mm = three_passes(nc, core.bank(m), seen(core, half, 2, a, m * P, (m + 1) * P),
                                              (core.s_hi[:, half, a, :], core.s_lo[:, half, a, :]),
                                              start=(isinstance(c, int) and c + half + a == 0), stop=(last and a == 1))
                            if last and a == 1:
                                mm.then_inc(banks_full, 1)
                    if not last:
                        mm.then_inc(used[half], 1)
            multiply(0, 0)
            if chunks > 2:
                with pe.Fori(1, chunks - 1) as c:
                    multiply(c, 0)
            multiply(chunks - 1, 0)

        @block.scalar
        def _(act):
            def split(c, j):
                for half in halves(c):
                    hold(act, used[half], c + 1)
                    nc.scalar.activation(core.s_hi[:, half, :, :], src[:, bass.ds(4 * c + 2 * half, 2), :],
                                         ACT.Copy).then_inc(source_rounded, 1)
                    if half in unsplit(c, prepared):
                        round_unit(core, act, sems, c, half, 1)
            split(0, 0)
            walk(act, chunks - 1, lambda c, j: split(c + 1, j))
            round_following(core, act, sems, following, chunks, 1)

        @block.vector
        def _(dve):
            def split(c, j):
                for half in halves(c):
                    dve.wait_ge(source_rounded, 2 * c + half + 1)
                    source_rest = nc.vector.tensor_tensor(
                        core.s_lo[:, half, :, :], src[:, bass.ds(4 * c + 2 * half, 2), :],
                        core.s_hi[:, half, :, :].bitcast(F32), ALU.subtract)
                    if half in unsplit(c, prepared):
                        rest_unit(core, dve, sems, c, half)
                    else:
                        source_rest.then_inc(sems[4], 1)
            split(0, 0)
            walk(dve, chunks - 1, lambda c, j: split(c + 1, j))
            rest_following(core, dve, sems, following, chunks)
            for m in range(KD):
                dve.wait_ge(banks_full, m + 1)
                finish(m).then_inc(finished, 1)


def add_to_residual(core):
    def finish(m):
        return core.nc.vector.tensor_tensor(core.x[:, m, :], core.x[:, m, :], core.bank(m), ALU.add)
    return finish


CHUNK_COLS = UNIT // KD
FF_CHUNKS = D_FF // CHUNK_COLS
CT = CHUNK_COLS // P


def first_gates(gate_w, up_w):
    return [(KD, w(0, 0, CHUNK_COLS, KD)) for w in (gate_w, up_w)]


def gated_hidden(core, gate_w, up_w, hidden, conv=None, prepared=0, following=None):
    nc = core.nc
    scratch = core.work(KF * T, 4 * CT, T)
    taps, width, bias = conv if conv else (None, 0, None)
    with stage(nc, *UNIT_SEMS, "silus", "made", "biased", "convolved", "conv_steps",
               starts={**prepared_starts(prepared), "made": CT + 1}) as (block, *sems):
        used = sems[6:8]
        silus, made, biased, convolved, conv_steps = sems[8:13]

        @block.sync
        def _(sp):
            def load(c, j):
                for half, w in enumerate((gate_w, up_w)):
                    load_unit(core, sp, sems, c, half, KD, w(0, c * CHUNK_COLS, CHUNK_COLS, KD))
            walk_loads(sp, FF_CHUNKS, load, prepared)
            load_following(core, sp, sems, following, (FF_CHUNKS, FF_CHUNKS))

        @block.tensor
        def _(pe):
            def multiply(c, j):
                pe.wait_ge(made, CT * c + 1)
                for half in range(2):
                    pe.wait_ge(sems[4 + half], c + 2)
                    for m in range(CT):
                        for k in range(KD):
                            mm = three_passes(nc, core.bank(4 * j + CT * half + m),
                                              seen(core, half, KD, k, m * P, (m + 1) * P),
                                              (core.h_hi[:, k, :], core.h_lo[:, k, :]),
                                              start=(k == 0), stop=(k == KD - 1))
                        mm.then_inc(used[half], 1)
            walk(pe, FF_CHUNKS, multiply)

        @block.scalar
        def _(act):
            def ahead(c):
                if isinstance(c, int) and c == FF_CHUNKS:
                    round_following(core, act, sems, following, c, CT)
                    return
                for half in unsplit(c, prepared):
                    round_unit(core, act, sems, c, half, CT)

            def work(c, j):
                act.wait_ge(made, CT * c + 1)
                for n in range(2 * CT if conv else CT):
                    half, m = n // CT, n % CT
                    hold(act, used[half], CT * c + m + 2)
                    to = scratch[:, 2 * CT * j + n, :]
                    if conv is None:
                        nc.scalar.activation(to, core.bank(4 * j + n), ACT.Silu).then_inc(silus, 1)
                    else:
                        f = (1 - half) * KF
                        nc.scalar.activation(to, core.bank(4 * j + n), ACT.Identity,
                                             scale=taps[:, bass.ds(2 * KF * (width - 1) + f + CT * c + m, 1)],
                                             bias=bias[:, bass.ds(f + CT * c + m, 1)]).then_inc(biased, 1)
                for m in range(CT if conv else 0):
                    act.wait_ge(convolved, 2 * CT * c + m + 1)
                    to = scratch[:, 2 * CT * j + m, :]
                    nc.scalar.activation(to, to, ACT.Silu).then_inc(silus, 1)
            walk(act, FF_CHUNKS, work, ahead)

        @block.vector
        def _(dve):
            def ahead(c):
                if isinstance(c, int) and c == FF_CHUNKS:
                    rest_following(core, dve, sems, following, c)
                    return
                for half in unsplit(c, prepared):
                    rest_unit(core, dve, sems, c, half)

            def work(c, j):
                for n in range(2 * CT if conv else 0):
                    half, m = n // CT, n % CT
                    dve.wait_ge(biased, 2 * CT * c + n + 1)
                    s = scratch[:, 2 * CT * j + n, :]
                    for back in range(1, width):
                        tap = taps[:, bass.ds(2 * KF * (width - 1 - back) + (1 - half) * KF + CT * c + m, 1)]
                        ins = nc.vector.scalar_tensor_tensor(
                            out=s[:, back:T], in0=core.bank(4 * j + n)[:, 0:T - back], scalar=tap,
                            in1=s[:, back:T], op0=ALU.mult, op1=ALU.add)
                        if back < width - 1:
                            ins.then_inc(conv_steps, 1)
                            dve.wait_ge(conv_steps, (width - 2) * (2 * CT * c + n) + back)
                    ins.then_inc(convolved, 1)
                for m in range(CT):
                    dve.wait_ge(silus, CT * c + m + 1)
                    if conv is None:
                        dve.wait_ge(used[1], CT * c + m + 2)
                        up = core.bank(4 * j + CT + m)
                    else:
                        dve.wait_ge(convolved, 2 * CT * c + CT + m + 1)
                        up = scratch[:, 2 * CT * j + CT + m, :]
                    nc.vector.tensor_tensor(hidden[:, CT * c + m, :], scratch[:, 2 * CT * j + m, :], up,
                                            ALU.mult).then_inc(made, 1)
            walk(dve, FF_CHUNKS, work, ahead)


def flip(core, jobs, ident, following=None, loaded=False, writes=()):
    nc = core.nc
    with stage(nc, "turned", "stored_act", "stored_dve", "written", *UNIT_SEMS,
               starts=prepared_starts(loaded and LOADED)) as (
            block, turned, stored_act, stored_dve, written, *sems):
        stored = [stored_act, stored_dve]

        @block.sync
        def _(sp):
            if not loaded:
                load_following(core, sp, sems, following, (0, 0))
            for n, (to, view) in enumerate(writes):
                sp.wait_ge(stored_act, n + 1)
                sp.wait_ge(stored_dve, n + 1)
                sp.dma_start(to, view).then_inc(written, 16)
            if writes:
                sp.wait_ge(written, 16 * len(writes))

        @block.tensor
        def _(pe):
            for n, (sources, dst, scale) in enumerate(jobs):
                if n >= BANKS:
                    pe.wait_ge(stored[n % 2], (n - BANKS) // 2 + 1)
                at = 0
                for src in sources:
                    p, c = src.shape
                    mm = nc.tensor.transpose(core.bank(n % BANKS)[0:c, at:at + p], src, ident[0:p, 0:p])
                    at += p
                mm.then_inc(turned, 1)

        def store(engine, parity, put):
            for n, (sources, dst, scale) in enumerate(jobs):
                if n % 2 == parity:
                    c, w = dst.shape
                    all_w = sum(src.shape[0] for src in sources)
                    engine.wait_ge(turned, n + 1)
                    put(dst, core.bank(n % BANKS)[0:c, all_w - w:all_w], scale).then_inc(stored[parity], 1)

        @block.scalar
        def _(act):
            if loaded:
                round_following(core, act, sems, following, 0, 1)
            store(act, 0, lambda to, what, scale: nc.scalar.activation(to, what, ACT.Copy, scale=scale))

        @block.vector
        def _(dve):
            if loaded:
                rest_following(core, dve, sems, following, 0)
            store(dve, 1, lambda to, what, scale: nc.vector.tensor_scalar(to, what, scale, None, ALU.mult))


DH = 64
ATTEND_WORDS = 8 * T + 16


def attend(core, scratch_at, ident, loops, unroll, q_of, k_of, v_of, bias_of, out_of, width, keys,
           meanwhile=None, started=0):
    nc = core.nc
    qs = core.cut(scratch_at, 2, T)
    sb = core.cut(scratch_at + 2 * T, 2, T)
    pb = core.cut(scratch_at + 4 * T, 2, T)
    pt = core.cut(scratch_at + 6 * T, 2, T)
    stats = core.cut(scratch_at + 8 * T, 4, 4)
    steps = unroll * TT

    def cuts(n):
        return [(k, min(P, n - k)) for k in range(0, n, P)]

    with stage(nc, "q_ready", "scored", "biased", "max_ready", "exp_done", "turned", "turned_stored",
               "weighed", "sum_inverted", "out_done", "other_steps", starts={"other_steps": started},
               from_one=("scored", "biased", "max_ready", "exp_done", "turned", "turned_stored", "weighed",
                         "sum_inverted", "out_done")) as (
            block, q_ready, scored, biased, max_ready, exp_done, turned, turned_stored,
            weighed, sum_inverted, out_done, other_steps):

        @block.gpsimd
        def _(pool):
            with pool.Fori(0, loops) as i:
                base = i * steps + 1
                for u in range(unroll):
                    if u >= 2:
                        hold(pool, scored, base + TT * (u - 1))
                    else:
                        hold(pool, weighed, base)
                    nc.gpsimd.tensor_copy(qs[0:DH, u % 2, :], q_of(i, u)).then_inc(q_ready, 1)

        @block.tensor
        def _(pe):
            with pe.Fori(0, loops) as i:
                base = i * steps + 1
                for n in range(steps + 3):
                    if n < steps:
                        u, t, b = n // TT, n % TT, n % 2
                        nk = keys(t)
                        if t == 0:
                            pe.wait_ge(q_ready, i * unroll + u + 1)
                        if n >= 2:
                            pe.wait_ge(biased, base + n - 1)
                        pe.nop(nofuse=True)
                        nc.tensor.matmul(core.bank(b)[:, 0:nk], qs[0:DH, u % 2, t * P:(t + 1) * P],
                                         k_of(i, u, nk), start=True, stop=True).then_inc(scored, 1)
                    if 2 <= n < steps + 2:
                        s = n - 2
                        t, b = s % TT, s % 2
                        pe.wait_ge(exp_done, base + s + 1)
                        if s >= 2:
                            pe.wait_ge(turned_stored, base + s - 1)
                        for k, kn in cuts(keys(t)):
                            mm = nc.tensor.transpose(core.bank(2 + b)[0:kn, k:k + P], pb[:, b, k:k + kn], ident)
                        mm.then_inc(turned, 1)
                    if n >= 3:
                        s = n - 3
                        u, t, b = s // TT, s % TT, s % 2
                        pe.wait_ge(turned_stored, base + s + 1)
                        pe.wait_ge(out_done, base + (s - 1 if s >= 2 else 0))
                        pe.nop(nofuse=True)
                        parts = cuts(keys(t))
                        for c, (k, kn) in enumerate(parts):
                            mm = nc.tensor.matmul(core.bank(4 + b)[:, 0:width], pt[0:kn, b, k:k + P],
                                                  v_of(i, u, c, kn), start=(c == 0), stop=(c == len(parts) - 1))
                        mm.then_inc(weighed, 1)

        @block.vector
        def _(dve):
            with dve.Fori(0, loops) as i:
                base = i * steps + 1
                for n in range(steps + 3):
                    if n >= 3:
                        s = n - 3
                        dve.wait_ge(exp_done, base + s + 1)
                        nc.vector.reciprocal(stats[:, s % 4, 3:4], stats[:, s % 4, 2:3]).then_inc(sum_inverted, 1)
                    if n < steps:
                        u, t, b = n // TT, n % TT, n % 2
                        nk = keys(t)
                        dve.wait_ge(scored, base + n + 1)
                        dve.wait_ge(exp_done, base + (n - 1 if n >= 2 else 0))
                        nc.vector.tensor_tensor(sb[:, b, 0:nk], core.bank(b)[:, 0:nk], bias_of(i, u, t, nk),
                                                ALU.add).then_inc(biased, 1)
                        dve.wait_ge(biased, base + n + 1)
                        nc.vector.tensor_reduce(stats[:, n % 4, 1:2], sb[:, b, 0:nk], AX_X, ALU.max,
                                                negate=True).then_inc(max_ready, 1)
                        if meanwhile:
                            meanwhile(dve, other_steps, i, n)
                    if n >= 3:
                        s = n - 3
                        u, t, b = s // TT, s % TT, s % 2
                        dve.wait_ge(sum_inverted, base + s + 1)
                        dve.wait_ge(weighed, base + s + 1)
                        nc.vector.tensor_scalar(out_of(i, u, t), core.bank(4 + b)[:, 0:width],
                                                stats[:, s % 4, 3:4], None, ALU.mult).then_inc(out_done, 1)

        @block.scalar
        def _(act):
            with act.Fori(0, loops) as i:
                base = i * steps + 1
                for n in range(steps + 2):
                    if n >= 2:
                        s = n - 2
                        t, b = s % TT, s % 2
                        act.wait_ge(turned, base + s + 1)
                        act.wait_ge(weighed, base + (s - 1 if s >= 2 else 0))
                        parts = cuts(keys(t))
                        kn, kw = parts[0][1], P * len(parts)
                        nc.scalar.copy(pt[0:kn, b, 0:kw], core.bank(2 + b)[0:kn, 0:kw]).then_inc(turned_stored, 1)
                    if n < steps:
                        t, b = n % TT, n % 2
                        nk = keys(t)
                        act.wait_ge(max_ready, base + n + 1)
                        act.wait_ge(turned, base + (n - 1 if n >= 2 else 0))
                        nc.scalar.activation(pb[:, b, 0:nk], sb[:, b, 0:nk], ACT.Exp,
                                             bias=stats[:, n % 4, 1:2],
                                             accum_out=stats[:, n % 4, 2:3]).then_inc(exp_done, 1)


def load_stage(nc, pairs_of):
    with stage(nc, "small_loaded") as (block, small_loaded):
        @block.sync
        def _(sp):
            for dst, src in pairs_of:
                sp.dma_start(dst, src).then_inc(small_loaded, 16)
            sp.wait_ge(small_loaded, 16 * len(pairs_of))


def input_parts(core, x):
    xt = core.work(0, TT, D)
    return ([(xt, x.rearrange("(t p) d -> p t d", p=P))],
            [([xt[:, t, k * P:(k + 1) * P] for t in range(TT)], core.x[:, k, :], 1.0) for k in range(KD)])


def store_output(core, src, y, ident):
    yt = core.work(0, TT, D)
    flip(core, [([src[:, 4 * g + k, t * P:(t + 1) * P] for k in range(4)],
                 yt[:, t, g * 4 * P:(g + 1) * 4 * P], 1.0) for t in range(TT) for g in range(KD // 4)], ident,
         writes=[(y[t * P:(t + 1) * P, :], yt[:, t, :]) for t in range(TT)])


def load_columns(core, rows_at, groups, ident, loads=(), jobs=()):
    loads, jobs = list(loads), list(jobs)
    for entries, dst in groups:
        width, at = entries[0].shape[1], 0
        tiles = -(-sum(src.shape[0] for src in entries) // P)
        rows = core.work(rows_at, tiles, P)
        rows_at += tiles * P
        for src in entries:
            done = 0
            while done < src.shape[0]:
                n = min(src.shape[0] - done, P - at % P)
                loads.append((rows[at % P:at % P + n, at // P, 0:width], src[done:done + n, :]))
                at += n
                done += n
        jobs.append(([rows[0:min(P, at - P * c), c, 0:width] for c in range(tiles)], dst[0:width, 0:at], 1.0))
    load_stage(core.nc, loads)
    flip(core, jobs, ident)


Q_HEADS, KV = 8, 2
GROUP = Q_HEADS // KV
D_Q, D_KV = Q_HEADS * DH, KV * DH
Q_COL = 0
KC_COL = Q_COL + D_Q
VC_COL, KS_COL, VS_COL, KW_COL, VW_COL = (KC_COL + D_KV * n for n in range(1, 6))
GATE_COL = VW_COL + D_KV
BRANCHES = 3
U_COL = GATE_COL + Q_HEADS * BRANCHES
D_GMLP = 512
V_COL = U_COL + D_GMLP
D_PROJ = V_COL + D_GMLP
CMP_BLOCK, CMP_STRIDE, CMP_HIDDEN = 32, 16, 256
CMP_N = (T - CMP_BLOCK) // CMP_STRIDE + 1
REL_BUCKETS, REL_MAX_DIST = 32, 128
SGU_GROUPS = 8
BIAS_ROW = T + P


def head_norms(core, views, at, loads=(), following=None):
    nc = core.nc
    sizes = [v.shape[1] * v.shape[2] for v in views]
    total = sum(sizes)
    p = views[0].shape[0]
    pieces, lo = [], 0
    ms = core.work(at, 3, total)
    sq_at = at + 3 * total
    for v in views:
        tiles, heads, width = v.shape[1:]
        for a in range(tiles):
            s = core.work(sq_at, heads * width)[0:p].rearrange("p (h w) -> p h w", h=heads)
            pieces.append((v[:, a], s, slice(lo, lo + heads), width))
            lo += heads
            sq_at += heads * width
    by_act = pieces[0::2] if len(pieces) > 1 else []
    by_pool = pieces[3::4]
    loads = list(loads) + [(core.raw(half, a)[:, :, 0:src.shape[2]], src)
                           for half, (a, src) in enumerate(following or ())]
    with stage(nc, "squared_act", "squared", "summed", "mean_ready", "root_ready", "inverted", "scaled", "loaded") as (
            block, squared_act, squared, summed, mean_ready, root_ready, inverted, scaled, loaded):
        @block.sync
        def _(sp):
            for dst, src in loads:
                sp.dma_start(dst, src).then_inc(loaded, 16)
            if loads:
                sp.wait_ge(loaded, 16 * len(loads))

        @block.scalar
        def _(act):
            for x, s, m, width in by_act:
                nc.scalar.activation(s, x, ACT.Square).then_inc(squared_act, 1)
            act.wait_ge(mean_ready, 1)
            nc.scalar.activation(ms[0:p, 1, :], ms[0:p, 0, :], ACT.Sqrt).then_inc(root_ready, 1)

        def scale(engine, piece):
            x, s, m, width = piece
            r = ms[0:p, 2, m].unsqueeze(2).broadcast_to([p, x.shape[1], width])
            engine.tensor_tensor(x, x, r, ALU.mult).then_inc(scaled, 1)

        @block.gpsimd
        def _(pool):
            for piece in by_pool:
                pool.wait_ge(inverted, 1)
                scale(nc.gpsimd, piece)

        @block.vector
        def _(dve):
            own = pieces[1::2] if by_act else pieces
            for x, s, m, width in own:
                nc.vector.tensor_tensor(s, x, x, ALU.mult).then_inc(squared, 1)
            for n, (x, s, m, width) in enumerate(pieces):
                if by_act and n % 2 == 0:
                    dve.wait_ge(squared_act, n // 2 + 1)
                else:
                    dve.wait_ge(squared, n // 2 + 1)
                nc.vector.tensor_reduce(ms[0:p, 0, m], s, AX_X, ALU.add).then_inc(summed, 1)
            dve.wait_ge(summed, len(pieces))
            lo = 0
            for v, n in zip(views, sizes):
                m = ms[0:p, 0, lo:lo + n]
                ins = nc.vector.tensor_scalar(m, m, 1.0 / v.shape[3], EPS, ALU.mult, ALU.add)
                lo += n
            ins.then_inc(mean_ready, 1)
            dve.wait_ge(root_ready, 1)
            nc.vector.reciprocal(ms[0:p, 2, :], ms[0:p, 1, :]).then_inc(inverted, 1)
            dve.wait_ge(inverted, 1)
            for n, piece in enumerate(pieces):
                if n % 4 != 3:
                    scale(nc.vector, piece)


def bias_stage(core, a, bias, scratch_dram, at):
    nc = core.nc
    table = core.work(at, Q_HEADS)
    buckets = core.work(at + Q_HEADS, BIAS_ROW)
    rows = core.work(at + Q_HEADS + BIAS_ROW, BIAS_ROW)
    back = core.work(at + Q_HEADS + 2 * BIAS_ROW, P)
    shifted = core.ring(0, Q_HEADS, T)
    with stage(nc, "small_loaded", "table_ready", "rows_ready", "rows_stored", "shifted_ready", "round_ready",
               "rows_saved", "bias_stored") as (
            block, small_loaded, table_ready, rows_ready, rows_stored, shifted_ready, round_ready, rows_saved,
            bias_stored):
        @block.gpsimd
        def _(pool):
            nc.gpsimd.memset(table[REL_BUCKETS:REL_BUCKETS + 1, :], NEG).then_inc(table_ready, 1)

        @block.sync
        def _(sp):
            sp.dma_start(table[0:REL_BUCKETS, :], a["rel_bias"]).then_inc(small_loaded, 16)
            sp.dma_start(buckets[0:REL_BUCKETS + 1, :], a["buckets"]).then_inc(small_loaded, 16)
            sp.dma_start(back, a["reversed"]).then_inc(small_loaded, 16)
            sp.wait_ge(rows_stored, 2)
            sp.dma_start(scratch_dram, rows[0:Q_HEADS, :]).then_inc(rows_saved, 16)
            sp.wait_ge(rows_saved, 16)
            for h in range(Q_HEADS):
                sp.dma_start(shifted[:, h, :], bass.AP(scratch_dram.tensor, h * BIAS_ROW, [[1, P], [1, T]])
                             ).then_inc(shifted_ready, 16)

        @block.tensor
        def _(pe):
            pe.wait_ge(small_loaded, 48)
            pe.wait_ge(table_ready, 1)
            n = REL_BUCKETS + 1
            for c, (lo, w) in enumerate([(0, T), (T, BIAS_ROW - T)]):
                nc.tensor.matmul(core.bank(c)[0:Q_HEADS, 0:w], table[0:n, :], buckets[0:n, lo:lo + w],
                                 start=True, stop=True).then_inc(rows_ready, 1)
            pe.wait_ge(rows_stored, 2)
            pe.wait_ge(shifted_ready, 16 * Q_HEADS)
            for h in range(Q_HEADS):
                nc.tensor.matmul(core.bank(h), back, shifted[:, h, :], start=True, stop=True).then_inc(round_ready, 1)

        @block.vector
        def _(dve):
            for c, (lo, w) in enumerate([(0, T), (T, BIAS_ROW - T)]):
                dve.wait_ge(rows_ready, c + 1)
                nc.vector.tensor_copy(rows[0:Q_HEADS, lo:lo + w], core.bank(c)[0:Q_HEADS, 0:w]).then_inc(rows_stored, 1)
            for h in range(Q_HEADS):
                dve.wait_ge(round_ready, h + 1)
                nc.vector.tensor_copy(bias[:, h, :], core.bank(h)).then_inc(bias_stored, 1)


def activation_stage(core, jobs):
    nc = core.nc
    with stage(nc, "activated") as (block, activated):
        @block.scalar
        def _(act):
            for out, x, func in jobs:
                nc.scalar.activation(out, x, func).then_inc(activated, 1)


def compress_stage(core, ident, w1_of, w2, turned, pe_cols, b1_cols, out, at):
    nc = core.nc
    pairs_n = CMP_BLOCK // 2
    N = KV * CMP_N
    blocks = core.work(at, 2 * pairs_n, N)
    hid = core.work(at + 2 * pairs_n * N, 4, N)
    plain = core.work(at + 2 * pairs_n * N + 4 * N, 2, CMP_HIDDEN)[0:N]
    hid_tiles = CMP_HIDDEN // P
    with stage(nc, "blocks_ready", "plain_ready", "plain_stored", "hidden_ready", "hidden_stored", "compressed", "out_stored") as (
            block, blocks_ready, plain_ready, plain_stored, hidden_ready, hidden_stored, compressed, out_stored):
        @block.vector
        def _(dve):
            half = pairs_n // 2
            for kind in range(2):
                for g in range(KV):
                    x = turned[kind][:, g, :].rearrange("p (n s) -> p s n", s=CMP_STRIDE)
                    for hh in range(2):
                        c = kind * pairs_n + half * hh
                        pe_v = pe_cols[:, c:c + half].unsqueeze(2).broadcast_to([P, half, CMP_N])
                        nc.vector.tensor_tensor(blocks[:, c:c + half, g * CMP_N:(g + 1) * CMP_N],
                                                x[:, 0:CMP_STRIDE:2, hh:hh + CMP_N], pe_v,
                                                ALU.add).then_inc(blocks_ready, 1)
            for kind in range(2):
                dve.wait_ge(plain_ready, kind + 1)
                nc.vector.tensor_copy(plain[:, kind, :], core.bank(kind)[0:N, 0:CMP_HIDDEN]).then_inc(plain_stored, 1)
            for kind in range(2):
                for g in range(KV):
                    n = kind * KV + g
                    dve.wait_ge(compressed, n + 1)
                    nc.vector.tensor_copy(out[kind][0:CMP_N, g, :], core.bank(4 + n)[0:CMP_N, 0:DH]).then_inc(out_stored, 1)

        @block.tensor
        def _(pe):
            pe.wait_ge(blocks_ready, 8)
            for kind in range(2):
                w1 = w1_of[kind]
                for c in range(pairs_n):
                    mm = nc.tensor.matmul(core.bank(kind)[0:N, 0:CMP_HIDDEN], blocks[:, kind * pairs_n + c, :],
                                          w1[:, c, :], start=(c == 0), stop=(c == pairs_n - 1))
                mm.then_inc(plain_ready, 1)
            for kind in range(2):
                pe.wait_ge(plain_stored, kind + 1)
                for m in range(hid_tiles):
                    nc.tensor.transpose(core.bank(2 + kind)[:, m * P:m * P + N],
                                        plain[:, kind, m * P:(m + 1) * P], ident[0:N, 0:N]).then_inc(hidden_ready, 1)
            for kind in range(2):
                pe.wait_ge(hidden_stored, 2 * kind + 2)
                for g in range(KV):
                    for k in range(hid_tiles):
                        mm = nc.tensor.matmul(core.bank(4 + kind * KV + g)[0:CMP_N, 0:DH],
                                              hid[:, 2 * kind + k, g * CMP_N:(g + 1) * CMP_N],
                                              w2[:, 2 * kind + k, :], start=(k == 0), stop=(k == hid_tiles - 1))
                    mm.then_inc(compressed, 1)

        @block.scalar
        def _(act):
            for n in range(4):
                act.wait_ge(hidden_ready, hid_tiles * (n // hid_tiles + 1))
                at_n = n % hid_tiles * P
                nc.scalar.activation(hid[:, n, :], core.bank(2 + n // hid_tiles)[:, at_n:at_n + N], ACT.Gelu_apprx_tanh,
                                     bias=b1_cols[:, n:n + 1]).then_inc(hidden_stored, 1)


def spatial_stage(core, pr, w_T, keep, gain_row, bias_cols, mixed, col, loads):
    nc = core.nc
    width = D_GMLP // SGU_GROUPS
    v = pr[:, :, V_COL:V_COL + D_GMLP]
    with stage(nc, "masked", "gained", "mixed_ready", "gated", "loaded") as (
            block, masked, gained, mixed_ready, gated, loaded):
        @block.sync
        def _(sp):
            for dst, src in loads:
                sp.dma_start(dst, src).then_inc(loaded, 16)
            sp.wait_ge(loaded, 16 * len(loads))

        @block.gpsimd
        def _(pool):
            nc.gpsimd.tensor_tensor(w_T, w_T, keep.unsqueeze(1).broadcast_to([P, SGU_GROUPS, P]),
                                    ALU.mult).then_inc(masked, 1)

        @block.tensor
        def _(pe):
            pe.wait_ge(masked, 1)
            pe.wait_ge(gained, 1)
            for g in range(SGU_GROUPS):
                nc.tensor.matmul(core.bank(g)[:, 0:TT * width], w_T[:, g, :], v[:, :, g * width:(g + 1) * width],
                                 start=True, stop=True).then_inc(mixed_ready, 1)

        @block.vector
        def _(dve):
            nc.vector.tensor_tensor(v, v, gain_row.unsqueeze(1).broadcast_to([P, TT, D_GMLP]),
                                    ALU.mult).then_inc(gained, 1)
            for g in range(SGU_GROUPS):
                dve.wait_ge(mixed_ready, g + 1)
                nc.vector.scalar_tensor_tensor(
                    out=mixed[:, :, col + g * width:col + (g + 1) * width],
                    in0=core.bank(g)[:, 0:TT * width].rearrange("p (t w) -> p t w", t=TT),
                    scalar=bias_cols[:, g:g + 1],
                    in1=pr[:, :, U_COL + g * width:U_COL + (g + 1) * width],
                    op0=ALU.add, op1=ALU.mult).then_inc(gated, 1)


def branches_stage(core, outs, gates, row_valid, mixed):
    nc = core.nc
    with stage(nc, "valid_ready", "scaled", "summed") as (block, valid_ready, scaled, summed):
        def scale(engine, n):
            o = outs[n].rearrange("p t (h w) -> p t h w", h=Q_HEADS)
            g = gates[:, :, n:Q_HEADS * BRANCHES:BRANCHES].unsqueeze(3).broadcast_to([P, TT, Q_HEADS, DH])
            engine.tensor_tensor(o, o, g, ALU.mult).then_inc(scaled, 1)

        @block.gpsimd
        def _(pool):
            scale(nc.gpsimd, 2)

        @block.vector
        def _(dve):
            nc.vector.tensor_scalar(gates[:, 0, 0:Q_HEADS * BRANCHES:BRANCHES],
                                    gates[:, 0, 0:Q_HEADS * BRANCHES:BRANCHES], row_valid, None,
                                    ALU.mult).then_inc(valid_ready, 1)
            scale(nc.vector, 1)
            dve.wait_ge(valid_ready, 1)
            scale(nc.vector, 0)
            dve.wait_ge(scaled, 3)
            m = mixed[:, :, 0:D_Q]
            nc.vector.tensor_tensor(m, outs[0], outs[1], ALU.add).then_inc(summed, 1)
            dve.wait_ge(summed, 1)
            nc.vector.tensor_tensor(m, m, outs[2], ALU.add).then_inc(summed, 1)


def first_block(core, a, scratch_dram, ident, ones, loads, jobs):
    nc = core.nc
    cols = core.const(2 * KD + SGU_GROUPS + CMP_BLOCK + 4)
    heads_cols = core.const(5)
    taps = core.const(3 * 2 * KF + 2 * KF)
    row_valid = core.const(1)
    kc_T = core.const(KV, CMP_N)
    kc = core.const(KV, DH)
    vc = core.const(KV, DH)
    PE_AT, B1_AT = 2 * KD + SGU_GROUPS, 2 * KD + SGU_GROUPS + CMP_BLOCK
    pr = core.work(0, TT, D_PROJ)
    at = TT * D_PROJ
    bias = core.work(at, Q_HEADS, T)
    kT = core.work(at + 8 * T, 2 * KV, T)
    scratch_at = at + 12 * T
    qT = core.ring(0, Q_HEADS, T)
    outs = [core.ring(8 * T + n * TT * D_Q, TT, D_Q) for n in range(BRANCHES)]
    mixed = core.cut(H_AT, TT, D)
    mixed_T = core.work(0, KD, T)

    rows = lambda v: v.rearrange("(k p) -> k p", p=P)
    pe_rows = lambda v: v.rearrange("(c a) d -> c (a d)", a=2)
    load_columns(core, TT * D, [
        ([rows(a["attn_norm"][0]), rows(a["ffn_norm"][0]), a["sgu_b"][0], pe_rows(a["cmp_pe_k"][0]),
          pe_rows(a["cmp_pe_v"][0]), rows(a["cmp_b1_k"][0]), rows(a["cmp_b1_v"][0])], cols),
        ([a[n] for n in ("q_norm", "k_norm_cmp", "k_norm_slc", "k_norm_win")], heads_cols),
        ([a["conv_w"][0].rearrange("w (f p) -> (w f) p", p=P), rows(a["conv_b"][0])], taps)], ident, loads, jobs)
    w_in = columns_of(a["w_in"][0])
    norm_stage(core, ones, cols[:, 0:KD], following=first_columns(w_in, D_PROJ))
    project(core, w_in, D_PROJ, pr, None, to_tokens=True, prepared=SPLIT)
    bias_stage(core, a, bias, scratch_dram, scratch_at)

    gates = pr[:, :, GATE_COL:GATE_COL + Q_HEADS * BRANCHES]
    activation_stage(core, [(pr[:, t, U_COL:U_COL + 2 * D_GMLP],) * 2 + (ACT.Gelu_apprx_tanh,) for t in range(TT)]
                     + [(gates, gates, ACT.Sigmoid)])
    pairs_n = CMP_BLOCK // 2
    w1_words = pairs_n * CMP_HIDDEN
    cmp_w1 = [core.ring(kind * w1_words, pairs_n, CMP_HIDDEN) for kind in range(2)]
    w_sgu = core.ring(2 * w1_words, SGU_GROUPS, P)
    w_T = core.ring(2 * w1_words + SGU_GROUPS * P, SGU_GROUPS, P)
    gain_row = core.ring(2 * w1_words + 2 * SGU_GROUPS * P, D_GMLP)
    keep = core.ring(2 * w1_words + 2 * SGU_GROUPS * P + D_GMLP, P)
    cmp_w2 = core.ring(2 * w1_words + 2 * SGU_GROUPS * P + D_GMLP + P, 4, DH)
    loads = [(w_sgu, a["sgu_w"][0].rearrange("g i j -> i g j")), (gain_row, a["sgu_norm"][0].partition_broadcast(P)),
             (keep, a["upper"]), (row_valid, a["row_valid"])]
    cmp_loads = [[], []]
    for kind, name in enumerate("kv"):
        cmp_loads[kind] += [(cmp_w1[kind], a[f"cmp_w1_{name}"][0].rearrange("(c p) n -> p c n", p=P)),
                  (cmp_w2[:, 2 * kind:2 * kind + 2, :], a[f"cmp_w2_{name}"][0].rearrange("(k p) n -> p k n", p=P))]
    by_head = lambda lo, heads, w: pr[:, :, lo:lo + heads * w].rearrange("p t (h w) -> p t h w", h=heads)
    head_norms(core, [by_head(Q_COL, Q_HEADS, DH), by_head(KS_COL, KV, DH), by_head(KW_COL, KV, DH),
                      by_head(V_COL, 1, D_GMLP)], scratch_at, loads=loads + cmp_loads[0])

    flip(core, [([w_sgu[:, g, :]], w_T[:, g, :], 1.0) for g in range(SGU_GROUPS)], ident)
    spatial_stage(core, pr, w_T, keep, gain_row, cols[:, 2 * KD:2 * KD + SGU_GROUPS], mixed, D_Q,
                  cmp_loads[1])

    pair_T = [core.work(scratch_at + KV * T * kind, KV, T) for kind in range(2)]
    jobs = []
    for kind, lo in enumerate((KC_COL, VC_COL)):
        for g in range(KV):
            src = [pr[:, t, lo + g * DH:lo + (g + 1) * DH] for t in range(TT)]
            jobs.append((src, pair_T[kind][0:DH, g, :], 1.0))
            jobs.append((src, pair_T[kind][DH:P, g, 0:T - 1], 1.0))
    flip(core, jobs, ident)
    compress_stage(core, ident, cmp_w1, cmp_w2, pair_T, cols[:, PE_AT:PE_AT + CMP_BLOCK], cols[:, B1_AT:B1_AT + 4], [kc, vc], scratch_at + ATTEND_WORDS)
    head_norms(core, [kc[0:CMP_N].unsqueeze(1)], scratch_at)

    with stage(nc, "scaled") as (block, scaled):
        @block.vector
        def _(dve):
            nc.vector.tensor_scalar(heads_cols[0:DH, 4:5], heads_cols[0:DH, 0:1], DH ** -0.5, None,
                                    ALU.mult).then_inc(scaled, 1)
    jobs = [([pr[:, t, Q_COL + h * DH:Q_COL + (h + 1) * DH] for t in range(TT)], qT[0:DH, h, :],
             heads_cols[0:DH, 4:5]) for h in range(Q_HEADS)]
    for b, lo in enumerate((KS_COL, KW_COL)):
        jobs += [([pr[:, t, lo + g * DH:lo + (g + 1) * DH] for t in range(TT)], kT[0:DH, b * KV + g, :],
                  heads_cols[0:DH, 2 + b:3 + b]) for g in range(KV)]
    jobs += [([kc[0:CMP_N, g, :]], kc_T[0:DH, g, :], heads_cols[0:DH, 1:2]) for g in range(KV)]
    flip(core, jobs, ident)

    attend(core, WORK_AT + scratch_at, ident, KV, 2 * GROUP,
           q_of=lambda i, u: qT[0:DH, i * GROUP + u % GROUP, :],
           k_of=lambda i, u, n: kT[0:DH, i + u // GROUP * KV, 0:n],
           v_of=lambda i, u, kt, n: pr[0:n, kt, bass.ds((VS_COL, VW_COL)[u // GROUP] + i * DH, DH)],
           bias_of=lambda i, u, t, n: bias[:, i * GROUP + u % GROUP, T - P - P * t:T - P - P * t + n],
           out_of=lambda i, u, t: outs[1 + u // GROUP][:, t, bass.ds((i * GROUP + u % GROUP) * DH, DH)],
           width=DH, keys=lambda t: P * (t + 1))
    first_end = CMP_BLOCK - 1
    attend(core, WORK_AT + scratch_at, ident, KV, GROUP,
           q_of=lambda i, u: qT[0:DH, i * GROUP + u, :],
           k_of=lambda i, u, n: kc_T[0:DH, i, 0:n],
           v_of=lambda i, u, kt, n: vc[0:n, i, :],
           bias_of=lambda i, u, t, n: bias[:, i * GROUP + u, T - P - P * t + first_end:
                                           T - P - P * t + first_end + CMP_STRIDE * (n - 1) + 1:CMP_STRIDE],
           out_of=lambda i, u, t: outs[0][:, t, bass.ds((i * GROUP + u) * DH, DH)],
           width=DH, keys=lambda t: (P * (t + 1) - CMP_BLOCK) // CMP_STRIDE + 1)
    branches_stage(core, outs, gates, row_valid, mixed)

    flip(core, [([mixed[:, t, k * P:(k + 1) * P] for t in range(TT)], mixed_T[:, k, :], 1.0) for k in range(KD)], ident,
         following=first_rows(rows_of(a["w_out"][0])))
    rows_product(core, mixed_T, KD, rows_of(a["w_out"][0]), add_to_residual(core), prepared=LOADED)
    hidden = core.work(0, KF, T)
    up = columns_of(a["w_up"][0])
    gate = lambda k, lo, n, tiles: up(k, lo + D_FF, n, tiles)
    down = rows_of(a["w_down"][0])
    norm_stage(core, ones, cols[:, KD:2 * KD], following=first_gates(gate, up))
    gated_hidden(core, gate, up, hidden, conv=(taps[:, 0:6 * KF], 3, taps[:, 6 * KF:8 * KF]),
                 prepared=SPLIT, following=first_rows(down))
    rows_product(core, hidden, KF, down, add_to_residual(core), prepared=SPLIT)


LAYERS_2 = 2
A_HEADS, IDX_HEADS, IDX_DIM, B_HEADS = 8, 8, 32, 4
D_A = A_HEADS * DH
D_B = B_HEADS * 2 * DH
TOPK = min(256, T // 4)
QA_AT, KA_AT, VA_AT = 0, D_A, 2 * D_A
IQ_AT = 3 * D_A
IK_AT = IQ_AT + IDX_HEADS * IDX_DIM
IW_AT = IK_AT + IDX_DIM
QB_AT = IW_AT + IDX_HEADS
KB_AT = QB_AT + D_B
VB_AT = KB_AT + D_B
D_IN_2 = VB_AT + D_B
PICKED = -3e38


def rotate(engine, steps, x, cos, sin, tmp):
    heads, d = x.shape[1], x.shape[2]
    half = d // 2
    a, b = tmp[:, 0, 0:heads * d], tmp[:, 1, 0:heads * d]
    a = a.rearrange("p (h d) -> p h d", h=heads)
    b = b.rearrange("p (h d) -> p h d", h=heads)
    c = cos.unsqueeze(1).broadcast_to([P, heads, d])
    s = sin.unsqueeze(1).broadcast_to([P, heads, d])
    steps.step(engine.tensor_tensor(a, x, c, ALU.mult))
    steps.step(engine.tensor_tensor(b[:, :, 0:half], x[:, :, half:d], s[:, :, 0:half], ALU.mult))
    steps.link(engine.tensor_tensor(b[:, :, half:d], x[:, :, 0:half], s[:, :, half:d], ALU.mult))
    steps.link(engine.tensor_tensor(x, a, b, ALU.add))


class Rope:

    def __init__(self, pr, tables, scratch):
        self.pr, (self.cos64, self.sin64, self.cos32, self.sin32) = pr, tables
        self.tmp = scratch

    def heads(self, engine, steps, t, at, parity):
        x = self.pr[:, t, at:at + 2 * D_A].rearrange("p (h d) -> p h d", d=DH)
        rotate(engine, steps, x, self.cos64[:, t, :], self.sin64[:, t, :], self.tmp[parity])

    def indexer(self, engine, steps, t, parity):
        x = self.pr[:, t, IQ_AT:IQ_AT + (IDX_HEADS + 1) * IDX_DIM].rearrange("p (h d) -> p h d", d=IDX_DIM)
        rotate(engine, steps, x, self.cos32[:, t, :], self.sin32[:, t, :], self.tmp[parity])


def indexer_rope_stage(nc, rope):
    with stage(nc, "dve_steps", "pool_steps") as (block, dve_steps, pool_steps):
        @block.vector
        def _(dve):
            steps = Count(dve, dve_steps)
            for t in range(TT - 1):
                rope.indexer(nc.vector, steps, t, 0)

        @block.gpsimd
        def _(pool):
            rope.indexer(nc.gpsimd, Count(pool, pool_steps), TT - 1, 1)


class Picker:
    TILES = range(1, TT)

    def __init__(self, core, scratch_at):
        self.core = core
        self.scores = core.cut(scratch_at, 2 * TT, T)
        self.best = core.cut(scratch_at + 2 * TT * T, TT, 8)
        self.iw = core.cut(scratch_at + 2 * TT * T + 8 * TT, TT, IDX_HEADS)

    def score(self, pr, iq, ik, chunk_mask, relu_at, rope):
        core, nc = self.core, self.core.nc
        relu = core.cut(relu_at, IDX_HEADS, T)
        jobs = [(t, h) for t in self.TILES for h in range(IDX_HEADS)]
        with stage(nc, "dotted", "relued", "weighed", "scaled", "masked", "dve_steps", "pool_steps") as (
                block, dotted, relued, weighed, scaled, masked, dve_steps, pool_steps):
            @block.gpsimd
            def _(pool):
                steps = Count(pool, pool_steps)
                for t in range(TT):
                    rope.heads(nc.gpsimd, steps, t, QB_AT, 1)

            @block.tensor
            def _(pe):
                for n, (t, h) in enumerate(jobs):
                    if n >= 4:
                        pe.wait_ge(relued, n - 3)
                    nk = P * (t + 1)
                    nc.tensor.matmul(core.bank(n % 4)[:, 0:nk], iq[0:IDX_DIM, h, t * P:(t + 1) * P],
                                     ik[0:IDX_DIM, 0:nk], start=True, stop=True).then_inc(dotted, 1)

            @block.scalar
            def _(act):
                for n, (t, h) in enumerate(jobs):
                    nk = P * (t + 1)
                    act.wait_ge(dotted, n + 1)
                    if n >= IDX_HEADS:
                        act.wait_ge(weighed, n - IDX_HEADS + 1)
                    nc.scalar.activation(relu[:, h, 0:nk], core.bank(n % 4)[:, 0:nk], ACT.Relu).then_inc(relued, 1)

            @block.vector
            def _(dve):
                steps = Count(dve, dve_steps)
                nc.vector.tensor_scalar(self.iw, pr[:, :, IW_AT:IW_AT + IDX_HEADS],
                                        IDX_DIM ** -0.5 * IDX_HEADS ** -0.5, None, ALU.mult).then_inc(scaled, 1)
                dve.wait_ge(scaled, 1)
                for n, (t, h) in enumerate(jobs):
                    nk = P * (t + 1)
                    acc, weight = self.scores[:, 2 * t, 0:nk], self.iw[:, t, h:h + 1]
                    dve.wait_ge(relued, n + 1)
                    if h == 0:
                        nc.vector.tensor_scalar(acc, relu[:, h, 0:nk], weight, None, ALU.mult).then_inc(weighed, 1)
                    else:
                        dve.wait_ge(weighed, n)
                        nc.vector.scalar_tensor_tensor(out=acc, in0=relu[:, h, 0:nk], scalar=weight, in1=acc,
                                                       op0=ALU.mult, op1=ALU.add).then_inc(weighed, 1)
                    if h == IDX_HEADS - 1:
                        dve.wait_ge(weighed, n + 1)
                        last = acc[:, nk - P:nk]
                        nc.vector.tensor_tensor(last, last, chunk_mask, ALU.add).then_inc(masked, 1)
                    if n % (len(jobs) // TT) == 1:
                        rope.heads(nc.vector, steps, n // (len(jobs) // TT), QA_AT, 0)

    STARTED = len(TILES)

    def half_round(self, steps, dve, sem, i, n):
        nc, r = self.core.nc, n // 2
        for t in self.TILES:
            now, then = (self.scores[:, 2 * t + (r + k) % 2, 0:P * (t + 1)] for k in range(2))
            hold(dve, sem, len(self.TILES) * (steps * i + n) + t)
            if n % 2 == 0:
                nc.vector.max(self.best[:, t, :], now).then_inc(sem, 1)
            else:
                nc.vector.match_replace(then, self.best[:, t, :], now, PICKED).then_inc(sem, 1)

    def pick(self, picks, chunk_mask):
        nc = self.core.nc
        with stage(nc, "picked") as (block, picked):
            @block.vector
            def _(dve):
                nc.vector.tensor_copy(picks[:, 0, 0:P], chunk_mask).then_inc(picked, 1)
                for t in self.TILES:
                    nk = P * (t + 1)
                    nc.vector.tensor_scalar(picks[:, t, 0:nk], self.scores[:, 2 * t + TOPK // 8 % 2, 0:nk],
                                            PICKED / 2, NEG, ALU.is_gt, ALU.mult).then_inc(picked, 1)


def difference_stage(core, ob, mixed, lam, lam_stats, gain_col, sub_gain, scratch_at):
    nc = core.nc
    W = 2 * DH
    sq = core.cut(scratch_at, TT, B_HEADS * W)
    ms = core.cut(scratch_at + TT * B_HEADS * W, 3, TT * B_HEADS)
    lam_v, steps_words = lam, lam_stats
    with stage(nc, "steps_done", "mean_ready", "root_ready", "exponents", "exps", "differed", "squared",
               "gain_ready") as (
            block, steps_done, mean_ready, root_ready, exponents, exps, differed, squared, gain_ready):
        @block.scalar
        def _(act):
            act.wait_ge(exponents, 2)
            nc.scalar.activation(steps_words[:, 2:4], steps_words[:, 0:2], ACT.Exp).then_inc(exps, 1)
            for t in range(TT):
                act.wait_ge(differed, t + 1)
                nc.scalar.activation(sq[:, t, :], mixed[:, t, D_A:D_A + D_B], ACT.Square).then_inc(squared, 1)
            act.wait_ge(mean_ready, 1)
            nc.scalar.activation(ms[:, 1, :], ms[:, 0, :], ACT.Sqrt).then_inc(root_ready, 1)

        @block.vector
        def _(dve):
            steps = Count(dve, steps_done)
            for n in range(2):
                nc.vector.tensor_tensor_reduce(lam_v[:, 2 * n, :], lam_v[:, 2 * n, :], lam_v[:, 2 * n + 1, :],
                                               1.0, 0.0, ALU.mult, ALU.add,
                                               steps_words[:, n:n + 1]).then_inc(exponents, 1)
            dve.wait_ge(exps, 1)
            steps.link(nc.vector.tensor_tensor(steps_words[:, 4:5], steps_words[:, 3:4], steps_words[:, 2:3], ALU.subtract))
            steps.link(nc.vector.tensor_tensor(steps_words[:, 5:6], steps_words[:, 4:5], steps_words[:, 6:7], ALU.subtract))
            outs = []
            for t in range(TT):
                o = ob[:, t, :].rearrange("p (h c w) -> p h c w", h=B_HEADS, c=2)
                outs.append(mixed[:, t, D_A:D_A + D_B].rearrange("p (h w) -> p h w", h=B_HEADS))
                nc.vector.scalar_tensor_tensor(out=outs[t], in0=o[:, :, 1, :], scalar=steps_words[:, 5:6],
                                               in1=o[:, :, 0, :], op0=ALU.mult, op1=ALU.add).then_inc(differed, 1)
            for t in range(TT):
                dve.wait_ge(squared, t + 1)
                s = sq[:, t, :].rearrange("p (h w) -> p h w", h=B_HEADS)
                steps.step(nc.vector.tensor_reduce(ms[:, 0, t * B_HEADS:(t + 1) * B_HEADS], s, AX_X, ALU.add))
            steps.settle()
            nc.vector.tensor_scalar(ms[:, 0, :], ms[:, 0, :], 1.0 / W, EPS, ALU.mult, ALU.add).then_inc(mean_ready, 1)
            dve.wait_ge(root_ready, 1)
            steps.link(nc.vector.reciprocal(ms[:, 2, :], ms[:, 1, :]))
            for t in range(TT):
                m = mixed[:, t, D_A:D_A + D_B].rearrange("p (h w) -> p h w", h=B_HEADS)
                r = ms[:, 2, t * B_HEADS:(t + 1) * B_HEADS].unsqueeze(2).broadcast_to([P, B_HEADS, W])
                steps.step(nc.vector.tensor_tensor(m, m, r, ALU.mult))
            nc.vector.tensor_tensor(sub_gain, gain_col, steps_words[:, 7:8], ALU.mult).then_inc(gain_ready, 1)


def swiglu(core, gate_w, up_w, down_w):
    hidden = core.work(0, KF, T)
    gated_hidden(core, gate_w, up_w, hidden, prepared=SPLIT, following=first_rows(down_w))
    rows_product(core, hidden, KF, down_w, add_to_residual(core), prepared=SPLIT)


def columns_of(w):
    w = w.rearrange("(k p) n -> p k n", p=P)
    return lambda k, lo, n, tiles=KD // 2: w[:, k:k + tiles, bass.ds(lo, n)]


def rows_of(w):
    w = w.rearrange("(k p) n -> p k n", p=P)
    return lambda k: w[:, bass.ds(k, 2), :]


def second_block(core, a, tables, chunk_mask, ident, ones):
    nc = core.nc
    pr = core.work(0, TT, D_IN_2)
    picks = core.work(TT * D_IN_2, TT, T)
    scratch_at = WORK_AT + TT * D_IN_2 + TT * T
    qT, kT = core.ring(0, A_HEADS, T), core.ring(8 * T, A_HEADS, T)
    mixed = core.cut(H_AT, TT, D)
    ob = core.cut(H_AT + TT * D, TT, B_HEADS * 4 * DH)
    mixed_T = core.work(0, KD, T)
    cols = core.const(2 * KD + 1)
    lam = core.const(4, DH)
    lam_words = core.const(8)
    sub_gain = core.const(1)
    one_minus = core.const(1)

    with nc.Fori(0, LAYERS_2) as layer:
        row = lambda v, n: v[layer].rearrange("(k p) -> k p", k=n)
        everywhere = lambda v: v.partition_broadcast(P)
        loads = [(lam[:, n, :], everywhere(a[name][layer])) for n, name in
                 enumerate(["lam_q1_2", "lam_k1_2", "lam_q2_2", "lam_k2_2"])]
        load_columns(core, 0, [([row(a["g_mix_2"], KD), row(a["g_ffn_2"], KD), row(a["g_subln_2"], 1)], cols)], ident,
                     loads + [(lam_words[:, 6:8], everywhere(a["lam_init"][layer]))])
        w_in = columns_of(a["w_in_2"][layer])
        norm_stage(core, ones, cols[:, 0:KD], following=first_columns(w_in, D_IN_2))
        project(core, w_in, D_IN_2, pr, None, to_tokens=True, prepared=SPLIT)
        rope = Rope(pr, tables, [core.cut(scratch_at + 4 * D_A * n, 2, 2 * D_A) for n in range(2)])
        indexer_rope_stage(nc, rope)

        def turned(lo, n, width, dst, scale=1.0):
            return [([pr[:, t, lo + width * h:lo + width * (h + 1)] for t in range(TT)],
                     dst[0:width, h, :], scale) for h in range(n)]
        flip(core, turned(IQ_AT, IDX_HEADS, IDX_DIM, qT) + turned(IK_AT, 1, IDX_DIM, kT), ident)
        assert 8 * D_A <= ATTEND_WORDS and D_A == D_B
        picker = Picker(core, scratch_at + ATTEND_WORDS)
        picker.score(pr, qT, kT[:, 0, :], chunk_mask, RING_AT + 9 * T, rope)

        U = 4
        loops, steps = 2 * B_HEADS // U, U * TT
        assert loops * steps // 2 == TOPK // 8 and steps % 4 == 0
        flip(core, turned(QB_AT, 2 * B_HEADS, DH, qT, DH ** -0.5) + turned(KB_AT, 2 * B_HEADS, DH, kT), ident)
        load_bias(core, picks, chunk_mask)
        attend(core, scratch_at, ident, loops, U,
               q_of=lambda i, u: qT[0:DH, i * U + u, :],
               k_of=lambda i, u, n: kT[0:DH, i * U + u, 0:n],
               v_of=lambda i, u, kt, n: pr[0:n, kt, bass.ds(VB_AT + (i * (U // 2) + u // 2) * 2 * DH, 2 * DH)],
               bias_of=lambda i, u, t, n: picks[:, t, 0:n],
               out_of=lambda i, u, t: ob[:, t, bass.ds((i * U + u) * 2 * DH, 2 * DH)],
               width=2 * DH, keys=lambda t: P * (t + 1),
               meanwhile=lambda dve, sem, i, n: picker.half_round(steps, dve, sem, i, n),
               started=Picker.STARTED)

        picker.pick(picks, chunk_mask)
        flip(core, turned(QA_AT, A_HEADS, DH, qT, DH ** -0.5) + turned(KA_AT, A_HEADS, DH, kT), ident)
        attend(core, scratch_at, ident, A_HEADS // U, U,
               q_of=lambda i, u: qT[0:DH, i * U + u, :],
               k_of=lambda i, u, n: kT[0:DH, i * U + u, 0:n],
               v_of=lambda i, u, kt, n: pr[0:n, kt, bass.ds(VA_AT + (i * U + u) * DH, DH)],
               bias_of=lambda i, u, t, n: picks[:, t, 0:n],
               out_of=lambda i, u, t: mixed[:, t, bass.ds((i * U + u) * DH, DH)],
               width=DH, keys=lambda t: P * (t + 1))
        difference_stage(core, ob, mixed, lam, lam_words, cols[:, 2 * KD:2 * KD + 1], sub_gain, RING_AT)
        flip(core, [([mixed[:, t, k * P:(k + 1) * P] for t in range(TT)], mixed_T[:, k, :],
                     1.0 if k < D_A // P else sub_gain) for k in range(KD)], ident,
             following=first_rows(rows_of(a["w_out_2"][layer])))
        rows_product(core, mixed_T, KD, rows_of(a["w_out_2"][layer]), add_to_residual(core), prepared=LOADED)
        gate, up = columns_of(a["w_gate_2"][layer]), columns_of(a["w_up_2"][layer])
        norm_stage(core, ones, cols[:, KD:2 * KD], following=first_gates(gate, up))
        swiglu(core, gate, up, rows_of(a["w_down_2"][layer]))
    load_columns(core, 0, [([a["g_final_2"].rearrange("(k p) -> k p", p=P)], cols[:, 0:KD])], ident)
    norm_stage(core, ones, cols[:, 0:KD], out=core.x)


def load_bias(core, picks, chunk_mask):
    nc = core.nc
    with stage(nc, "cleared", "masked") as (block, cleared, masked):
        @block.gpsimd
        def _(pool):
            for t in range(1, TT):
                nc.gpsimd.memset(picks[:, t, 0:t * P], 0.0).then_inc(cleared, 1)

        @block.vector
        def _(dve):
            for t in range(TT):
                nc.vector.tensor_copy(picks[:, t, t * P:(t + 1) * P], chunk_mask).then_inc(masked, 1)


S_HEADS, S_GROUPS, S_STATE = 16, 2, 128
S_INNER = S_HEADS * DH
G_HEADS, G_DIM = 8, 128
Z_COL = 0
XBC_COL = Z_COL + S_INNER
XBC = S_INNER + 2 * S_GROUPS * S_STATE
DT_COL = XBC_COL + XBC
QKV_COL = DT_COL + S_HEADS
QKV = 3 * G_HEADS * G_DIM
GZ_COL = QKV_COL + QKV
AB_COL = GZ_COL + G_HEADS * G_DIM
GATE_S_COL = AB_COL + 2 * G_HEADS
GATE_G_COL = GATE_S_COL + D
ROWS = 40
G_ROW = 32
BETA_ROW = 64
SMALL_COLS = BETA_ROW + G_HEADS
SPANS = [(sum(T - P * m for m in range(j)), T - P * j) for j in range(TT)]
SPAN_WORDS = sum(w for _, w in SPANS)
LOG_TERMS = 8


def small_projections(core, weights, raw, beta_raw):
    nc = core.nc
    w = weights.rearrange("p k n -> p (k n)")
    words = w.shape[1]
    hi, lo = core.w_hi[:, 0, 0:words], core.w_lo[:, 0, 0:words]
    with stage(nc, "weights_rounded", "weights_split", "projected", "stored") as (
            block, weights_rounded, weights_split, projected, stored):
        @block.scalar
        def _(act):
            nc.scalar.activation(hi, w, ACT.Copy).then_inc(weights_rounded, 1)

        @block.tensor
        def _(pe):
            pe.wait_ge(weights_split, 1)
            for k in range(KD):
                s = slice(k * SMALL_COLS, (k + 1) * SMALL_COLS)
                mm = three_passes(nc, core.bank(0)[0:SMALL_COLS, :], (hi[:, s], lo[:, s]),
                                  (core.h_hi[:, k, :], core.h_lo[:, k, :]), start=(k == 0), stop=(k == KD - 1))
            mm.then_inc(projected, 1)

        @block.vector
        def _(dve):
            dve.wait_ge(weights_rounded, 1)
            nc.vector.tensor_tensor(lo, w, hi.bitcast(F32), ALU.subtract).then_inc(weights_split, 1)
            dve.wait_ge(projected, 1)
            nc.vector.tensor_copy(raw, core.bank(0)[0:ROWS, :]).then_inc(stored, 1)
            nc.vector.tensor_copy(beta_raw, core.bank(0)[BETA_ROW:SMALL_COLS, :]).then_inc(stored, 1)


def decay_stage(core, raw, beta_raw, bias_col, log_col, steps_row, sums, delta_rows, at):
    nc = core.nc
    neg, e, z, z2, series, one = (core.work(at + T * n, T)[0:ROWS] for n in range(6))
    with stage(nc, "decay_steps", "ready", "exp_done", "coefficient", "beta_done") as (
            block, decay_steps, ready, exp_done, coefficient, beta_done):
        @block.scalar
        def _(act):
            nc.scalar.activation(log_col, log_col, ACT.Exp).then_inc(coefficient, 1)
            act.wait_ge(ready, 1)
            nc.scalar.activation(e, neg, ACT.Exp).then_inc(exp_done, 1)
            nc.scalar.activation(delta_rows[:, 1, :], beta_raw, ACT.Sigmoid).then_inc(beta_done, 1)

        @block.vector
        def _(dve):
            v = nc.vector
            s = Count(dve, decay_steps)
            s.step(v.memset(one, 1.0))
            s.link(v.tensor_scalar(raw, raw, bias_col, None, ALU.add))
            s.link(v.tensor_scalar(neg, raw, -1.0, None, ALU.mult))
            s.link(v.tensor_tensor(neg, neg, raw, ALU.min))
            v.tensor_scalar(raw, raw, 0.0, None, ALU.max).then_inc(ready, 1)
            dve.wait_ge(exp_done, 1)
            dve.wait_ge(ready, 1)
            s.link(v.tensor_scalar(z2, e, 2.0, None, ALU.add))
            s.link(v.reciprocal(neg, z2))
            s.link(v.tensor_tensor(z, e, neg, ALU.mult))
            s.link(v.tensor_tensor(z2, z, z, ALU.mult))
            s.link(v.tensor_scalar(series, z2, 1.0 / (2 * LOG_TERMS + 1), None, ALU.mult))
            for k in range(LOG_TERMS - 1, 0, -1):
                s.link(v.scalar_tensor_tensor(out=series, in0=series, scalar=1.0 / (2 * k + 1), in1=z2,
                                              op0=ALU.add, op1=ALU.mult))
            s.link(v.scalar_tensor_tensor(out=series, in0=series, scalar=1.0, in1=z, op0=ALU.add, op1=ALU.mult))
            s.link(v.scalar_tensor_tensor(out=steps_row, in0=series, scalar=2.0, in1=raw, op0=ALU.mult, op1=ALU.add))
            dve.wait_ge(coefficient, 1)
            s.link(v.tensor_scalar(neg, steps_row, log_col, -1.0, ALU.mult, ALU.mult))
            for j, (lo, w) in enumerate(SPANS):
                s.step(v.tensor_tensor_scan(sums[:, lo:lo + w], one[:, 0:w], neg[:, T - w:T], 0.0,
                                            ALU.mult, ALU.add))
            s.settle()
            for j, (lo, w) in enumerate(SPANS):
                s.step(v.tensor_copy(delta_rows[:, 0, j * P:(j + 1) * P], sums[G_ROW:G_ROW + G_HEADS, lo:lo + P]))


def ssd_stage(core, ones, pick, b_T, c_T, xs, xdt, sums, sums_tok, d_skip, keep, y, at, following):
    nc = core.nc
    gram = core.work(at, S_GROUPS, SPAN_WORDS)
    decay = core.ring(2 * UNIT, 2, SPAN_WORDS)
    one_row = core.ring(2 * UNIT + 2 * SPAN_WORDS, 2, SPAN_WORDS)[0:S_HEADS]
    per_group = S_HEADS // S_GROUPS
    with stage(nc, "gram_ready", "gram_stored", "gram_masked") as (block, gram_ready, gram_stored, gram_masked):
        @block.tensor
        def _(pe):
            for g in range(S_GROUPS):
                for j, (lo, w) in enumerate(SPANS):
                    nc.tensor.matmul(core.bank(g * TT + j)[:, 0:w], b_T[:, g, j * P:(j + 1) * P],
                                     c_T[:, g, j * P:T], start=True, stop=True).then_inc(gram_ready, 1)

        @block.vector
        def _(dve):
            for g in range(S_GROUPS):
                for j, (lo, w) in enumerate(SPANS):
                    dve.wait_ge(gram_ready, g * TT + j + 1)
                    if w > P:
                        nc.vector.tensor_copy(gram[:, g, lo + P:lo + w], core.bank(g * TT + j)[:, P:w]
                                              ).then_inc(gram_stored, 1)
                    nc.vector.tensor_tensor(gram[:, g, lo:lo + P], core.bank(g * TT + j)[:, 0:P], keep,
                                            ALU.mult).then_inc(gram_masked, 1)

    with stage(nc, "row_ready", "spread", "spread_read", "decayed", "weighted", "output", "output_stored", "following_in",
               from_one=("spread", "spread_read", "output", "output_stored")) as (
            block, row_ready, spread, spread_read, decayed, weighted, output, output_stored, following_in):
        U = per_group
        bodies = S_HEADS // U

        @block.sync
        def _(sp):
            for half, (rows, src) in enumerate(following):
                sp.dma_start(core.raw(half, rows)[:, :, 0:src.shape[2]], src).then_inc(following_in, 16)
            sp.wait_ge(following_in, 32)

        @block.gpsimd
        def _(pool):
            with pool.Fori(0, bodies) as i:
                for u in range(U):
                    hold(pool, spread, TT * (U * i + u - 1) + 1 if u >= 1 else TT * U * i + 1)
                    own = pick[0:S_HEADS, bass.ds(U * i + u, 1)].broadcast_to([S_HEADS, SPAN_WORDS])
                    nc.gpsimd.tensor_tensor(one_row[:, u % 2, :], sums[0:S_HEADS, :], own, ALU.mult).then_inc(row_ready, 1)

        @block.tensor
        def _(pe):
            with pe.Fori(0, bodies) as i:
                for n in range(U + 1):
                    if n < U:
                        h = U * i + n
                        pe.wait_ge(row_ready, h + 1)
                        for j, (lo, w) in enumerate(SPANS):
                            pe.wait_ge(spread_read, TT * (h - 1) + j + 2 if n else TT * h + 1)
                            nc.tensor.matmul(core.bank(j)[:, 0:w], ones[0:S_HEADS, :],
                                             one_row[:, n % 2, lo:lo + w], start=True, stop=True).then_inc(spread, 1)
                    if n:
                        h, b = U * i + n - 1, 4 + (n - 1) % 2
                        pe.wait_ge(weighted, h + 1)
                        pe.wait_ge(output_stored, h if n >= 3 else U * i + 1)
                        for t in range(TT):
                            for j in range(t + 1):
                                at_j = SPANS[j][0] + (t - j) * P
                                mm = nc.tensor.matmul(core.bank(b)[:, t * DH:(t + 1) * DH],
                                                      decay[:, (n - 1) % 2, at_j:at_j + P],
                                                      xdt[:, j, bass.ds(h * DH, DH)], start=(j == 0), stop=(j == t))
                        mm.then_inc(output, 1)

        @block.scalar
        def _(act):
            with act.Fori(0, bodies) as i:
                for u in range(U):
                    h, d = U * i + u, decay[:, u % 2, :]
                    act.wait_ge(output, h if u >= 2 else U * i + 1)
                    for j, (lo, w) in enumerate(SPANS):
                        hold(act, spread, TT * h + j + 2)
                        nc.scalar.activation(d[:, lo:lo + w], core.bank(j)[:, 0:w], ACT.Relu, scale=-1.0,
                                             bias=sums_tok[:, j, bass.ds(h, 1)]).then_inc(spread_read, 1)
                    act.wait_ge(spread_read, TT * h + TT + 1)
                    nc.scalar.activation(d, d, ACT.Exp, scale=-1.0).then_inc(decayed, 1)

        @block.vector
        def _(dve):
            assert per_group % U == 0
            with dve.Fori(0, bodies) as i:
                for n in range(U + 1):
                    if n < U:
                        dve.wait_ge(decayed, U * i + n + 1)
                        nc.vector.tensor_tensor(decay[:, n % 2, :], decay[:, n % 2, :],
                                                gram[:, i // (per_group // U), :], ALU.mult).then_inc(weighted, 1)
                    if n:
                        h = U * i + n - 1
                        dve.wait_ge(output, h + 2)
                        nc.vector.scalar_tensor_tensor(
                            out=y[:, :, bass.ds(h * DH, DH)], in0=xs[:, :, bass.ds(h * DH, DH)],
                            scalar=d_skip[:, bass.ds(h, 1)],
                            in1=core.bank(4 + (n - 1) % 2)[:, 0:TT * DH].rearrange("p (t d) -> p t d", t=TT),
                            op0=ALU.mult, op1=ALU.add).then_inc(output_stored, 1)


def multiply_stage(core, jobs):
    nc = core.nc
    with stage(nc, "multiplied") as (block, multiplied):
        @block.gpsimd
        def _(pool):
            out, a, b = jobs[-1]
            nc.gpsimd.tensor_tensor(out, a, b, ALU.mult).then_inc(multiplied, 1)

        @block.vector
        def _(dve):
            for out, a, b in jobs[:-1]:
                nc.vector.tensor_tensor(out, a, b, ALU.mult).then_inc(multiplied, 1)


def unit_stage(core, ones, ident, x, n, queries):
    nc = core.nc
    sq = core.ring(0, 4, T)
    sums, root, factors = (core.ring((4 + m) * T, T)[0:n] for m in range(3))
    hot = core.ring(7 * T, 2 * n - 1)
    rows = core.ring(7 * T + 2 * n, n, P)[0:n]
    with stage(nc, "cleared", "hot_ready", "rows_ready", "squared_pool", "squared_act", "summed", "sum_ready",
               "root_ready", "inverted", "spread", "scaled") as (
            block, cleared, hot_ready, rows_ready, squared_pool, squared_act, summed, sum_ready, root_ready,
            inverted, spread, scaled):
        def squares(engine, parity, put, sem):
            for m in range(parity, n, 2):
                if m >= 4:
                    engine.wait_ge(summed, m - 3)
                put(sq[:, m % 4, :], x[:, m, :]).then_inc(sem, 1)

        @block.gpsimd
        def _(pool):
            nc.gpsimd.memset(hot, 0.0).then_inc(cleared, 1)
            pool.wait_ge(cleared, 1)
            nc.gpsimd.memset(hot[:, n - 1:n], 1.0).then_inc(hot_ready, 1)
            squares(pool, 1, lambda to, v: nc.gpsimd.tensor_tensor(to, v, v, ALU.mult), squared_pool)

        @block.tensor
        def _(pe):
            pe.wait_ge(hot_ready, 1)
            for m in range(n):
                pe.wait_ge((squared_act, squared_pool)[m % 2], m // 2 + 1)
                nc.tensor.matmul(core.bank(0)[0:n, :], hot[:, n - 1 - m:2 * n - 1 - m], sq[:, m % 4, :],
                                 start=(m == 0), stop=(m == n - 1)).then_inc(summed, 1)
            pe.wait_ge(rows_ready, 1)
            pe.wait_ge(inverted, 1)
            for m in range(n):
                if m >= 4:
                    pe.wait_ge(scaled, m - 3)
                nc.tensor.matmul(core.bank(1 + m % 4), rows[:, m, :], factors, start=True, stop=True
                                 ).then_inc(spread, 1)

        @block.scalar
        def _(act):
            squares(act, 0, lambda to, v: nc.scalar.activation(to, v, ACT.Square), squared_act)
            act.wait_ge(sum_ready, 1)
            nc.scalar.activation(root, sums, ACT.Sqrt).then_inc(root_ready, 1)

        @block.vector
        def _(dve):
            nc.vector.tensor_copy(rows, ident[0:n, 0:n].unsqueeze(2).broadcast_to([n, n, P])).then_inc(rows_ready, 1)
            dve.wait_ge(summed, n)
            nc.vector.tensor_scalar(sums, core.bank(0)[0:n, :], EPS, None, ALU.add).then_inc(sum_ready, 1)
            dve.wait_ge(root_ready, 1)
            nc.vector.reciprocal(factors, root).then_inc(inverted, 1)
            for m in range(n):
                dve.wait_ge(spread, m + 1)
                scale = G_DIM ** -0.5 if m < queries else 1.0
                nc.vector.scalar_tensor_tensor(out=x[:, m, :], in0=x[:, m, :], scalar=scale, in1=core.bank(1 + m % 4),
                                               op0=ALU.mult, op1=ALU.mult).then_inc(scaled, 1)


def delta_prepare(core, ones, pick, q_T, k_T, delta_rows, sums_tok, keep, couple_T, attn_T, last_sum, last_decay):
    nc = core.nc
    one_row = core.ring(0, 2, 2 * T)[0:G_HEADS]
    kb = core.ring(4 * T, 2, T)
    dec = core.ring(6 * T, 2, T)
    eg = core.ring(8 * T, 2, T)
    k_static = core.ring(10 * T, 2, T)
    with stage(nc, "row_ready", "spread", "sums_read", "exp_ready", "keys_scaled", "products", "differences", "decay_ready",
               "decay_kept", "used", "lasts", from_one=("spread", "used", "products")) as (
            block, row_ready, spread, sums_read, exp_ready, keys_scaled, products, differences, decay_ready, decay_kept, used, lasts):
        bodies = G_HEADS // 2

        @block.gpsimd
        def _(pool):
            with pool.Fori(0, bodies) as i:
                for u in range(2):
                    h = 2 * i + u
                    hold(pool, spread, 4 * i + 1)
                    own = pick[0:G_HEADS, bass.ds(h, 1)].broadcast_to([G_HEADS, 2 * T])
                    nc.gpsimd.tensor_tensor(one_row[:, u, :], delta_rows.rearrange("p a b -> p (a b)"), own,
                                            ALU.mult).then_inc(row_ready, 1)
                for u in range(2):
                    h = 2 * i + u
                    pool.wait_ge(decay_ready, h + 1)
                    d = dec[:, u, :].rearrange("p (t i) -> p t i", t=TT)
                    nc.gpsimd.tensor_tensor(d, d, keep.unsqueeze(1).broadcast_to([P, TT, P]), ALU.mult).then_inc(decay_kept, 1)

        @block.tensor
        def _(pe):
            with pe.Fori(0, bodies) as i:
                for u in range(2):
                    h = 2 * i + u
                    pe.wait_ge(row_ready, h + 1)
                    pe.wait_ge(used, 6 * i + 1)
                    for c in range(2):
                        nc.tensor.matmul(core.bank(4 * u + c), ones[0:G_HEADS, :], one_row[:, u, c * T:(c + 1) * T],
                                         start=True, stop=True).then_inc(spread, 1)
                for u in range(2):
                    h = 2 * i + u
                    pe.wait_ge(keys_scaled, 2 * h + 2)
                    for c in range(2):
                        for t in range(TT):
                            s = slice(t * P, (t + 1) * P)
                            mm = nc.tensor.matmul(core.bank(4 * u + 2 + c)[:, s], k_static[:, u, s],
                                                  q_T[:, h, s] if c else kb[:, u, s], start=True, stop=True)
                        mm.then_inc(products, 1)

        @block.scalar
        def _(act):
            with act.Fori(0, bodies) as i:
                for u in range(2):
                    h = 2 * i + u
                    act.wait_ge(spread, 4 * i + 2 * u + 2)
                    hold(act, used, 6 * i + 1)
                    for t in range(TT):
                        nc.scalar.activation(dec[:, u, t * P:(t + 1) * P], core.bank(4 * u)[:, t * P:(t + 1) * P],
                                             ACT.Relu, scale=-1.0, bias=sums_tok[:, t, bass.ds(G_ROW + h, 1)]
                                             ).then_inc(differences, 1)
                    act.wait_ge(differences, TT * h + TT)
                    nc.scalar.activation(dec[:, u, :], dec[:, u, :], ACT.Exp, scale=-1.0).then_inc(decay_ready, 1)
                    nc.scalar.copy(last_sum[:, h, :], core.bank(4 * u)[:, P - 1:T:P]).then_inc(exp_ready, 1)
                    nc.scalar.activation(eg[:, u, :], core.bank(4 * u), ACT.Exp).then_inc(exp_ready, 1)

        @block.vector
        def _(dve):
            with dve.Fori(0, bodies) as i:
                for u in range(2):
                    h = 2 * i + u
                    dve.wait_ge(spread, 4 * i + 2 * u + 3)
                    dve.wait_ge(products, 4 * i + 1)
                    nc.vector.tensor_tensor(kb[:, u, :], k_T[:, h, :], core.bank(4 * u + 1), ALU.mult).then_inc(keys_scaled, 1)
                    nc.vector.tensor_copy(k_static[:, u, :], k_T[:, h, :]).then_inc(keys_scaled, 1)
                for u in range(2):
                    h = 2 * i + u
                    dve.wait_ge(decay_kept, h + 1)
                    dve.wait_ge(products, 2 * h + 2)
                    nc.vector.tensor_tensor(couple_T[:, h, :], dec[:, u, :], core.bank(4 * u + 2), ALU.mult).then_inc(used, 1)
                    dve.wait_ge(products, 2 * h + 3)
                    nc.vector.tensor_tensor(attn_T[:, h, :], dec[:, u, :], core.bank(4 * u + 3), ALU.mult).then_inc(used, 1)
                    dve.wait_ge(exp_ready, 2 * h + 2)
                    nc.vector.tensor_copy(last_decay[:, h, :], eg[:, u, P - 1:T:P]).then_inc(lasts, 1)
                    nc.vector.tensor_tensor(q_T[:, h, :], q_T[:, h, :], eg[:, u, :], ALU.mult).then_inc(used, 1)


def delta_solve(core, ident, level_masks, couple_T, inverse_T):
    nc = core.nc
    levels = level_masks.shape[1]
    last = levels - 1
    inv = core.ring(0, 2, T)
    inv_T = core.ring(2 * T, 2, T)
    join = core.ring(4 * T, 4, T)
    part = core.ring(8 * T, 2, T)
    products_n, stored_n, updates_n, updated_n = 2 * levels, 2 * last, 4 * (last - 1) + 2, 4 * last + 2
    product_at = lambda l, u: 2 * l + u + 1
    stored_at = lambda l, u: 2 * (l - 1) + u + 1
    updates_at = lambda l, u: 4 * (l - 1) + (2 * u + 2 if l < last else u + 1)
    updated_at = lambda l, u: 4 * l + (2 * u + 2 if l < last else u + 1)
    tiled = lambda v: v.rearrange("p (t i) -> p t i", t=TT)
    with stage(nc, "joined", "part_ready", "part_stored", "updates", "updated", from_one=("part_ready",)) as (
            block, joined, part_ready, part_stored, updates, updated):
        bodies = G_HEADS // 2

        @block.gpsimd
        def _(pool):
            with pool.Fori(0, bodies) as i:
                for n in range(2 * levels):
                    l, u = n // 2, n % 2
                    if l == 2:
                        pool.wait_ge(updated, updated_n * i + updated_at(0, u))
                    hold(pool, part_ready, products_n * i + max(n - 3, 0) + 1)
                    nc.gpsimd.tensor_tensor(tiled(join[:, 2 * u + l % 2, :]), tiled(couple_T[:, 2 * i + u, :]),
                                            level_masks[:, l, :].unsqueeze(1).broadcast_to([P, TT, P]),
                                            ALU.mult).then_inc(joined, 1)

        @block.tensor
        def _(pe):
            def product(bank, left, right):
                for t in range(TT):
                    s = slice(t * P, (t + 1) * P)
                    mm = nc.tensor.matmul(core.bank(bank)[:, s], left[:, s], ident if right is None else right[:, s],
                                          start=True, stop=True)
                return mm
            with pe.Fori(0, bodies) as i:
                for l in range(levels):
                    for u in range(2):
                        pe.wait_ge(joined, products_n * i + product_at(l, u))
                        if l:
                            pe.wait_ge(updated, updated_n * i + updated_at(l - 1, u) - 1)
                        product(4 * u, join[:, 2 * u + l % 2, :], inv[:, u, :] if l else None).then_inc(part_ready, 1)
                    for u in range(2 if l else 0):
                        pe.wait_ge(part_stored, stored_n * i + stored_at(l, u))
                        pe.wait_ge(updated, updated_n * i + updated_at(l - 1, u))
                        if l < last:
                            product(4 * u + 1, inv_T[:, u, :], part[:, u, :]).then_inc(updates, 1)
                        product(4 * u + 2, part[:, u, :], inv_T[:, u, :]).then_inc(updates, 1)

        @block.scalar
        def _(act):
            with act.Fori(0, bodies) as i:
                for l in range(1, levels):
                    for u in range(2):
                        act.wait_ge(part_ready, products_n * i + product_at(l, u) + 1)
                        nc.scalar.copy(part[:, u, :], core.bank(4 * u)).then_inc(part_stored, 1)

        @block.vector
        def _(dve):
            eye = ident.unsqueeze(1).broadcast_to([P, TT, P])
            with dve.Fori(0, bodies) as i:
                for u in range(2):
                    dve.wait_ge(part_ready, products_n * i + product_at(0, u) + 1)
                    nc.vector.tensor_tensor(tiled(inv[:, u, :]), eye, tiled(core.bank(4 * u)),
                                            ALU.subtract).then_inc(updated, 1)
                    nc.vector.tensor_tensor(tiled(inv_T[:, u, :]), eye, tiled(join[:, 2 * u, :]),
                                            ALU.subtract).then_inc(updated, 1)
                for l in range(1, levels):
                    for u in range(2):
                        dve.wait_ge(updated, updated_n * i + updated_at(l - 1, u))
                        if l < last:
                            dve.wait_ge(updates, updates_n * i + updates_at(l, u) - 1)
                            nc.vector.tensor_tensor(inv[:, u, :], inv[:, u, :], core.bank(4 * u + 1),
                                                    ALU.subtract).then_inc(updated, 1)
                        dve.wait_ge(updates, updates_n * i + updates_at(l, u))
                        to = inverse_T[:, 2 * i + u, :] if l == last else inv_T[:, u, :]
                        nc.vector.tensor_tensor(to, inv_T[:, u, :], core.bank(4 * u + 2), ALU.subtract).then_inc(updated, 1)
                dve.wait_ge(updated, updated_n * i + updated_n)


def delta_inputs(core, k_tok, v_tok, beta_tok, sums_tok, last_sum, inverse_T, minus_w_T, tail_k):
    nc = core.nc
    k_in = core.ring(0, TT, D)
    factor = core.ring(TT * D, 3, TT * G_HEADS)
    heads = lambda x: x.rearrange("p t (h d) -> p t h d", h=G_HEADS)
    wide = lambda f: f.rearrange("p (t h) -> p t h", t=TT).unsqueeze(3).broadcast_to([P, TT, G_HEADS, G_DIM])
    with stage(nc, "exp_sum", "rest", "exp_rest", "input_ready", "factor_ready", "scaled", "w_ready", "w_stored") as (
            block, exp_sum, rest, exp_rest, input_ready, factor_ready, scaled, w_ready, w_stored):
        f = lambda n: factor[:, n, :].rearrange("p (t h) -> p t h", t=TT)
        gsum = sums_tok[:, :, G_ROW:G_ROW + G_HEADS]

        @block.scalar
        def _(act):
            nc.scalar.activation(f(0), gsum, ACT.Exp).then_inc(exp_sum, 1)
            act.wait_ge(rest, 1)
            nc.scalar.activation(f(1), f(1), ACT.Exp).then_inc(exp_rest, 1)
            for h in range(G_HEADS):
                act.wait_ge(w_ready, h + 1)
                nc.scalar.activation(minus_w_T[:, h, :], core.bank(h), ACT.Copy, scale=-1.0).then_inc(w_stored, 1)

        @block.vector
        def _(dve):
            nc.vector.tensor_tensor(f(1), last_sum.rearrange("p h t -> p t h"), gsum, ALU.subtract).then_inc(rest, 1)
            dve.wait_ge(exp_sum, 1)
            nc.vector.tensor_tensor(f(2), f(0), beta_tok, ALU.mult).then_inc(factor_ready, 1)
            dve.wait_ge(factor_ready, 1)
            nc.vector.tensor_tensor(heads(k_in), heads(k_tok), wide(factor[:, 2, :]), ALU.mult).then_inc(input_ready, 1)
            nc.vector.tensor_tensor(heads(v_tok), heads(v_tok),
                                    beta_tok.unsqueeze(3).broadcast_to([P, TT, G_HEADS, G_DIM]),
                                    ALU.mult).then_inc(scaled, 1)

        @block.gpsimd
        def _(pool):
            pool.wait_ge(exp_rest, 1)
            nc.gpsimd.tensor_tensor(heads(tail_k), heads(k_tok), wide(factor[:, 1, :]), ALU.mult).then_inc(scaled, 1)

        @block.tensor
        def _(pe):
            pe.wait_ge(input_ready, 1)
            for h in range(G_HEADS):
                for t in range(TT):
                    mm = nc.tensor.matmul(core.bank(h)[:, t * P:(t + 1) * P], k_in[:, t, h * G_DIM:(h + 1) * G_DIM],
                                          inverse_T[:, h, t * P:(t + 1) * P], start=True, stop=True)
                mm.then_inc(w_ready, 1)


def delta_scan(core, q_T, v_tok, tail_k, inverse_T, minus_w_T, attn_T, last_decay, out):
    nc = core.nc
    state = core.ring(0, G_HEADS, G_DIM)
    fresh = core.ring(G_HEADS * G_DIM, 2, G_DIM)
    with stage(nc, "cleared", "fresh_ready", "fresh_stored", "out_ready", "step_ready", "out_stored", "state_ready") as (
            block, cleared, fresh_ready, fresh_stored, out_ready, step_ready, out_stored, state_ready):
        order = [(t, h) for t in range(TT) for h in range(G_HEADS)]

        @block.gpsimd
        def _(pool):
            nc.gpsimd.memset(state, 0.0).then_inc(cleared, 1)

        @block.tensor
        def _(pe):
            pe.wait_ge(cleared, 1)

            def finish(n):
                t, h = order[n]
                s = slice(t * P, (t + 1) * P)
                pe.wait_ge(fresh_stored, n + 1)
                if n >= 2:
                    pe.wait_ge(out_stored, n - 1)
                    pe.wait_ge(state_ready, n - 1)
                b = core.bank(2 + n % 2)[:, 0:G_DIM]
                nc.tensor.matmul(b, q_T[:, h, s], state[:, h, :], start=True, stop=False)
                nc.tensor.matmul(b, attn_T[:, h, s], fresh[:, n % 2, :], start=False, stop=True).then_inc(out_ready, 1)
                nc.tensor.matmul(core.bank(4 + n % 2)[:, 0:G_DIM], tail_k[:, t, h * G_DIM:(h + 1) * G_DIM],
                                 fresh[:, n % 2, :], start=True, stop=True).then_inc(step_ready, 1)

            for n, (t, h) in enumerate(order):
                s = slice(t * P, (t + 1) * P)
                if n >= 2:
                    pe.wait_ge(fresh_stored, n - 1)
                if n >= G_HEADS:
                    pe.wait_ge(state_ready, n - G_HEADS + 1)
                b = core.bank(n % 2)[:, 0:G_DIM]
                nc.tensor.matmul(b, inverse_T[:, h, s], v_tok[:, t, h * G_DIM:(h + 1) * G_DIM], start=True, stop=False)
                nc.tensor.matmul(b, minus_w_T[:, h, s], state[:, h, :], start=False, stop=True).then_inc(fresh_ready, 1)
                if n:
                    finish(n - 1)
            finish(len(order) - 1)

        @block.scalar
        def _(act):
            for n in range(len(order)):
                act.wait_ge(fresh_ready, n + 1)
                if n >= 2:
                    act.wait_ge(step_ready, n - 1)
                nc.scalar.copy(fresh[:, n % 2, :], core.bank(n % 2)[:, 0:G_DIM]).then_inc(fresh_stored, 1)

        @block.vector
        def _(dve):
            for n, (t, h) in enumerate(order):
                dve.wait_ge(step_ready, n + 1)
                dve.wait_ge(out_ready, n + 1)
                nc.vector.scalar_tensor_tensor(out=state[:, h, :], in0=state[:, h, :],
                                               scalar=last_decay[:, h, t:t + 1],
                                               in1=core.bank(4 + n % 2)[:, 0:G_DIM],
                                               op0=ALU.mult, op1=ALU.add).then_inc(state_ready, 1)
                nc.vector.tensor_copy(out[:, t, h * G_DIM:(h + 1) * G_DIM], core.bank(2 + n % 2)[:, 0:G_DIM]
                                      ).then_inc(out_stored, 1)


def third_block(core, a, ident, ones):
    nc = core.nc
    KX, KQ = XBC // P, QKV // P
    cols = core.const(4 * KD + 1)
    conv_s = core.const(CONV_K * KX + KX)
    conv_g = core.const(CONV_K * KQ + KQ)
    keep = core.const(P)
    masks = core.const(7, P)
    d_skip = core.const(S_HEADS)
    bias_col, log_col = core.const(1)[0:ROWS], core.const(1)[0:ROWS]
    sums_tok = core.const(TT, ROWS)
    steps_tok = core.const(TT, S_HEADS)
    beta_tok = core.const(TT, G_HEADS)
    last_sum, last_decay = core.const(G_HEADS, TT), core.const(G_HEADS, TT)
    w_in = columns_of(a["w_in_3"][0])
    section = lambda col: lambda k, lo, n: w_in(k, lo + col, n)
    rows = lambda v: v.rearrange("(k p) -> k p", p=P)
    small_w = core.ring(0, KD, SMALL_COLS)
    with stage(nc, "cleared") as (block, cleared):
        @block.gpsimd
        def _(pool):
            nc.gpsimd.memset(conv_g[:, CONV_K * KQ:(CONV_K + 1) * KQ], 0.0).then_inc(cleared, 1)
            nc.gpsimd.memset(bias_col, 0.0).then_inc(cleared, 1)
            nc.gpsimd.memset(small_w, 0.0).then_inc(cleared, 1)
            nc.gpsimd.memset(log_col, 0.0).then_inc(cleared, 1)
    column = lambda v: v.unsqueeze(1)
    w = a["w_in_3"][0].rearrange("(k p) n -> p k n", p=P)
    loads = ([(keep, a["upper"]), (masks, a["levels"].rearrange("l p i -> p l i")),
                    (d_skip, a["ssm_d_3"][0].partition_broadcast(P)),
                    (bias_col[0:S_HEADS], column(a["ssm_dt_bias_3"][0])),
                    (bias_col[G_ROW:G_ROW + G_HEADS], column(a["gdn_dt_bias_3"][0])),
                    (log_col[0:S_HEADS], column(a["ssm_a_log_3"][0])),
                    (log_col[G_ROW:G_ROW + G_HEADS], column(a["gdn_a_log_3"][0]))]
               + [(small_w[:, :, to:to + n], w[:, :, col:col + n]) for to, col, n in (
                   (0, DT_COL, S_HEADS), (G_ROW, AB_COL, G_HEADS), (BETA_ROW, AB_COL + G_HEADS, G_HEADS))])
    load_columns(core, 0, [
        ([rows(a["norm_mix_w_3"][0]), rows(a["ssm_norm_w_3"][0]), rows(a["norm_ffn_w_3"][0]),
          rows(a["final_norm_w_3"]), a["gdn_norm_w_3"]], cols),
        ([a["ssm_conv_w_3"][0].rearrange("w (f p) -> (w f) p", p=P), rows(a["ssm_conv_b_3"][0])], conv_s),
        ([a["gdn_conv_w_3"][0].rearrange("w (f p) -> (w f) p", p=P)], conv_g[:, 0:CONV_K * KQ])], ident, loads)
    norm_stage(core, ones, cols[:, 0:KD])

    merged = core.work(0, KD, T)
    delta_rows = core.work(24576, 2, T)[0:G_HEADS]
    raw, steps_row = core.work(8192, T)[0:ROWS], core.work(8192 + T, T)[0:ROWS]
    beta_raw = core.work(8192 + 2 * T, T)[0:G_HEADS]
    sums = core.work(18432 + 2 * SPAN_WORDS, SPAN_WORDS)[0:ROWS]
    small_projections(core, small_w, raw, beta_raw)
    decay_stage(core, raw, beta_raw, bias_col, log_col, steps_row, sums, delta_rows, 8192 + 3 * T)
    flip(core, [([sums[:, lo:lo + P] for lo, _ in SPANS], sums_tok.rearrange("p t h -> p (t h)"), 1.0),
                ([steps_row[0:S_HEADS, t * P:(t + 1) * P] for t in range(TT)],
                 steps_tok.rearrange("p t h -> p (t h)"), 1.0),
                ([delta_rows[:, 1, t * P:(t + 1) * P] for t in range(TT)],
                 beta_tok.rearrange("p t h -> p (t h)"), 1.0)], ident,
         following=first_columns(section(XBC_COL), XBC))

    xbc = core.work(0, KX, T)
    xs, xdt = core.work(6144, TT, S_INNER), core.work(10240, TT, S_INNER)
    y = core.work(14336, TT, S_INNER)
    project(core, section(XBC_COL), XBC, xbc, ACT.Silu,
            conv=(conv_s[:, 0:CONV_K * KX], conv_s[:, CONV_K * KX:(CONV_K + 1) * KX]), prepared=LOADED)
    flip(core, [([xbc[:, 4 * g + k, t * P:(t + 1) * P] for k in range(4)], xs[:, t, g * 4 * P:(g + 1) * 4 * P], 1.0)
                for t in range(TT) for g in range(2)], ident)
    by_head = lambda v: v.rearrange("p t (h d) -> p t h d", h=S_HEADS)
    multiply_stage(core, [(by_head(xdt)[:, t], by_head(xs)[:, t],
                           steps_tok[:, t, :].unsqueeze(2).broadcast_to([P, S_HEADS, DH])) for t in range(TT)])
    ssd_stage(core, ones, ident, xbc[:, 8:10, :], xbc[:, 10:12, :], xs, xdt, sums, sums_tok, d_skip, keep, y, 18432,
              first_columns(section(Z_COL), S_INNER))
    z = core.work(0, TT, S_INNER)
    project(core, section(Z_COL), S_INNER, z, ACT.Silu, to_tokens=True, prepared=LOADED)
    multiply_stage(core, [(y[:, t], y[:, t], z[:, t]) for t in range(TT)])
    head_norms(core, [y.rearrange("p t (g w) -> p t g w", g=S_GROUPS)], 18432, following=first_columns(section(GATE_S_COL), D))
    y_T = core.work(4096, KD, T)
    flip(core, [([y[:, t, k * P:(k + 1) * P] for t in range(TT)], y_T[:, k, :], cols[:, KD + k:KD + k + 1])
                for k in range(KD)], ident, following=first_columns(section(GATE_S_COL), D), loaded=True)
    gate = core.work(8192, KD, T)
    w_proj_s, w_proj_g, w_out = (rows_of(a[n][0]) for n in ("w_proj_ssm_3", "w_proj_gdn_3", "w_out_3"))
    project(core, section(GATE_S_COL), D, gate, ACT.Sigmoid, prepared=SPLIT, following=first_rows(w_proj_s))
    rows_product(core, y_T, KD, w_proj_s,
                 lambda m: nc.vector.tensor_tensor(merged[:, m, :], gate[:, m, :], core.bank(m), ALU.mult),
                 prepared=SPLIT, following=first_columns(section(QKV_COL), QKV))

    qkv = core.work(4096, KQ, T)
    q_T, k_T, v_T = (qkv[:, n * G_HEADS:(n + 1) * G_HEADS, :] for n in range(3))
    k_tok, v_tok = core.work(16384, TT, D), core.work(20480, TT, D)
    couple_T, attn_T = core.cut(H_AT, G_HEADS, T), core.cut(H_AT + G_HEADS * T, G_HEADS, T)
    project(core, section(QKV_COL), QKV, qkv, ACT.Silu,
            conv=(conv_g[:, 0:CONV_K * KQ], conv_g[:, CONV_K * KQ:(CONV_K + 1) * KQ]), prepared=SPLIT)
    unit_stage(core, ones, ident, qkv, 2 * G_HEADS, G_HEADS)
    flip(core, [([src[:, 4 * g + k, t * P:(t + 1) * P] for k in range(4)], dst[:, t, g * 4 * P:(g + 1) * 4 * P], 1.0)
                for src, dst in ((k_T, k_tok), (v_T, v_tok)) for t in range(TT) for g in range(2)], ident)
    delta_prepare(core, ones, ident, q_T, k_T, delta_rows, sums_tok, keep, couple_T, attn_T, last_sum, last_decay)
    inverse_T = v_T
    delta_solve(core, ident, masks, couple_T, inverse_T)
    minus_w_T, tail_k = k_T, core.cut(H_AT, TT, D)
    delta_inputs(core, k_tok, v_tok, beta_tok, sums_tok, last_sum, inverse_T, minus_w_T, tail_k)
    o = k_tok
    delta_scan(core, q_T, v_tok, tail_k, inverse_T, minus_w_T, attn_T, last_decay, o)
    norm_stage(core, ones, cols[:, 0:KD], following=first_columns(section(GZ_COL), D))
    gz = core.work(20480, TT, D)
    project(core, section(GZ_COL), D, gz, ACT.Silu, to_tokens=True, prepared=SPLIT)
    head_norms(core, [o.rearrange("p t (h d) -> p t h d", h=G_HEADS)], 8192, following=first_columns(section(GATE_G_COL), D))
    multiply_stage(core, [(o[:, t], o[:, t], gz[:, t]) for t in range(TT)])
    o_T = core.work(4096, KD, T)
    flip(core, [([o[:, t, k * P:(k + 1) * P] for t in range(TT)], o_T[:, k, :], cols[:, 4 * KD:4 * KD + 1])
                for k in range(KD)], ident, following=first_columns(section(GATE_G_COL), D), loaded=True)
    project(core, section(GATE_G_COL), D, gate, ACT.Sigmoid, prepared=SPLIT, following=first_rows(w_proj_g))
    rows_product(core, o_T, KD, w_proj_g,
                 lambda m: nc.vector.tensor_tensor(gate[:, m, :], gate[:, m, :], core.bank(m), ALU.mult),
                 prepared=SPLIT, following=first_rows(w_out))
    with stage(nc, "added") as (block, added):
        @block.vector
        def _(dve):
            for m in range(KD - KD // 4):
                nc.vector.tensor_tensor(merged[:, m, :], merged[:, m, :], gate[:, m, :], ALU.add).then_inc(added, 1)

        @block.gpsimd
        def _(pool):
            for m in range(KD - KD // 4, KD):
                nc.gpsimd.tensor_tensor(merged[:, m, :], merged[:, m, :], gate[:, m, :], ALU.add).then_inc(added, 1)
    rows_product(core, merged, KD, w_out, add_to_residual(core), prepared=SPLIT)
    ffn = columns_of(a["w_ffn_in_3"][0])
    up = lambda k, lo, n, tiles: ffn(k, lo + D_FF, n, tiles)
    norm_stage(core, ones, cols[:, 2 * KD:3 * KD], following=first_gates(ffn, up))
    swiglu(core, ffn, up, rows_of(a["w_ffn_down_3"][0]))
    norm_stage(core, ones, cols[:, 3 * KD:4 * KD], out=core.x)


def shape_constants():
    pos = np.arange(T, dtype=np.float32)

    def rope(dim):
        inv = np.float32(10000.0) ** (-np.arange(0, dim, 2, dtype=np.float32) / np.float32(dim))
        ang = pos[:, None] * inv[None, :].astype(np.float32)
        c, s = np.cos(ang), np.sin(ang)
        return np.concatenate([c, c], 1), np.concatenate([-s, s], 1)

    def tiles(m):
        return m.reshape(TT, P, -1).transpose(1, 0, 2).reshape(P, -1)

    c64, s64 = rope(64)
    c32, s32 = rope(32)
    dist = T - 1 - np.arange(BIAS_ROW)
    exact = REL_BUCKETS // 2
    d = np.maximum(dist, 1).astype(np.float32)
    log_b = exact + (np.log(d / np.float32(exact)) / np.float32(math.log(REL_MAX_DIST / exact))
                     * np.float32(REL_BUCKETS - exact)).astype(np.int32)
    bucket = np.where(dist < exact, dist, np.clip(log_b, exact, REL_BUCKETS - 1))
    bucket = np.where(dist < 0, REL_BUCKETS, bucket)
    q = np.arange(P)[:, None]
    k = np.arange(P)[None, :]
    chunk = np.where(k // 64 <= q // 64, 0.0, NEG)
    out = {
        "ident": np.eye(P), "ones": np.ones((P, P)), "chunk_mask": chunk,
        "cos64": tiles(c64), "sin64": tiles(s64), "cos32": tiles(c32), "sin32": tiles(s32),
        "buckets": bucket[None, :] == np.arange(REL_BUCKETS + 1)[:, None],
        "levels": np.stack([(q // (2 * b) == k // (2 * b)) & (q // b % 2 == 0) & (k // b % 2 == 1)
                            for b in (1, 2, 4, 8, 16, 32, 64)]),
        "reversed": np.eye(P)[::-1], "upper": q <= k, "row_valid": q >= CMP_BLOCK - 1,
        "lam_init": np.array([[0.8 - 0.6 * math.exp(-0.3 * n), 1.0 - (0.8 - 0.6 * math.exp(-0.3 * n))]
                              for n in range(2)]),
    }
    return {n: np.ascontiguousarray(v, dtype=np.float32) for n, v in out.items()}


def common_constants(core, a):
    names = ["ident", "ones", "chunk_mask", "cos64", "sin64", "cos32", "sin32"]
    views = {n: core.const(a[n].shape[1]) for n in names}
    tables = [views[n].rearrange("p (t d) -> p t d", t=TT) for n in names[3:]]
    return views["ident"], views["ones"], views["chunk_mask"], tables, [(views[n], a[n]) for n in names]


def build(nc, a, bias_rows, out):
    core = Core(nc)
    ident, ones, chunk_mask, tables, constant_loads = common_constants(core, a)
    resident = core.const_used
    input_loads, input_jobs = input_parts(core, a["x"][0])
    first_block(core, a, bias_rows, ident, ones, constant_loads + input_loads, input_jobs)
    core.const_used = resident
    second_block(core, a, tables, chunk_mask, ident, ones)
    core.const_used = CONST_AT + 2 * P
    third_block(core, a, ident, ones)
    store_output(core, core.x, out[0], ident)


def kernel(**inputs):
    import concourse.bacc as bacc
    from concourse.bass_utils import run_bass_kernel_spmd

    nc = bacc.Bacc("TRN2", target_bir_lowering=False, num_devices=1)
    arrays, views = {}, {}
    for name, value in {**inputs, **shape_constants()}.items():
        array = np.ascontiguousarray(value)
        arrays[f"in_{name}"] = array
        views[name] = nc.dram_tensor(f"in_{name}", array.shape, F32, kind="ExternalInput").ap()
    bias_rows = nc.dram_tensor("bias_rows", (Q_HEADS, BIAS_ROW), F32).ap()
    out = nc.dram_tensor("out_0", (1, T, D), F32, kind="ExternalOutput").ap()
    build(nc, views, bias_rows, out)
    result = run_bass_kernel_spmd(nc, [arrays], core_ids=[0])
    return result.results[0]["out_0"]
```
